# Optimizing a Trainium2 kernel written in Bass

```python
import math
import jax, jax.numpy as jnp
from jax import lax
import numpy as np

D_MODEL = 1024
BATCH = 1
SEQ = 256
DEPTH = 1

N_ATTN_HEADS = 8
HEAD_DIM = 64
D_ATTN = N_ATTN_HEADS * HEAD_DIM
MOBA_BLOCK = 256
MOBA_TOPK = 3
Q_CHUNK = 16
N_BUCKETS = 32
MAX_EXACT = N_BUCKETS // 2
MAX_DISTANCE = 128
D_LRU = D_MODEL // 2
N_LRU_BLOCKS = 8
LRU_BLOCK = D_LRU // N_LRU_BLOCKS
LRU_CONV_W = 4
LRU_C = 8.0
D_MIX = D_ATTN + D_LRU
D_IN_PROJ = 3 * D_ATTN + 2 * D_LRU
D_FF = 2816
FFN_CONV_W = 3
RMS_EPS = 1e-6


def rms_norm(x, g):
    xf = x.astype(jnp.float32)
    y = xf * lax.rsqrt(jnp.mean(xf * xf, axis=-1, keepdims=True) + RMS_EPS)
    return (y * g.astype(jnp.float32)).astype(x.dtype)

def causal_dwconv(x, w, b):
    width, ch = w.shape
    y = lax.conv_general_dilated(
        x, w[:, None, :].astype(x.dtype), window_strides=(1,), padding=[(width - 1, 0)],
        dimension_numbers=("NWC", "WIO", "NWC"), feature_group_count=ch)
    return y + b.astype(x.dtype)

def t5_bucket(dist):
    n = jnp.maximum(dist, 0)
    nf = jnp.maximum(n, 1).astype(jnp.float32)
    large = MAX_EXACT + (jnp.log(nf / MAX_EXACT) / math.log(MAX_DISTANCE / MAX_EXACT)
                         * (N_BUCKETS - MAX_EXACT)).astype(jnp.int32)
    large = jnp.minimum(large, N_BUCKETS - 1)
    return jnp.where(n < MAX_EXACT, n, large)

def moba_attention(q, k, v, rel_bias):
    B, H, S, dh = q.shape
    nb = -(-S // MOBA_BLOCK)
    pad = nb * MOBA_BLOCK - S
    k_pad = jnp.pad(k, ((0, 0), (0, 0), (0, pad), (0, 0)))
    v_pad = jnp.pad(v, ((0, 0), (0, 0), (0, pad), (0, 0)))
    k_blocks = k_pad.reshape(B, H, nb, MOBA_BLOCK, dh)
    v_blocks = v_pad.reshape(B, H, nb, MOBA_BLOCK, dh)
    k_mean = jnp.mean(k_blocks.astype(jnp.float32), axis=3)
    top = min(MOBA_TOPK, nb)
    scale = HEAD_DIM ** -0.5
    key_off = jnp.arange(MOBA_BLOCK, dtype=jnp.int32)
    b_i = jnp.arange(B)[:, None, None, None]
    h_i = jnp.arange(H)[None, :, None, None]
    bias_T = rel_bias.astype(jnp.float32).T

    def chunk(c):
        q0 = c * Q_CHUNK
        qc = lax.dynamic_slice_in_dim(q, q0, Q_CHUNK, axis=2)
        q_pos = q0 + jnp.arange(Q_CHUNK, dtype=jnp.int32)
        own = q0 // MOBA_BLOCK
        gate = jnp.einsum("bhqd,bhnd->bhqn", qc.astype(jnp.float32), k_mean)
        past = jnp.arange(nb) < own
        gate = jnp.where(past[None, None, None, :], gate, -jnp.inf)
        _, idx = lax.top_k(gate, top)
        valid = idx < own
        k_sel = k_blocks[b_i, h_i, idx]
        v_sel = v_blocks[b_i, h_i, idx]
        s_sel = jnp.einsum("bhqd,bhqjkd->bhqjk", qc, k_sel,
                           preferred_element_type=jnp.float32) * scale
        k_pos_sel = idx[..., None] * MOBA_BLOCK + key_off
        bucket_sel = t5_bucket(q_pos[None, None, :, None, None] - k_pos_sel)
        s_sel = s_sel + bias_T[h_i[..., None], bucket_sel]
        s_sel = jnp.where(valid[..., None], s_sel, -jnp.inf)
        k_own = lax.dynamic_slice_in_dim(k_pad, own * MOBA_BLOCK, MOBA_BLOCK, axis=2)
        v_own = lax.dynamic_slice_in_dim(v_pad, own * MOBA_BLOCK, MOBA_BLOCK, axis=2)
        s_own = jnp.einsum("bhqd,bhkd->bhqk", qc, k_own,
                           preferred_element_type=jnp.float32) * scale
        dist_own = q_pos[:, None] - (own * MOBA_BLOCK + key_off)[None, :]
        s_own = s_own + jnp.transpose(rel_bias.astype(jnp.float32)[t5_bucket(dist_own)], (2, 0, 1))[None]
        s_own = jnp.where((dist_own >= 0)[None, None], s_own, -jnp.inf)
        logits = jnp.concatenate([s_sel.reshape(B, H, Q_CHUNK, top * MOBA_BLOCK), s_own], axis=-1)
        p = jax.nn.softmax(logits, axis=-1).astype(v.dtype)
        p_sel = p[..., :top * MOBA_BLOCK].reshape(B, H, Q_CHUNK, top, MOBA_BLOCK)
        p_own = p[..., top * MOBA_BLOCK:]
        return (jnp.einsum("bhqjk,bhqjkd->bhqd", p_sel, v_sel)
                + jnp.einsum("bhqk,bhkd->bhqd", p_own, v_own))

    outs = lax.map(chunk, jnp.arange(S // Q_CHUNK))
    return jnp.transpose(outs, (1, 2, 0, 3, 4)).reshape(B, H, S, dh)

def rg_lru(x, w_r, b_r, w_i, b_i, lam):
    B, S, _ = x.shape
    xf = x.astype(jnp.float32)
    xb = xf.reshape(B, S, N_LRU_BLOCKS, LRU_BLOCK)
    r = jax.nn.sigmoid(jnp.einsum("bsnc,ncd->bsnd", xb, w_r.astype(jnp.float32)).reshape(B, S, D_LRU)
                       + b_r.astype(jnp.float32))
    i = jax.nn.sigmoid(jnp.einsum("bsnc,ncd->bsnd", xb, w_i.astype(jnp.float32)).reshape(B, S, D_LRU)
                       + b_i.astype(jnp.float32))
    log_a = -LRU_C * r * jax.nn.softplus(-lam.astype(jnp.float32))
    a = jnp.exp(log_a)
    u = jnp.sqrt(-jnp.expm1(2.0 * log_a)) * (i * xf)

    def combine(left, right):
        a1, b1 = left
        a2, b2 = right
        return a1 * a2, a2 * b1 + b2

    _, h = lax.associative_scan(combine, (a, u), axis=1)
    return h.astype(x.dtype)

def first_inputs(seed: int = 0) -> dict:
    key = jax.random.key(seed)
    ks = jax.random.split(key, 24)
    nrm = lambda k, shape, s: jax.random.normal(k, shape, jnp.float32) * s
    u_a = jax.random.uniform(ks[10], (DEPTH, D_LRU), jnp.float32, 0.9, 0.999)
    base = u_a ** (1.0 / LRU_C)
    lam = jnp.log(base) - jnp.log1p(-base)
    return {
        "x": nrm(ks[0], (BATCH, SEQ, D_MODEL), 1.0),
        "g_pre_mix": 1.0 + nrm(ks[1], (DEPTH, D_MODEL), 0.05),
        "w_in": nrm(ks[2], (DEPTH, D_MODEL, D_IN_PROJ), D_MODEL ** -0.5),
        "rel_bias": nrm(ks[3], (N_BUCKETS, N_ATTN_HEADS), 0.3),
        "w_conv_lru": nrm(ks[4], (DEPTH, LRU_CONV_W, D_LRU), LRU_CONV_W ** -0.5),
        "b_conv_lru": nrm(ks[5], (DEPTH, D_LRU), 0.02),
        "w_r": nrm(ks[6], (DEPTH, N_LRU_BLOCKS, LRU_BLOCK, LRU_BLOCK), LRU_BLOCK ** -0.5),
        "b_r": nrm(ks[7], (DEPTH, D_LRU), 0.02),
        "w_i": nrm(ks[8], (DEPTH, N_LRU_BLOCKS, LRU_BLOCK, LRU_BLOCK), LRU_BLOCK ** -0.5),
        "b_i": nrm(ks[9], (DEPTH, D_LRU), 0.02),
        "lam": lam,
        "w_out": nrm(ks[11], (DEPTH, D_MIX, D_MODEL), D_MIX ** -0.5),
        "g_post_mix": 1.0 + nrm(ks[12], (DEPTH, D_MODEL), 0.05),
        "g_pre_ffn": 1.0 + nrm(ks[13], (DEPTH, D_MODEL), 0.05),
        "w_up": nrm(ks[14], (DEPTH, D_MODEL, 2 * D_FF), D_MODEL ** -0.5),
        "w_conv_ffn": nrm(ks[15], (DEPTH, FFN_CONV_W, 2 * D_FF), FFN_CONV_W ** -0.5),
        "b_conv_ffn": nrm(ks[16], (DEPTH, 2 * D_FF), 0.02),
        "w_down": nrm(ks[17], (DEPTH, D_FF, D_MODEL), D_FF ** -0.5),
        "g_post_ffn": 1.0 + nrm(ks[18], (DEPTH, D_MODEL), 0.05),
    }

def first_block(x, g_pre_mix, w_in, rel_bias, w_conv_lru, b_conv_lru, w_r, b_r, w_i, b_i, lam,
              w_out, g_post_mix, g_pre_ffn, w_up, w_conv_ffn, b_conv_ffn, w_down, g_post_ffn):
    B, S, _ = x.shape
    for l in range(DEPTH):
        h = rms_norm(x, g_pre_mix[l])
        proj = h @ w_in[l].astype(h.dtype)
        q, k, v, xr, gr = jnp.split(
            proj, [D_ATTN, 2 * D_ATTN, 3 * D_ATTN, 3 * D_ATTN + D_LRU], axis=-1)
        to_heads = lambda t: jnp.transpose(t.reshape(B, S, N_ATTN_HEADS, HEAD_DIM), (0, 2, 1, 3))
        attn = moba_attention(to_heads(q), to_heads(k), to_heads(v), rel_bias)
        attn = jnp.transpose(attn, (0, 2, 1, 3)).reshape(B, S, D_ATTN)
        xr = causal_dwconv(xr, w_conv_lru[l], b_conv_lru[l])
        lru = rg_lru(xr, w_r[l], b_r[l], w_i[l], b_i[l], lam[l]) * jax.nn.gelu(gr, approximate=True)
        mix = jnp.concatenate([attn, lru], axis=-1) @ w_out[l].astype(h.dtype)
        x = x + rms_norm(mix, g_post_mix[l])
        h = rms_norm(x, g_pre_ffn[l])
        up = causal_dwconv(h @ w_up[l].astype(h.dtype), w_conv_ffn[l], b_conv_ffn[l])
        c_u, c_g = jnp.split(up, 2, axis=-1)
        ffn = (jax.nn.gelu(c_g, approximate=True) * c_u) @ w_down[l].astype(h.dtype)
        x = x + rms_norm(ffn, g_post_ffn[l])
    return x


DEPTH_2 = 2

GRID_W = 64
NA_HEADS = 16
NA_HEAD_DIM = D_MODEL // NA_HEADS
NA_WIN_H = 8
NA_WIN_W = 16
MLA_HEADS = 16
MLA_Q_LORA = D_MODEL // 4
MLA_KV_LORA = D_MODEL // 8
MLA_NOPE = 64
MLA_ROPE = 32
MLA_V = 64
ROPE_THETA = 10000.0
Q_BLOCK = 128
FFN_DIM = 2816
N_EXPERTS = 8
TOP_K = 2
EXPERT_DIM = 1792
NORM_EPS = 1e-6


def _rmsnorm(x):
    xf = x.astype(jnp.float32)
    y = xf * lax.rsqrt(jnp.mean(xf * xf, axis=-1, keepdims=True) + NORM_EPS)
    return y.astype(x.dtype)

def _modulate(x, shift, scale):
    return _rmsnorm(x) * (1 + scale[:, None, :]) + shift[:, None, :]

def _swiglu(h, w_gu, w_down):
    gate, up = jnp.split(h @ w_gu, 2, axis=-1)
    return (jax.nn.silu(gate) * up) @ w_down

def _rope_2d_tables(seq_len):
    t = jnp.arange(seq_len)
    row = (t // GRID_W).astype(jnp.float32)
    col = (t % GRID_W).astype(jnp.float32)
    n = MLA_ROPE // 4
    inv = ROPE_THETA ** (-jnp.arange(n, dtype=jnp.float32) / n)
    ang = jnp.concatenate([row[:, None] * inv, col[:, None] * inv], axis=-1)
    return jnp.cos(ang), jnp.sin(ang)

def _apply_rope(x, cos, sin):
    x1 = x[..., 0::2].astype(jnp.float32)
    x2 = x[..., 1::2].astype(jnp.float32)
    out = jnp.stack([x1 * cos - x2 * sin, x1 * sin + x2 * cos], axis=-1)
    return out.reshape(x.shape).astype(x.dtype)

def _neighborhood_attention(h, w_qkv, rpb, w_o):
    B, S, D = h.shape
    rows = S // GRID_W
    kh = min(NA_WIN_H, rows)
    kw = min(NA_WIN_W, GRID_W)
    qkv = (h @ w_qkv).reshape(B, rows, GRID_W, 3, NA_HEADS, NA_HEAD_DIM)
    q = qkv[:, :, :, 0] * (NA_HEAD_DIM ** -0.5)
    k = qkv[:, :, :, 1]
    v = qkv[:, :, :, 2]
    cols = jnp.arange(GRID_W)
    col_idx = jnp.clip(cols - kw // 2, 0, GRID_W - kw)[:, None] + jnp.arange(kw)[None, :]
    dc_idx = col_idx - cols[:, None] + NA_WIN_W - 1

    def row_block(r):
        rs = jnp.clip(r - kh // 2, 0, rows - kh)
        q_r = lax.dynamic_index_in_dim(q, r, axis=1, keepdims=False)
        k_g = lax.dynamic_slice_in_dim(k, rs, kh, axis=1)[:, :, col_idx]
        v_g = lax.dynamic_slice_in_dim(v, rs, kh, axis=1)[:, :, col_idx]
        dr_idx = rs + jnp.arange(kh) - r + NA_WIN_H - 1
        bias = rpb[:, dr_idx[None, :, None], dc_idx[:, None, :]]
        s = jnp.einsum('bqhd,bkqjhd->bhqkj', q_r, k_g).astype(jnp.float32) + bias.astype(jnp.float32)
        p = jax.nn.softmax(s.reshape(B, NA_HEADS, GRID_W, kh * kw), axis=-1)
        p = p.reshape(s.shape).astype(v.dtype)
        return jnp.einsum('bhqkj,bkqjhd->bqhd', p, v_g)

    o = lax.map(row_block, jnp.arange(rows))
    o = jnp.moveaxis(o, 0, 1).reshape(B, S, D)
    return o @ w_o

def _mla(h, w_down, q_norm, w_uq, kv_norm, w_ukv, w_o):
    B, S, D = h.shape
    down = h @ w_down
    c_q = _rmsnorm(down[..., :MLA_Q_LORA]) * q_norm
    c_kv = _rmsnorm(down[..., MLA_Q_LORA:MLA_Q_LORA + MLA_KV_LORA]) * kv_norm
    k_rope = down[..., MLA_Q_LORA + MLA_KV_LORA:]
    q = (c_q @ w_uq).reshape(B, S, MLA_HEADS, MLA_NOPE + MLA_ROPE)
    kv = (c_kv @ w_ukv).reshape(B, S, MLA_HEADS, MLA_NOPE + MLA_V)
    k_nope, v = kv[..., :MLA_NOPE], kv[..., MLA_NOPE:]
    cos, sin = _rope_2d_tables(S)
    q_nope = q[..., :MLA_NOPE]
    q_rope = _apply_rope(q[..., MLA_NOPE:], cos[:, None, :], sin[:, None, :])
    k_rope = _apply_rope(k_rope, cos, sin)
    scale = (MLA_NOPE + MLA_ROPE) ** -0.5
    nb = S // Q_BLOCK

    def to_blocks(t):
        return jnp.moveaxis(t.reshape(B, nb, Q_BLOCK, *t.shape[2:]), 1, 0)

    def q_block(blk):
        qn, qr = blk
        s = (jnp.einsum('bqhd,bkhd->bhqk', qn, k_nope)
             + jnp.einsum('bqhr,bkr->bhqk', qr, k_rope)).astype(jnp.float32) * scale
        p = jax.nn.softmax(s, axis=-1).astype(v.dtype)
        return jnp.einsum('bhqk,bkhd->bqhd', p, v)

    o = lax.map(q_block, (to_blocks(q_nope), to_blocks(q_rope)))
    o = jnp.moveaxis(o, 0, 1).reshape(B, S, MLA_HEADS * MLA_V)
    return o @ w_o

def _moe(h, w_router, w_gu, w_down):
    B, S, D = h.shape
    hf = h.reshape(B * S, D)
    probs = jax.nn.softmax((hf @ w_router).astype(jnp.float32), axis=-1)
    vals, idx = lax.top_k(probs, TOP_K)
    wts = vals / jnp.sum(vals, axis=-1, keepdims=True)
    combine = jnp.sum(jax.nn.one_hot(idx, N_EXPERTS, dtype=jnp.float32) * wts[..., None], axis=1)
    combine = combine.astype(h.dtype)
    y = jnp.zeros_like(hf)
    for e in range(N_EXPERTS):
        y = y + combine[:, e:e + 1] * _swiglu(hf, w_gu[e], w_down[e])
    return y.reshape(B, S, D)

def second_inputs(seed: int = 0) -> dict:
    key = jax.random.key(seed)
    ks = iter(jax.random.split(key, 32))
    n_even = (DEPTH_2 + 1) // 2
    n_odd = DEPTH_2 // 2
    D = D_MODEL

    def nrm(shape, fan_in, mult=1.0):
        return jax.random.normal(next(ks), shape, jnp.float32) * (mult * fan_in ** -0.5)

    return {
        "x": jax.random.normal(next(ks), (BATCH, SEQ, D), jnp.float32),
        "c": jax.random.normal(next(ks), (BATCH, D), jnp.float32),
        "w_ada": nrm((DEPTH_2, D, 6 * D), D, 0.5),
        "b_ada": 0.02 * jax.random.normal(next(ks), (DEPTH_2, 6 * D), jnp.float32),
        "na_w_qkv": nrm((n_even, D, 3 * D), D),
        "na_rpb": 0.1 * jax.random.normal(next(ks), (n_even, NA_HEADS, 2 * NA_WIN_H - 1, 2 * NA_WIN_W - 1), jnp.float32),
        "na_w_o": nrm((n_even, D, D), D),
        "ffn_w_gu": nrm((n_even, D, 2 * FFN_DIM), D),
        "ffn_w_down": nrm((n_even, FFN_DIM, D), FFN_DIM),
        "mla_w_down": nrm((n_odd, D, MLA_Q_LORA + MLA_KV_LORA + MLA_ROPE), D),
        "mla_q_norm": 1.0 + 0.01 * jax.random.normal(next(ks), (n_odd, MLA_Q_LORA), jnp.float32),
        "mla_w_uq": nrm((n_odd, MLA_Q_LORA, MLA_HEADS * (MLA_NOPE + MLA_ROPE)), MLA_Q_LORA),
        "mla_kv_norm": 1.0 + 0.01 * jax.random.normal(next(ks), (n_odd, MLA_KV_LORA), jnp.float32),
        "mla_w_ukv": nrm((n_odd, MLA_KV_LORA, MLA_HEADS * (MLA_NOPE + MLA_V)), MLA_KV_LORA),
        "mla_w_o": nrm((n_odd, MLA_HEADS * MLA_V, D), MLA_HEADS * MLA_V),
        "moe_w_router": nrm((n_odd, D, N_EXPERTS), D),
        "moe_w_gu": nrm((n_odd, N_EXPERTS, D, 2 * EXPERT_DIM), D),
        "moe_w_down": nrm((n_odd, N_EXPERTS, EXPERT_DIM, D), EXPERT_DIM),
        "final_norm": 1.0 + 0.01 * jax.random.normal(next(ks), (D,), jnp.float32),
    }

def second_block(x, c, w_ada, b_ada, na_w_qkv, na_rpb, na_w_o, ffn_w_gu, ffn_w_down,
              mla_w_down, mla_q_norm, mla_w_uq, mla_kv_norm, mla_w_ukv, mla_w_o,
              moe_w_router, moe_w_gu, moe_w_down, final_norm):
    c_act = jax.nn.silu(c)
    for i in range(DEPTH_2):
        j = i // 2
        mod = c_act @ w_ada[i] + b_ada[i]
        sh_a, sc_a, g_a, sh_f, sc_f, g_f = jnp.split(mod, 6, axis=-1)
        h = _modulate(x, sh_a, sc_a)
        if i % 2 == 0:
            m = _neighborhood_attention(h, na_w_qkv[j], na_rpb[j], na_w_o[j])
        else:
            m = _mla(h, mla_w_down[j], mla_q_norm[j], mla_w_uq[j], mla_kv_norm[j], mla_w_ukv[j], mla_w_o[j])
        x = x + g_a[:, None, :] * m
        h = _modulate(x, sh_f, sc_f)
        if i % 2 == 0:
            f = _swiglu(h, ffn_w_gu[j], ffn_w_down[j])
        else:
            f = _moe(h, moe_w_router[j], moe_w_gu[j], moe_w_down[j])
        x = x + g_f[:, None, :] * f
    return _rmsnorm(x) * final_norm


def setup_inputs(seed=0):
    out = dict(first_inputs(seed))
    for name, value in second_inputs(seed + 1).items():
        if name != "x":
            out[name + "_2"] = value
    return out


def reference(
    x, g_pre_mix, w_in, rel_bias, w_conv_lru, b_conv_lru, w_r, b_r, w_i, b_i, lam, w_out,
    g_post_mix, g_pre_ffn, w_up, w_conv_ffn, b_conv_ffn, w_down, g_post_ffn, c_2, w_ada_2,
    b_ada_2, na_w_qkv_2, na_rpb_2, na_w_o_2, ffn_w_gu_2, ffn_w_down_2, mla_w_down_2,
    mla_q_norm_2, mla_w_uq_2, mla_kv_norm_2, mla_w_ukv_2, mla_w_o_2, moe_w_router_2, moe_w_gu_2,
    moe_w_down_2, final_norm_2,
):
    x = first_block(
        x, g_pre_mix, w_in, rel_bias, w_conv_lru, b_conv_lru, w_r, b_r, w_i, b_i, lam, w_out,
        g_post_mix, g_pre_ffn, w_up, w_conv_ffn, b_conv_ffn, w_down, g_post_ffn,
    )
    return second_block(
        x, c_2, w_ada_2, b_ada_2, na_w_qkv_2, na_rpb_2, na_w_o_2, ffn_w_gu_2, ffn_w_down_2,
        mla_w_down_2, mla_q_norm_2, mla_w_uq_2, mla_kv_norm_2, mla_w_ukv_2, mla_w_o_2,
        moe_w_router_2, moe_w_gu_2, moe_w_down_2, final_norm_2,
    )


_drawn_inputs = setup_inputs


def setup_inputs(seed=0):
    import zlib

    import numpy as np

    out = dict(_drawn_inputs(seed))
    spreads = {}
    factors = {'b_r': 8.0,
     'b_i': 8.0,
     'b_conv_ffn': 3.061,
     'b_ada_2': 3.505,
     'na_rpb_2': 8.0,
     'mla_q_norm_2': 8.0,
     'mla_w_uq_2': 3.033,
     'mla_kv_norm_2': 8.0,
     'final_norm_2': 5.568}
    for name, (base, spread) in spreads.items():
        noise = np.random.default_rng([zlib.crc32(name.encode()), seed]).standard_normal(out[name].shape)
        drawn = base * np.exp(spread * noise) if base else spread * noise
        out[name] = __import__('jax').numpy.asarray(drawn.astype(out[name].dtype))
    for name, factor in factors.items():
        out[name] = (out[name] * factor).astype(out[name].dtype)
    return out
```

```python
import math
from contextlib import ExitStack

import numpy as np

import concourse.bass as bass
from concourse import mybir

F32 = mybir.dt.float32
F32R = mybir.dt.float32r
I32 = mybir.dt.int32
ALU = mybir.AluOpType
ACT = mybir.ActivationFunctionType
AXX = mybir.AxisListType.X

P = 128
S = 256
NT = S // P
D = 1024
KT = D // P
EPS = 1e-6
HD = 64
H1 = 8
DA = H1 * HD
DL = D // 2
LT = DL // P
NBK = 32
CW = 4
FF = 2816
FT = FF // P
GU_STEPS = FT // 2
DN_CHUNKS = FT // 2
H2 = 16
GW = 64
GR = S // GW
RPB_H, RPB_W = 15, 31
QL, KVL, ROPE = 256, 128, 32
QKW = HD + ROPE
MLA_DN = QL + KVL + ROPE
NE = 8
ED = 1792
ET = ED // P
EC = ED // 4
MAX_PASSES = NE + 3
PASS_CHUNKS = 24
NEG = -1.0e30

CHUNK = 2048
NRAW, NSPLIT, NADA = 4, 2, 2
MOE_RAW, MOE_SPLIT = NRAW + NADA, NSPLIT + 1
N_PASS = 15

W_IN = 0
W_OUT = W_IN + 10
W_UP = W_OUT + 4
W_DOWN = W_UP + 2 * GU_STEPS
W_QKV = W_DOWN + DN_CHUNKS
W_NAO = W_QKV + 12
W_GU = W_NAO + 4
W_DN2 = W_GU + 2 * GU_STEPS
W_MDN = W_DN2 + DN_CHUNKS
W_UQ = W_MDN + 2
W_UKV = W_UQ + 2
W_MLO = W_UKV + 1
W_MOE = W_MLO + 4

ADA_CHUNKS = 24
ADA_IN_GU = GU_STEPS + 2

VEC = {}


def _plan_vectors():
    tiles = [
        [("c", 8), ("g_pre_mix", 8), ("g_pre_ffn", 8), ("w_conv_lru", 16), ("b_conv_lru", 4), ("b_r", 4),
         ("b_i", 4), ("lam", 4), ("q_norm", 2), ("kv_norm", 1), ("b_conv_ffn", 44)],
        [("b_ada", 96)],
        [("w_conv_ffn01", 88)],
        [("w_conv_ffn2", 44)],
    ]
    at = 0
    out = []
    for n, tile in enumerate(tiles):
        row = 0
        for name, rows in tile:
            VEC[name] = (n, row, rows, at + row)
            row += rows
        out.append((at, row))
        at += row
    return out, at


VEC_TILES, VEC_COLS = _plan_vectors()

C_ID, C_IOTA, C_TRI, C_ONE = 0, 128, 256, 384
C_NAM = 512
C_COS = C_NAM + GW
C_SIN = C_COS + 32
C_LT = C_SIN + 32
C_EID = C_LT + 64
C_HOT = C_EID + 8
C_ALL = C_HOT + S


def shape_constants():
    c = np.zeros((P, C_ALL), np.float32)
    i = np.arange(P)
    c[:, C_ID:C_ID + P] = np.eye(P)
    c[:, C_IOTA:C_IOTA + P] = i[None, :]
    c[:, C_TRI:C_TRI + P] = i[:, None] < i[None, :]
    c[:, C_ONE:C_ONE + P] = 1.0
    col, key = (GW - 1 - i % GW)[:, None], np.arange(GW)[None, :]
    first = np.clip(col - 8, 0, GW - 16)
    c[:, C_NAM:C_NAM + GW] = np.where((key >= first) & (key < first + 16), 0.0, NEG)
    t = np.arange(S)
    n = ROPE // 4
    inv = np.float32(10000.0) ** (-np.arange(n, dtype=np.float32) / np.float32(n))
    ang = np.concatenate([(t // GW).astype(np.float32)[:, None] * inv, (t % GW).astype(np.float32)[:, None] * inv], 1)
    for at, f in ((C_COS, np.cos), (C_SIN, np.sin)):
        c[:, at:at + 32] = f(ang.astype(np.float32)).reshape(NT, P, 16).transpose(1, 0, 2).reshape(P, 32)
    e = np.arange(NE)
    c[:, C_LT:C_LT + 64] = (e[None, :] < e[:, None]).reshape(1, 64)
    c[:, C_EID:C_EID + 8] = e
    dist = 255 - np.arange(S)
    nf = np.maximum(dist, 1).astype(np.float32)
    large = 16 + (np.log(nf / np.float32(16)) / np.float32(math.log(8.0)) * np.float32(16)).astype(np.int32)
    bucket = np.where(dist < 16, dist, np.minimum(large, NBK - 1))
    c[bucket, C_HOT + np.arange(S)] = 1.0
    return c


STAGES = [0, 1, 2, 3, 4, "m", 5]
TILES_OF = {s: 3 if s == "m" else KT for s in STAGES}
TURN0 = {s: sum(TILES_OF[r] for r in STAGES[:n]) for n, s in enumerate(STAGES)}
XN0 = {s: NT * n for n, s in enumerate(STAGES)}
RMS0 = {s: n for n, s in enumerate([0, "r0", 1, "r1", 2, 3, 4, 5, "f"])}
HEADS0 = {1: 0, 2: H1, 3: H1 + H2}


class Chunk:

    def __init__(self, base, reg=None, per=0):
        self.moe = base >= W_MOE
        first, ring, halves = (W_MOE, MOE_RAW, MOE_SPLIT) if self.moe else (0, NRAW, NSPLIT)
        assert per % ring == 0 and per % halves == 0
        self.n = base if reg is None else base + reg * per
        at, part = (base - first) % ring, (base - first) % halves
        self.slot = (first + at) % NRAW if at < NRAW else at
        self.half = (first + part) % NSPLIT if part < NSPLIT else part
        self.first_use = reg is None and base - first < ring
        self.first_half = reg is None and base - first < halves
        self.ring, self.halves = ring, halves
        loads = (base - first) // ring + 1
        self.loads = loads if reg is None else loads + reg * (per // ring)


def reversed_in(ap, n):
    return ap.rearrange("p (b n) -> p b n", n=n)[:, :, ::-1]


class Chain:

    def __init__(self, eng, sem):
        self.eng, self.sem, self.n, self.loop = eng, sem, 0, None

    def count(self):
        return self.n if self.loop is None else self.n + self.loop[0] * self.loop[1]

    def mark(self, ins):
        ins.then_inc(self.sem, 1)
        self.n += 1
        return self.count()

    def after(self, mark):
        self.eng.wait_ge(self.sem, mark)

    def link(self, ins):
        self.after(self.mark(ins))

    def enter(self, reg, per):
        self.loop = (reg, per, self.n)

    def leave(self, times):
        reg, per, start = self.loop
        assert self.n - start == per, (self.n - start, per)
        self.loop = None
        self.n = start + per * times


def blocks(nc, a, out):
    ctx = ExitStack()
    with ctx:
        base = [(nc.sbuf_base + 63) // 64 * 64]

        def at(name, cols, dt=F32, offset=None, parts=P):
            if offset is None:
                offset = base[0]
                base[0] += (cols * 4 + 31) // 32 * 32
                assert base[0] <= nc.sbuf_usable_end, (name, base[0], nc.sbuf_usable_end)
            t = nc.alloc_sbuf_tensor_at(name, [parts, cols], dt, offset=offset)
            return t.ap() if hasattr(t, "ap") and callable(t.ap) else t[:, :]

        def room(cols):
            o = base[0]
            base[0] += cols * 4
            assert base[0] <= nc.sbuf_usable_end, base[0]
            return o

        sems = {}

        def sem(name):
            if name not in sems:
                sems[name] = ctx.enter_context(nc.semaphore(name))
            return sems[name]

        raw = at("raw", NRAW * CHUNK).rearrange("p (s n) -> p s n", s=NRAW)
        whi2 = at("whi", NSPLIT * CHUNK, F32R).rearrange("p (s n) -> p s n", s=NSPLIT)
        wlo2 = at("wlo", NSPLIT * CHUNK, F32R).rearrange("p (s n) -> p s n", s=NSPLIT)
        ada_at = room(NADA * CHUNK)
        ada = at("ada", NADA * CHUNK, offset=ada_at).rearrange("p (s n) -> p s n", s=NADA)
        x = at("x", NT * D).rearrange("p (t n) -> p t n", t=NT)
        xn_at = room(NT * D)
        xn = at("xn", NT * D, offset=xn_at).rearrange("p (t n) -> p t n", t=NT)
        ahi_flat, alo_flat = at("ahi", KT * S, F32R), at("alo", KT * S, F32R)
        ahi, alo = (f.rearrange("p (k s) -> p k s", k=KT) for f in (ahi_flat, alo_flat))
        raws = [raw[:, s] for s in range(NRAW)] + [ada[:, s] for s in range(NADA)]
        whi = [whi2[:, s] for s in range(NSPLIT)] + [ahi_flat]
        wlo = [wlo2[:, s] for s in range(NSPLIT)] + [alo_flat]
        gates = at("gates", 2 * D).rearrange("p (g n) -> p g n", g=2)
        gvec = at("gvec", D)
        vecs = at("vecs", VEC_COLS)
        cst = at("cst", C_ALL)
        small = at("small", 256)
        mod = at("mod", 4 * KT)
        hm = at("hm", 2 * S).rearrange("p (r s) -> p r s", r=2)
        odd = at("odd", S)
        union = base[0]
        here = [union]

        def u(name, cols, dt=F32, parts=P):
            o = here[0]
            here[0] += (cols * 4 + 31) // 32 * 32
            assert here[0] <= nc.sbuf_usable_end, (name, here[0], nc.sbuf_usable_end)
            return at(name, cols, dt, offset=o, parts=parts)

        ghi = u("ghi", FT * S, F32R).rearrange("p (k s) -> p k s", k=FT)
        glo = u("glo", FT * S, F32R).rearrange("p (k s) -> p k s", k=FT)
        acc = u("acc", 6 * D)
        cv = at("cv", 2 * 2 * 2 * S, offset=xn_at)[:, 0:4 * S].rearrange("p (h f s) -> p h f s", h=2, f=2)
        pr = at("pr", 4 * S, offset=xn_at + 4 * S * 4)[:, 0:2 * S].rearrange("p (f s) -> p f s", f=2)

        def core_buffers(tag):
            sbf = u(f"scores{tag}", 2 * 512).rearrange("p (r n) -> p r n", r=2)
            pbf = u(f"probs{tag}", 3 * 512).rearrange("p (r n) -> p r n", r=3)
            ptb = u(f"probsT{tag}", 2 * 512).rearrange("p (r n) -> p r n", r=2)
            return sbf, pbf, ptb

        here[0] = union
        core1 = core_buffers("1")
        qT1 = u("qT1", LT * S).rearrange("p (k s) -> p k s", k=LT)
        kT1 = u("kT1", LT * S).rearrange("p (k s) -> p k s", k=LT)
        v1 = u("v1", NT * DA).rearrange("p (t n) -> p t n", t=NT)
        bias1 = u("bias1", H1 * 384).rearrange("p (h n) -> p h n", h=H1)
        lru = [u(f"lru{n}", LT * S).rearrange("p (k s) -> p k s", k=LT) for n in range(6)]
        here[0] = union
        rows = u("rows", 4 * P).rearrange("p (n c) -> p n c", n=4)
        here[0] = base[0]
        wr = at("wr", LT * P, offset=ada_at).rearrange("p (k c) -> p k c", k=LT)
        wi = at("wi", LT * P, offset=ada_at + LT * P * 4).rearrange("p (k c) -> p k c", k=LT)
        tbl = at("tbl", 512, offset=ada_at + 2 * LT * P * 4, parts=8)
        relb = at("relb", H1, offset=ada_at + 2 * LT * P * 4 + 2048, parts=NBK)

        here[0] = union
        core2 = core_buffers("2")
        qT2 = u("qT2", KT * S).rearrange("p (k s) -> p k s", k=KT)
        kT2 = u("kT2", KT * S).rearrange("p (k s) -> p k s", k=KT)
        v2 = u("v2", NT * D).rearrange("p (t n) -> p t n", t=NT)
        HB = H2 // 2
        bias2 = [u("bias2a", HB * 512), at("bias2b", HB * 512, offset=ada_at)]
        bias2 = [b.rearrange("p (h t n) -> p h t n", h=HB, t=NT) for b in bias2]

        here[0] = union
        core3 = core_buffers("3")
        NH3 = H2 + 1
        qtok = u("qtok", NT * NH3 * QKW).rearrange("p (t h n) -> p t h n", t=NT, h=NH3)
        ktok = u("ktok", NT * H2 * QKW).rearrange("p (t h n) -> p t h n", t=NT, h=H2)
        v3 = u("v3", NT * D).rearrange("p (t n) -> p t n", t=NT)
        qkT = u("qkT", 2 * 512).rearrange("p (r n) -> p r n", r=2)
        rt = at("rt", 4 * NT * NH3 * 16, offset=ada_at).rearrange("p (r t h i) -> p r t h i", r=4, t=NT, h=NH3)

        here[0] = union
        hchi = u("hchi", KT * P, F32R).rearrange("p (k s) -> p k s", k=KT)
        hclo = u("hclo", KT * P, F32R).rearrange("p (k s) -> p k s", k=KT)
        gchi = u("gchi", ET * P, F32R).rearrange("p (k s) -> p k s", k=ET)
        gclo = u("gclo", ET * P, F32R).rearrange("p (k s) -> p k s", k=ET)
        hc = u("hc", KT * P).rearrange("p (k s) -> p k s", k=KT)
        ge = u("ge", ED)
        sg = u("sg", 2 * EC).rearrange("p (r n) -> p r n", r=2)
        dc = u("dc", D)
        y = u("y", NT * D).rearrange("p (t n) -> p t n", t=NT)
        pick = u("pick", NT * P).rearrange("p (t s) -> p t s", t=NT)
        pickT = u("pickT", S)
        rw = u("rw", 32 * NE).rearrange("p (r n) -> p r n", r=32)
        rtr = u("rtr", KT * NE)
        rthi = u("rthi", KT * NE, F32R).rearrange("p (k e) -> p k e", k=KT)
        rtlo = u("rtlo", KT * NE, F32R).rearrange("p (k e) -> p k e", k=KT)
        cmp_ = u("cmp", 4 * NT * NE * NE)
        posn = u("posn", NT * 12).rearrange("p (t n) -> p t n", t=NT)
        wcol = u("wcol", NT * 12).rearrange("p (t n) -> p t n", t=NT)
        eidf = u("eidf", 16)
        eidi = u("eidi", 16, I32)

        ps = ctx.enter_context(nc.psum_tensor("ps", [P, 8, 512], F32))

        ident = cst[:, C_ID:C_ID + P]
        ones = cst[:, C_ONE:C_ONE + P]
        epsc = small[:, 0:1]
        ss = small[:, 2:4]
        std = small[:, 4:6]
        rstd = small[:, 6:8]
        mx = small[:, 8:8 + 32].rearrange("p (h t) -> p h t", t=NT)
        sume = small[:, 40:72].rearrange("p (h t) -> p h t", t=NT)
        rsum = small[:, 72:104].rearrange("p (h t) -> p h t", t=NT)
        nmx = small[:, 104:136].rearrange("p (h t) -> p h t", t=NT)
        sp8 = small[:, 136:140]
        lamw = small[:, 140:164].rearrange("p (r k) -> p r k", k=LT)
        ssm = small[:, 164:168]
        stm = small[:, 168:172]
        rsm = small[:, 172:176]

        def vec(name):
            _, _, n, col = VEC[name]
            return vecs[:, col:col + n]

        scratch = nc.dram_tensor("rel_table", [H1, 512], F32).ap()

        def view(slot_ap, k, n):
            return slot_ap[:, 0:k * n].rearrange("p (k n) -> p k n", k=k)

        def kn(ap, k0, k, n0, n):
            return ap[k0 * P:(k0 + k) * P, n0:n0 + n].rearrange("(k p) n -> p k n", p=P)

        def chunk_shape(c):
            if c < W_OUT or W_UP <= c < W_DOWN or W_QKV <= c < W_NAO or W_GU <= c < W_DN2:
                return KT, 256
            if W_MDN <= c < W_UQ:
                return KT, MLA_DN // 2
            if W_UQ <= c < W_UKV:
                return 2, 768
            if c == W_UKV:
                return 1, 2048
            if c < W_MOE:
                return 2, D
            c = (c - W_MOE) % PASS_CHUNKS
            return (4, EC) if c < 16 else (2, D) if c < 22 else (1, D)

        IN_COLS = [3 * DA, 3 * DA + 256, 3 * DA + DL, 3 * DA + DL + 256, 0, 256, DA, DA + 256, 2 * DA, 2 * DA + 256]

        def dram_chunk(c):
            k, n = chunk_shape(c)
            if c < W_OUT:
                return kn(a["w_in"][0], 0, k, IN_COLS[c], n)
            if c < W_UP:
                return kn(a["w_out"][0], 2 * (c - W_OUT), k, 0, n)
            if c < W_DOWN:
                g = c - W_UP
                return kn(a["w_up"][0], 0, k, (1 - g % 2) * FF + g // 2 * 256, n)
            if c < W_QKV:
                return kn(a["w_down"][0], 2 * (c - W_DOWN), k, 0, n)
            if c < W_NAO:
                return kn(a["na_w_qkv_2"][0], 0, k, 256 * (c - W_QKV), n)
            if c < W_GU:
                return kn(a["na_w_o_2"][0], 2 * (c - W_NAO), k, 0, n)
            if c < W_DN2:
                g = c - W_GU
                return kn(a["ffn_w_gu_2"][0], 0, k, g % 2 * FF + g // 2 * 256, n)
            if c < W_MDN:
                return kn(a["ffn_w_down_2"][0], 2 * (c - W_DN2), k, 0, n)
            if c < W_UQ:
                return kn(a["mla_w_down_2"][0], 0, k, (c - W_MDN) * n, n)
            if c < W_UKV:
                return kn(a["mla_w_uq_2"][0], 0, k, (c - W_UQ) * n, n)
            if c < W_MLO:
                return kn(a["mla_w_ukv_2"][0], 0, k, 0, n)
            return kn(a["mla_w_o_2"][0], 2 * (c - W_MLO), k, 0, n)

        raw_in = [sem(f"raw_in{s}") for s in range(NRAW)]
        moe_in = [sem(f"moe_in{s}") for s in range(MOE_RAW)]
        ada_in = [sem(f"ada_in{s}") for s in range(NADA)]
        hi_done, lo_done, mm_done = sem("hi_done"), sem("lo_done"), sem("mm_done")
        ada_used = sem("ada_used")

        def attention_plan(n):
            causal = n == 1
            seg = [(0, 0, P), (1, P, S)] if causal else [(0, 0, S), (1, S, S)]
            return (H1 if causal else H2), causal, seg

        def number_of_passes(eng):
            return eng.value_load(eidi[0:1, N_PASS:N_PASS + 1], min_val=NE, max_val=MAX_PASSES)

        block = ctx.enter_context(nc.Block())

        @block.sync
        def _(sp):
            def load(c, src=None, reg=None, per=0):
                ck = Chunk(c, reg, per)
                if ck.first_use and ck.slot >= NRAW:
                    sp.wait_ge(sem("roped"), 1)
                elif c >= NRAW:
                    sp.wait_ge(lo_done, ck.n - ((NRAW if ck.first_use else ck.ring) - 1))
                    if reg is not None:
                        sp.sem_inc(sem("sync_step"), 1)
                k, n = chunk_shape(c)
                sp.dma_start(view(raws[ck.slot], k, n), dram_chunk(c) if src is None else src)\
                    .then_inc((moe_in if ck.moe else raw_in)[ck.slot], 16)

            def load_ada(layer, j, col=None, reg=None, per=0):
                g = layer * ADA_CHUNKS + j
                n = g if reg is None else g + reg * per
                sp.wait_ge(ada_used, n + 1)
                col = 256 * j if col is None else col
                w = a["w_ada_2"][layer].rearrange("(k p) n -> p k n", p=P)
                sp.dma_start(view(ada[:, g % NADA], KT, 256), w[:, :, bass.ds(col, 256)])\
                    .then_inc(ada_in[g % NADA], 16)

            def load_ffn(gu, w, halves, layer):
                w = w.rearrange("(k p) n -> p k n", p=P)
                with sp.Fori(0, GU_STEPS // 2) as i:
                    for s in range(2):
                        for part in range(2):
                            src = w[:, :, bass.ds(halves[part] + s * 256 + i * 512, 256)]
                            load(gu + 2 * s + part, src, i, 4)
                        if layer == 0 and s == 0:
                            sp.wait_ge(sem("ada_free"), 1)
                        if layer == 1 and s == 0:
                            sp.wait_ge(sem("ada_free2"), 1)
                        load_ada(layer, s, s * 256 + i * 512, i, 2)
                for part in range(2):
                    load(gu + 2 * (GU_STEPS - 1) + part)
                load_ada(layer, GU_STEPS - 1)
                for c in range(2):
                    load(gu + 2 * GU_STEPS + c)
                for j in range(GU_STEPS, ADA_IN_GU):
                    load_ada(layer, j)

            for c in range(W_UP):
                load(c)
            load_ffn(W_UP, a["w_up"][0], [FF, 0], 0)
            for c in range(DN_CHUNKS):
                load(W_DOWN + c + 2)
                load_ada(0, ADA_IN_GU + c)
            for c in range(W_QKV + 2, W_GU):
                load(c)
            load_ffn(W_GU, a["ffn_w_gu_2"][0], [0, FF], 1)
            for c in range(DN_CHUNKS):
                load(W_DN2 + c + 2)
                load_ada(1, ADA_IN_GU + c)
            for c in range(W_MDN + 2, W_MOE):
                load(c)

            gu = a["moe_w_gu_2"][0].rearrange("e (k p) n -> p e k n", p=P)
            dn = a["moe_w_down_2"][0].rearrange("e (k p) n -> p e k n", p=P)

            def expert_chunk(c, e):
                if c < 16:
                    j, part, half = c // 4, c % 4 // 2, c % 2
                    return gu[:, bass.ds(e, 1), 4 * half:4 * half + 4, part * ED + j * EC:part * ED + (j + 1) * EC]\
                        .rearrange("p e k n -> p (e k) n")
                k0 = 2 * (c - 16) if c < 22 else 12 + c - 22
                return dn[:, bass.ds(e, 1), k0:k0 + chunk_shape(W_MOE + c)[0], :].rearrange("p e k n -> p (e k) n")

            for c in range(MOE_SPLIT):
                load(W_MOE + c, expert_chunk(c, 0))
            sp.wait_ge(sem("experts_known"), 1)
            passes = number_of_passes(sp)
            with sp.Fori(0, passes) as p:
                e = sp.value_load(eidi[0:1, bass.ds(p, 1)], min_val=0, max_val=NE - 1)
                for c in range(MOE_SPLIT, PASS_CHUNKS):
                    load(W_MOE + c, expert_chunk(c, e), p, PASS_CHUNKS)
                e2 = sp.value_load(eidi[0:1, bass.ds(p + 1, 1)], min_val=0, max_val=NE - 1)
                for c in range(MOE_SPLIT):
                    load(W_MOE + PASS_CHUNKS + c, expert_chunk(c, e2), p, PASS_CHUNKS)
            for c in range(MOE_SPLIT):
                ck = Chunk(W_MOE + c, passes, PASS_CHUNKS)
                sp.wait_ge(moe_in[ck.slot], 16 * ck.loads)
                sp.sem_inc(sem("sync_step"), 1)
            sp.wait_ge(sem("result"), NT)
            sp.dma_start(out[0].rearrange("(t p) n -> p t n", p=P), xn).then_inc(sem("stored"), 16)
            sp.wait_ge(sem("stored"), 16)

        @block.tensor
        def _(pe):
            def columns_form(ck, f, psum_ap, k_tiles, width, bhi, blo):
                h, l = (view(w[ck.half], k_tiles, width) for w in (whi, wlo))
                cols = slice(f * P, f * P + P)
                for k in range(k_tiles):
                    pe.matmul(psum_ap, h[:, k, cols], bhi[:, k], start=(k == 0), stop=False)
                    pe.matmul(psum_ap, h[:, k, cols], blo[:, k], start=False, stop=False)
                    m = pe.matmul(psum_ap, l[:, k, cols], bhi[:, k], start=False, stop=(k == k_tiles - 1))
                return m

            def rows_form(ck, k_tiles, width, k0, k_all, bhi, blo, toks, psums):
                h, l = (view(w[ck.half], k_tiles, width) for w in (whi, wlo))
                for t in toks:
                    tok = slice(t * P, t * P + P)
                    mine = [(n0, n, o) for tt, n0, n, o in psums if tt == t]
                    for k in range(k_tiles):
                        first, last = k0 + k == 0, k0 + k == k_all - 1
                        for n0, n, o in mine:
                            pe.matmul(o, bhi[:, k0 + k, tok], h[:, k, n0:n0 + n], start=first, stop=False)
                        for n0, n, o in mine:
                            pe.matmul(o, bhi[:, k0 + k, tok], l[:, k, n0:n0 + n], start=False, stop=False)
                        for n0, n, o in mine:
                            m = pe.matmul(o, blo[:, k0 + k, tok], h[:, k, n0:n0 + n], start=False, stop=last)
                return m

            def begin(c, reg=None, per=0):
                ck = Chunk(c, reg, per)
                pe.wait_ge(lo_done, ck.n + 1)
                return ck

            def transposes(s, tiles=KT):
                pe.wait_ge(sem("xn_ready"), XN0[s] + NT)
                for k in range(tiles):
                    for t in range(NT):
                        m = pe.transpose(ps[:, k // 2, k % 2 * S + t * P:k % 2 * S + t * P + P],
                                         xn[:, t, k * P:(k + 1) * P], ident)
                    m.then_inc(sem("turned"), 1)

            def output_projection(first, k_all, bhi, blo, s):
                outs = [(t, n * 512, 512, ps[:, 4 + 2 * t + n, :]) for t in range(NT) for n in range(2)]
                for c in range(k_all // 2):
                    ck = begin(first + c)
                    m = rows_form(ck, 2, D, 2 * c, k_all, bhi, blo, range(NT), outs)
                    m.then_inc(mm_done, 1)

            def gate_up_step(gu, s, first, reg=None):
                j = s if reg is None else 2 * reg + s
                if reg is None:
                    j = GU_STEPS - 1
                pe.wait_ge(sem(f"gu_free{first}"), j + 1)
                for part in range(2):
                    ck = begin(gu + 2 * s + part, reg, 4) if reg is not None else begin(gu + 2 * j + part)
                    for f in range(2):
                        m = columns_form(ck, f, ps[:, 2 * s + part, f * S:(f + 1) * S], KT, 256, ahi, alo)
                    m.then_inc(mm_done, 1)

            def gate_up(gu, stage):
                pe.wait_ge(sem("aT_ready"), TURN0[stage] + KT)
                with pe.Fori(0, GU_STEPS // 2) as i:
                    for s in range(2):
                        gate_up_step(gu, s, stage, i)
                gate_up_step(gu, 0, stage)

            def modulation(layer):
                pe.wait_ge(ada_used, NADA + ADA_CHUNKS * (layer + 1))
                pe.wait_ge(sem(f"gu_free{1 + 2 * layer}"), GU_STEPS + 2)
                tiles = [c for c in range(6 * KT) if c // KT not in (2, 5)]
                for n, c in enumerate(tiles):
                    m = pe.matmul(ps[:, 0, n:n + 1], acc[:, c * P:(c + 1) * P], ones[:, 0:1], start=True, stop=True)
                m.then_inc(sem(f"mod_sum{layer}"), 1)
                for g in range(2):
                    for n in range(2):
                        b = 1 + 2 * g + n
                        if b == 4:
                            pe.wait_ge(sem(f"mod_read{layer}"), 1)
                        col = (2 + 3 * g) * D + n * 512
                        m = pe.matmul(ps[:, b % 4, :], ones, acc[:, col:col + 512], start=True, stop=True)
                m.then_inc(sem(f"gate_sum{layer}"), 1)

            def attention(n, q_ap, k_ap, v_ap, before=None):
                heads, causal, seg = attention_plan(n)
                for i in range(-1 if before else 0, heads + 3):
                    if before and i + 1 < heads:
                        before(i + 1)
                    if 0 <= i < heads:
                        if i >= 2:
                            pe.wait_ge(sem("a_exp" if before else "a_sfree"), HEADS0[n] + i - 1)
                        if before:
                            pe.wait_ge(sem("a_qkT"), i + 1)
                        for qt, col, w in seg:
                            m = pe.matmul(ps[:, i % 2, col:col + w], q_ap(i)[:, qt * P:(qt + 1) * P],
                                          k_ap(i)[:, 0:w], start=True, stop=True)
                        m.then_inc(sem("a_score"), 1)
                    h = i - 2
                    if 0 <= h < heads:
                        pe.wait_ge(sem("a_norm"), HEADS0[n] + h + 1)
                        if h >= 2:
                            pe.wait_ge(sem("a_pT"), HEADS0[n] + h - 1)
                        for qt, col, w in seg:
                            for kt in range(w // P):
                                m = pe.transpose(ps[:, 2 + h % 2, kt * S + qt * P - (P if causal and kt else 0):][:, 0:P],
                                                 core[n][1][:, h % 3, col + kt * P:col + kt * P + P], ident)
                        m.then_inc(sem("a_turned"), 1)
                    h = i - 3
                    if 0 <= h < heads:
                        pe.wait_ge(sem("a_pT"), HEADS0[n] + h + 1)
                        if h % 2 == 0 and h >= 4:
                            pe.wait_ge(sem("a_out"), HEADS0[n] // 2 + h // 2 - 1)
                        half = slice(HD * (h % 2), HD * (h % 2) + HD)
                        o = ps[half, 4 + h // 2 % 2, :]
                        pT = core[n][2][:, h % 2]
                        pe.matmul(o[:, 0:S], v_ap(h, 0), pT[:, 0:S], start=True, stop=False)
                        if causal:
                            m = pe.matmul(o[:, P:S], v_ap(h, 1), pT[:, S:S + P], start=False, stop=True)
                        else:
                            m = pe.matmul(o[:, 0:S], v_ap(h, 1), pT[:, S:2 * S], start=False, stop=True)
                        m.then_inc(sem("a_pv"), 1)

            core = {1: core1, 2: core2, 3: core3}

            pe.wait_ge(sem("cst_in"), 16)
            pe.wait_ge(sem("rows_in"), 16 * ROW_DMAS)
            for n, (col, count) in enumerate(VEC_TILES):
                m = pe.transpose(ps[:, 0, n * P:n * P + count], rows[0:count, n, :], ident[0:count, 0:count])
            m.then_inc(sem("vec_turned"), 1)
            pe.wait_ge(sem("relb_in"), 16)
            pe.matmul(ps[0:H1, 1, 0:S], relb, cst[0:NBK, C_HOT:C_HOT + S], start=True, stop=True)\
                .then_inc(sem("rel_mm"), 1)

            pe.wait_ge(sem("vecs_ready"), 1)
            pe.wait_ge(sem("rel_read"), 1)
            transposes(0)
            pe.wait_ge(sem("aT_ready"), TURN0[0] + KT)

            def projection(first, chunks, v_from, tag):
                for c in range(chunks):
                    if c >= 4:
                        pe.wait_ge(sem(f"{tag}_free"), c - 3)
                    ck = begin(first + c)
                    b = 4 + c % 4
                    if c < v_from:
                        for f in range(2):
                            m = columns_form(ck, f, ps[:, b, f * S:(f + 1) * S], KT, 256, ahi, alo)
                    else:
                        m = rows_form(ck, KT, 256, 0, KT, ahi, alo, range(NT),
                                      [(t, 0, 256, ps[:, b, t * S:(t + 1) * S]) for t in range(NT)])
                    m.then_inc(mm_done, 1)

            projection(W_IN, 10, 8, "in")
            pe.wait_ge(sem("wri_in"), 1)
            pe.wait_ge(sem("xc_ready"), LT)
            for g, w in enumerate((wr, wi)):
                for k in range(LT):
                    m = pe.matmul(ps[:, 2 * g + k // 2, k % 2 * S:(k % 2 + 1) * S], w[:, k, :], lru[0][:, k, :],
                                  start=True, stop=True)
                m.then_inc(sem("ri_mm"), 1)
            pe.wait_ge(sem("qkv_ready"), 1)
            pe.wait_ge(sem("ri_read"), 2)

            def head(ap):
                return lambda h: ap[HD * (h % 2):HD * (h % 2) + HD, h // 2, :]

            attention(1, head(qT1), head(kT1), lambda h, kt: v1[:, kt, HD * h:HD * h + HD])
            pe.wait_ge(sem("mix_ready"), 1)
            output_projection(W_OUT, KT, ahi, alo, 0)
            transposes(1)
            gate_up(W_UP, 1)
            pe.wait_ge(sem("gT_ready1"), GU_STEPS)
            output_projection(W_DOWN, FT, ghi, glo, 1)
            modulation(0)
            pe.wait_ge(sem("gate_read0"), 1)
            transposes(2)
            pe.wait_ge(sem("aT_ready"), TURN0[2] + KT)
            projection(W_QKV, 12, 8, "qkv2")
            pe.wait_ge(sem("qkv2_free"), 12)
            attention(2, head(qT2), head(kT2), lambda h, kt: v2[:, kt, HD * h:HD * h + HD])
            pe.wait_ge(sem("mix_ready2"), 1)
            output_projection(W_NAO, KT, ahi, alo, 2)
            transposes(3)
            gate_up(W_GU, 3)
            pe.wait_ge(sem("gT_ready3"), GU_STEPS)
            output_projection(W_DN2, FT, ghi, glo, 3)
            modulation(1)
            pe.wait_ge(sem("gate_read1"), 1)
            transposes(4)
            pe.wait_ge(sem("aT_ready"), TURN0[4] + KT)
            for c in range(2):
                ck = begin(W_MDN + c)
                n = MLA_DN // 2
                rows_form(ck, KT, n, 0, KT, ahi, alo, range(NT),
                          [(t, 0, n, ps[:, 4 + t + 2 * c, 0:n]) for t in range(NT)]).then_inc(mm_done, 1)
            transposes("m", 3)
            pe.wait_ge(sem("aT_ready"), TURN0["m"] + 3)
            for c in range(2):
                ck = begin(W_UQ + c)
                rows_form(ck, 2, 768, 0, 2, ahi, alo, range(NT),
                          [(t, n * 384, 384, ps[:, 4 * c + 2 * t + n, 0:384]) for t in range(NT) for n in range(2)])\
                    .then_inc(mm_done, 1)
            ck = begin(W_UKV)
            for t in range(NT):
                pe.wait_ge(sem("uq_read"), 2)
                m = rows_form(ck, 1, 2048, 0, 1, ahi[:, 2:3], alo[:, 2:3], [t],
                              [(t, n * 512, 512, ps[:, 4 * t + n, :]) for n in range(4)])
            m.then_inc(mm_done, 1)
            pe.wait_ge(sem("ktok_ready"), 1)
            pe.wait_ge(sem("roped"), 1)

            def mla_columns(h):
                if h >= 2:
                    pe.wait_ge(sem("a_qkT"), h - 1)
                for w, src in enumerate((qtok, ktok)):
                    for t in range(NT):
                        m = pe.transpose(ps[0:QKW, 6 + h % 2, w * S + t * P:w * S + (t + 1) * P],
                                         src[:, t, h, :], ident)
                m.then_inc(sem("a_qkmm"), 1)

            attention(3, lambda h: qkT[0:QKW, h % 2, 0:S], lambda h: qkT[0:QKW, h % 2, S:2 * S],
                      lambda h, kt: v3[:, kt, HD * h:HD * h + HD], mla_columns)
            pe.wait_ge(sem("mix_ready3"), 1)
            output_projection(W_MLO, KT, ahi, alo, 4)
            transposes(5)
            pe.wait_ge(sem("aT_ready"), TURN0[5] + KT)
            pe.wait_ge(sem("router_ready"), 1)
            for t in range(NT):
                tok = slice(t * P, t * P + P)
                o = ps[:, 4, t * NE:(t + 1) * NE]
                for k in range(KT):
                    pe.matmul(o, ahi[:, k, tok], rthi[:, k], start=(k == 0), stop=False)
                    pe.matmul(o, ahi[:, k, tok], rtlo[:, k], start=False, stop=False)
                    m = pe.matmul(o, alo[:, k, tok], rthi[:, k], start=False, stop=(k == KT - 1))
            m.then_inc(sem("logits"), 1)
            pe.wait_ge(sem("chosen"), 1)
            sel = [rw[:, 8 + t, :] for t in range(NT)]
            tri = cst[:, C_TRI:C_TRI + P]
            pe.matmul(ps[:, 5, 0:NE], tri, sel[0], start=True, stop=True)
            pe.matmul(ps[:, 5, NE:2 * NE], tri, sel[1], start=True, stop=False)
            pe.matmul(ps[:, 5, NE:2 * NE], ones, sel[0], start=False, stop=True)
            pe.matmul(ps[:, 5, 2 * NE:3 * NE], ones, sel[0], start=True, stop=False)
            pe.matmul(ps[:, 5, 2 * NE:3 * NE], ones, sel[1], start=False, stop=True).then_inc(sem("places"), 1)

            def gather(count):
                pe.wait_ge(sem("pick_ready"), count)
                for k in range(KT):
                    for t in range(NT):
                        m = pe.matmul(ps[:, 6 + k // 4, k % 4 * P:(k % 4 + 1) * P], xn[:, t, k * P:(k + 1) * P],
                                      pick[:, t, :], start=(t == 0), stop=(t == NT - 1))
                m.then_inc(sem("gathered"), 1)

            def combine(t):
                for n in range(2):
                    m = pe.matmul(ps[:, 6 + n, :], pickT[:, t * P:(t + 1) * P], dc[:, n * 512:(n + 1) * 512],
                                  start=True, stop=True)
                m.then_inc(sem("combined"), 1)

            def turn_gated(q):
                for k in range(4 * q, min(4 * q + 4, ET)):
                    m = pe.transpose(ps[:, q, (k - 4 * q) * P:(k - 4 * q + 1) * P], ge[:, k * P:(k + 1) * P], ident)
                m.then_inc(sem("ge_turned"), 1)

            gather(1)
            pe.wait_ge(sem("experts_known"), 1)
            passes = number_of_passes(pe)
            with pe.Fori(0, passes) as p:
                pe.wait_ge(sem("hc_ready"), 1 + p)
                for j in range(4):
                    if j >= 2:
                        pe.wait_ge(sem("ge_ready"), (j + 3) + 4 * p)
                    elif j == 0:
                        pe.wait_ge(sem("gc_ready"), 4 + 4 * p)
                    for part in range(2):
                        for half in range(2):
                            ck = begin(W_MOE + 4 * j + 2 * part + half, p, PASS_CHUNKS)
                            h, l = (view(w[ck.half], 4, EC) for w in (whi, wlo))
                            o = ps[:, (2 * j + part) % 4, 0:EC]
                            for k in range(4):
                                kk = 4 * half + k
                                pe.matmul(o, hchi[:, kk], h[:, k], start=(kk == 0), stop=False)
                                pe.matmul(o, hchi[:, kk], l[:, k], start=False, stop=False)
                                m = pe.matmul(o, hclo[:, kk], h[:, k], start=False, stop=(kk == KT - 1))
                            m.then_inc(mm_done, 1)
                        if (j, part) == (3, 0):
                            pe.wait_ge(sem("ge_ready"), 7 + 4 * p)
                            turn_gated(0)
                            turn_gated(1)
                    if j == 0:
                        pe.wait_ge(sem("dc_ready"), 1 + p)
                        combine(0)
                    if j == 1:
                        pe.wait_ge(sem("y_added"), 1 + 2 * p)
                        combine(1)
                    if j == 2:
                        pe.wait_ge(sem("y_added"), 2 + 2 * p)
                        for t in range(NT):
                            m = pe.transpose(ps[:, 6, t * P:(t + 1) * P], pick[:, t, :], ident)
                        m.then_inc(sem("pick_turned"), 1)
                k0 = 0
                for c in range(16, PASS_CHUNKS):
                    kc = chunk_shape(W_MOE + c)[0]
                    pe.wait_ge(sem("gc_ready"), (4 + (k0 + kc - 1) // 4 + 1) + 4 * p)
                    ck = begin(W_MOE + c, p, PASS_CHUNKS)
                    h, l = (view(w[ck.half], kc, D) for w in (whi, wlo))
                    for k in range(kc):
                        for lhs, rhs, stop in ((gchi, h, False), (gchi, l, False), (gclo, h, k0 + k == ET - 1)):
                            for n in range(2):
                                m = pe.matmul(ps[:, 4 + n, :], lhs[:, k0 + k], rhs[:, k, n * 512:(n + 1) * 512],
                                              start=(k0 + k == 0 and rhs is h and lhs is gchi), stop=stop)
                    m.then_inc(mm_done, 1)
                    k0 += kc
                    if c == 16:
                        pe.wait_ge(sem("ge_ready"), 8 + 4 * p)
                        turn_gated(2)
                        turn_gated(3)
                    if c == 17:
                        pe.wait_ge(sem("pickT_ready"), 2 + p)
                        gather(2 + p)
            pe.wait_ge(sem("dc_ready"), 1 + passes)
            pe.wait_ge(sem("hc_ready"), 1 + passes)
            combine(0)
            pe.wait_ge(sem("y_added"), 1 + 2 * passes)
            combine(1)

        @block.scalar
        def _(act):
            own = Chain(act, sem("act_own"))
            core = {1: core1, 2: core2, 3: core3}

            def split(c, reg=None, per=0):
                ck = Chunk(c, reg, per)
                act.wait_ge((moe_in if ck.moe else raw_in)[ck.slot], 16 * ck.loads)
                if ck.first_half and ck.half >= NSPLIT:
                    act.wait_ge(sem("logits"), 1)
                elif c >= NSPLIT:
                    act.wait_ge(mm_done, ck.n - ((NSPLIT if ck.first_half else ck.halves) - 1))
                k, n = chunk_shape(c)
                act.activation(whi[ck.half][:, 0:k * n], raws[ck.slot][:, 0:k * n], ACT.Copy).then_inc(hi_done, 1)

            def rms(s, src, first_wait, n=D, outs=None):
                for t in range(NT):
                    first_wait(t)
                    act.activation(xn[:, t, 0:n], src(t), ACT.Square, accum_out=ss[:, t:t + 1])\
                        .then_inc(sem("sum_squares"), 1)
                act.wait_ge(sem("sum_squares"), NT * (RMS0[s] + 1))
                act.activation(std, ss, ACT.Sqrt, scale=1.0 / n, bias=epsc).then_inc(sem("std"), 1)

            def norm(s):
                rms(s, lambda t: x[:, t], lambda t: act.wait_ge(sem("x_ready"), NT * (s - 1) + t + 1) if s else act.wait_ge(sem("x_in"), 16))

            def turned(s, tiles=KT):
                for k in range(tiles):
                    act.wait_ge(sem("modulated"), TURN0[s] + k + 1)
                    act.activation(ahi[:, k], hm[:, k % 2], ACT.Copy).then_inc(sem("aT_hi"), 1)

            def ld(dst, src, s, n=16):
                act.dma_start(dst, src).then_inc(sem(s), n)

            xv = a["x"][0].rearrange("(t p) n -> p t n", p=P)
            ld(x, xv, "x_in")
            for name, (tile, row, count, _) in VEC.items():
                ld(rows[row:row + count, tile, :], VEC_SRC[name](a), "rows_in")
            ld(cst, a["consts"], "cst_in")
            ld(relb, a["rel_bias"], "relb_in")
            for w, dram in ((wr, a["w_r"]), (wi, a["w_i"])):
                act.wait_ge(sem("wri_zero"), 1)
                v = dram[0].rearrange("(k two) c d -> two c k d", two=2)
                for two in range(2):
                    ld(w[64 * two:64 * two + 64, :, 64 * two:64 * two + 64], v[two], "wri_dma")
            act.dma_start(gvec, a["g_post_mix"][0:1, :].broadcast_to([P, D])).then_inc(sem("gvec_in"), 16)

            act.wait_ge(sem("eps_set"), 1)
            norm(0)
            act.wait_ge(sem("vecs_ready"), 1)
            act.activation(lamw[:, 0], vec("lam"), ACT.Abs).then_inc(sem("lam_abs"), 1)
            act.wait_ge(sem("lam_abs"), 1)
            act.activation(lamw[:, 1], lamw[:, 0], ACT.Exp, scale=-1.0).then_inc(sem("lam_exp"), 1)
            act.activation(vec("c"), vec("c"), ACT.Silu).then_inc(sem("c_ready"), 1)
            turned(0)

            act.wait_ge(sem("tbl_ready"), 1)
            ld(scratch, tbl, "tbl_out")
            act.wait_ge(sem("tbl_out"), 16)
            for off, col, w in ((P, 0, P), (0, P, S)):
                src = bass.AP(scratch.tensor, scratch.offset + off, [[1, P], [512, H1], [1, w]])
                ld(bias1[:, :, col:col + w], src, "bias1_in")

            split(0)
            split(1)
            wc, bc = vec("w_conv_lru"), vec("b_conv_lru")
            for c in range(10):
                split(c + 2)
                act.wait_ge(mm_done, W_IN + c + 1)
                b = 4 + c % 4
                if c < 2:
                    for f in range(2):
                        k = 2 * c + f
                        act.activation(lru[0][:, k], ps[:, b, f * S:(f + 1) * S], ACT.Identity,
                                       scale=wc[:, 3 * LT + k:3 * LT + k + 1], bias=bc[:, k:k + 1])\
                            .then_inc(sem("tap3"), 1)
                    continue
                dst = lru[1] if c < 4 else qT1 if c < 6 else kT1 if c < 8 else v1
                if c < 8:
                    k = 2 * (c % 2)
                    o = dst[:, k:k + 2, :]
                    i = ps[:, b, :].rearrange("p (f s) -> p f s", f=2)
                else:
                    o = v1[:, :, 256 * (c - 8):256 * (c - 8) + 256]
                    i = ps[:, b, :].rearrange("p (t n) -> p t n", t=NT)
                if 4 <= c < 6:
                    o, i = o.rearrange("p f (b n) -> p (f b) n", n=P), reversed_in(ps[:, b, :], P)
                act.activation(o, i, ACT.Gelu_apprx_tanh if c < 4 else ACT.Copy).then_inc(sem("in_free"), 1)
            for g, (name, dst) in enumerate((("b_r", lru[2]), ("b_i", lru[3]))):
                act.wait_ge(sem("ri_mm"), g + 1)
                for k in range(LT):
                    m = act.activation(dst[:, k], ps[:, 2 * g + k // 2, k % 2 * S:(k % 2 + 1) * S], ACT.Sigmoid,
                                       bias=vec(name)[:, k:k + 1])
                m.then_inc(sem("ri_read"), 1)
            act.wait_ge(sem("ri_read"), 2)
            act.wait_ge(sem("sp_ready"), 1)
            for k in range(LT):
                act.activation(lru[4][:, k], lru[2][:, k], ACT.Tanh, scale=sp8[:, k:k + 1]).then_inc(sem("tanh_a"), 1)
            act.wait_ge(sem("tanh_a"), LT)
            for k in range(LT):
                act.activation(lru[2][:, k], lru[2][:, k], ACT.Exp, scale=sp8[:, k:k + 1]).then_inc(sem("exp_a"), 1)

            def attention(n, scale, between=None, side=None):
                heads, causal, seg = attention_plan(n)
                biased = n != 3
                for i in range(-1 if side else 0, heads + 5):
                    if side and 0 <= i + 1 < heads:
                        side(i + 1)
                    if 0 <= i < heads:
                        act.wait_ge(sem("a_max"), HEADS0[n] + i + 1)
                        if i >= 3:
                            act.wait_ge(sem("a_turned"), HEADS0[n] + i - 2)
                        for s, (qt, col, w) in enumerate(seg):
                            src = core[n][0][:, i % 2, col:col + w] if biased else ps[:, i % 2, col:col + w]
                            m = act.activation(core[n][1][:, i % 3, col:col + w], src, ACT.Exp,
                                               scale=1.0 if biased else scale,
                                               bias=(mx if biased else nmx)[:, i, qt:qt + 1],
                                               accum_out=sume[:, i, qt:qt + 1])
                        m.then_inc(sem("a_exp"), 1)
                    h = i - 2
                    if 0 <= h < heads:
                        act.wait_ge(sem("a_turned"), HEADS0[n] + h + 1)
                        if h >= 2:
                            act.wait_ge(sem("a_pv"), HEADS0[n] + h - 1)
                        w = 384 if causal else 512
                        o, src = core[n][2][:, h % 2, 0:w], ps[:, 2 + h % 2, 0:w]
                        if biased:
                            run = P if causal else GW
                            o, src = o.rearrange("p (b n) -> p b n", n=run), reversed_in(src, run)
                        act.activation(o, src, ACT.Copy)\
                            .then_inc(sem("a_pT"), 1)
                    h = i - 4
                    if 0 <= h < heads and h % 2 == 1:
                        j = h // 2
                        act.wait_ge(sem("a_pv"), HEADS0[n] + h + 1)
                        act.activation(ahi[:, j], ps[:, 4 + j % 2, 0:S], ACT.Copy).then_inc(sem("a_ohi"), 1)

            def residual_rms(s, first):
                act.wait_ge(mm_done, first)
                rms(f"r{s}", lambda t: ps[:, 4 + 2 * t:6 + 2 * t, :].rearrange("p b n -> p (b n)"), lambda t: None)

            def down(first, chunks, s):
                for c in range(chunks):
                    split(first + c + 2)

            for k in range(LT):
                act.wait_ge(sem("lru_v"), k + 1)
                act.activation(lru[4][:, k], lru[4][:, k], ACT.Sqrt).then_inc(sem("lru_sqrt"), 1)
            attention(1, 1.0)
            for k in range(LT):
                act.wait_ge(sem("lru_out"), k + 1)
                act.activation(ahi[:, LT + k], lru[0][:, k], ACT.Copy).then_inc(sem("lru_hi"), 1)

            down(W_OUT, 4, 0)
            residual_rms(0, W_UP)
            norm(1)
            act.dma_start(gvec, a["g_post_ffn"][0:1, :].broadcast_to([P, D])).then_inc(sem("gvec_in"), 16)
            turned(1)

            def ffn_conv(j, s):
                taps, b = vec("w_conv_ffn2"), vec("b_conv_ffn")
                for h in range(2):
                    for f in range(2):
                        k = (1 - h) * FT + f + 2 * j
                        m = act.activation(cv[:, h, f], ps[:, 2 * s + h, f * S:(f + 1) * S], ACT.Identity,
                                           scale=taps[:, bass.ds(k, 1)], bias=b[:, bass.ds(k, 1)])
                m.then_inc(sem("tap2"), 1)
                act.wait_ge(sem("conv_done"), j + 1)
                act.activation(cv[:, 0], cv[:, 0], ACT.Gelu_apprx_tanh).then_inc(sem("gelu_done"), 1)

            def gate_up(gu, stage):
                def evac(j, s, used):
                    act.wait_ge(mm_done, used)
                    act.wait_ge(sem(f"pr_ready{stage}"), j + 1)
                    if stage == 1:
                        ffn_conv(j, s)
                    else:
                        act.activation(cv[:, 0].rearrange("p f s -> p (f s)"), ps[:, 2 * s, :], ACT.Silu)\
                            .then_inc(sem("silu_done"), 1)

                with act.Fori(0, GU_STEPS // 2) as i:
                    for s in range(2):
                        split(gu + 2 * s + 2, i, 4)
                        split(gu + 2 * s + 3, i, 4)
                        evac(2 * i + s, s, (gu + 2 * s + 2) + 4 * i)
                split(gu + 2 * GU_STEPS)
                split(gu + 2 * GU_STEPS + 1)
                evac(GU_STEPS - 1, 0, gu + 2 * GU_STEPS)

            gate_up(W_UP, 1)
            down(W_DOWN, DN_CHUNKS, 1)
            residual_rms(1, W_QKV)
            for g in range(2):
                src = a["b_ada_2"][0:1, (2 + 3 * g) * D:(3 + 3 * g) * D].broadcast_to([P, D])
                act.dma_start(gates[:, g], src).then_inc(sem("gbias_in"), 16)
            norm(2)
            for hb in range(2):
                for r in range(GR):
                    if hb == 0 and r == 0:
                        act.wait_ge(sem("gate_sum0"), 1)
                    for i in range(GR):
                        rp = a["na_rpb_2"]
                        first = (hb * HB * RPB_H + i + 7 - r) * RPB_W + 15 - (GW - 1)
                        src = bass.AP(rp.tensor, rp.offset + first, [[1, GW], [RPB_H * RPB_W, HB], [1, GW]])
                        dst = bias2[hb][GW * (r % 2):GW * (r % 2) + GW, :, r // 2, i * GW:(i + 1) * GW]
                        act.dma_start(dst, src).then_inc(sem(f"bias2_in{hb}"), 16)
            turned(2)
            for c in range(12):
                split(W_QKV + c + 2)
                act.wait_ge(mm_done, W_QKV + c + 1)
                b = 4 + c % 4
                if c < 8:
                    o = (qT2 if c < 4 else kT2)[:, 2 * (c % 4):2 * (c % 4) + 2, :]
                    i = ps[:, b, :].rearrange("p (f s) -> p f s", f=2)
                else:
                    o = v2[:, :, 256 * (c - 8):256 * (c - 8) + 256]
                    i = ps[:, b, :].rearrange("p (t n) -> p t n", t=NT)
                if c < 4:
                    o, i = o.rearrange("p f (b n) -> p (f b) n", n=GW), reversed_in(ps[:, b, :], GW)
                act.activation(o, i, ACT.Copy).then_inc(sem("qkv2_free"), 1)
            attention(2, 1.0)
            down(W_NAO, 4, 2)
            norm(3)
            turned(3)
            gate_up(W_GU, 3)
            down(W_DN2, DN_CHUNKS, 3)
            act.wait_ge(sem("x_ready"), 4 * NT)
            for g in range(2):
                src = a["b_ada_2"][1:2, (2 + 3 * g) * D:(3 + 3 * g) * D].broadcast_to([P, D])
                act.dma_start(gates[:, g], src).then_inc(sem("gbias_in"), 16)
            norm(4)
            turned(4)
            split(W_UQ)
            split(W_UQ + 1)
            act.wait_ge(mm_done, W_UQ)
            act.wait_ge(sem("aT_ready"), TURN0[4] + KT)
            act.wait_ge(sem("mla_down"), 1)
            for t in range(NT):
                for w, (c0, n) in enumerate(((0, QL), (QL, KVL))):
                    act.activation(xn[:, t, 512 + c0:512 + c0 + n], xn[:, t, c0:c0 + n], ACT.Square,
                                   accum_out=ssm[:, 2 * w + t:2 * w + t + 1]).then_inc(sem("act_ssm"), 1)
            act.wait_ge(sem("act_ssm"), 4)
            act.activation(stm[:, 0:2], ssm[:, 0:2], ACT.Sqrt, scale=1.0 / QL, bias=epsc).then_inc(sem("stdm"), 1)
            act.activation(stm[:, 2:4], ssm[:, 2:4], ACT.Sqrt, scale=1.0 / KVL, bias=epsc).then_inc(sem("stdm"), 1)
            turned("m", 3)
            split(W_UKV)
            split(W_MLO)
            for c in range(2):
                act.wait_ge(mm_done, W_UQ + c + 1)
                for t in range(NT):
                    for n in range(2):
                        m = act.activation(qtok[:, t, 8 * c + 4 * n:8 * c + 4 * n + 4, :],
                                           ps[:, 4 * c + 2 * t + n, 0:384].rearrange("p (h d) -> p h d", d=QKW), ACT.Copy)
                m.then_inc(sem("uq_read"), 1)
            act.wait_ge(mm_done, W_UKV + 1)
            for t in range(NT):
                for n in range(4):
                    m = act.activation(ktok[:, t, 4 * n:4 * n + 4, 0:HD],
                                       ps[:, 4 * t + n, :].rearrange("p (h d) -> p h d", d=2 * HD)[:, :, 0:HD], ACT.Copy)
            m.then_inc(sem("k_rows"), 1)
            split(W_MLO + 1)

            def mla_columns(h):
                act.wait_ge(sem("a_qkmm"), h + 1)
                if h >= 2:
                    act.wait_ge(sem("a_score"), HEADS0[3] + h - 1)
                act.activation(qkT[0:QKW, h % 2], ps[0:QKW, 6 + h % 2, :], ACT.Copy).then_inc(sem("a_qkT"), 1)

            attention(3, QKW ** -0.5, side=mla_columns)
            for c in range(4):
                split(W_MLO + c + 2)
            norm(5)
            turned(5)
            act.wait_ge(sem("router_in"), 1)
            act.activation(rthi.rearrange("p k e -> p (k e)"), rtr, ACT.Copy).then_inc(sem("router_hi"), 1)
            for t in range(NT):
                act.wait_ge(sem("router_max"), 1)
                act.activation(rw[:, t, :], ps[:, 4, t * NE:(t + 1) * NE], ACT.Exp, bias=nmx[:, 0, t:t + 1],
                               accum_out=sume[:, 0, t:t + 1]).then_inc(sem("router_exp"), 1)

            def gathered_hi(count):
                act.wait_ge(sem("hc_f32"), count)
                act.activation(hchi.rearrange("p k s -> p (k s)"), hc.rearrange("p k s -> p (k s)"), ACT.Copy)\
                    .then_inc(sem("hc_hi"), 1)

            def turned_hi(q, p):
                act.wait_ge(sem("ge_turned"), (5 + q) + 4 * p)
                n = min(4, ET - 4 * q)
                act.activation(gchi[:, 4 * q:4 * q + n].rearrange("p k s -> p (k s)"), ps[:, q, 0:n * P], ACT.Copy)\
                    .then_inc(sem("gc_hi"), 1)

            split(W_MOE + 2)
            gathered_hi(1)
            act.wait_ge(sem("experts_known"), 1)
            with act.Fori(0, number_of_passes(act)) as p:
                for c in range(PASS_CHUNKS):
                    if c in (3, 7, 11, 15):
                        j = c // 4
                        act.wait_ge(mm_done, (W_MOE + c + 1) + PASS_CHUNKS * p)
                        act.wait_ge(sem("ge_ready"), (j + 3) + 4 * p)
                        act.activation(sg[:, j % 2], ps[:, 2 * j % 4, 0:EC], ACT.Silu).then_inc(sem("sg_ready"), 1)
                    if c == 12:
                        act.wait_ge(sem("pick_turned"), 1 + p)
                        act.activation(pickT, ps[:, 6, 0:S], ACT.Copy).then_inc(sem("pickT_ready"), 1)
                    if c == 14:
                        turned_hi(0, p)
                        turned_hi(1, p)
                    if c == 17:
                        turned_hi(2, p)
                        turned_hi(3, p)
                    if c == 18:
                        gathered_hi(2 + p)
                    if c == PASS_CHUNKS - 1:
                        act.wait_ge(mm_done, (W_MOE + PASS_CHUNKS) + PASS_CHUNKS * p)
                        act.activation(dc, ps[:, 4:6, :].rearrange("p b n -> p (b n)"), ACT.Copy).then_inc(sem("dc_ready"), 1)
                    split(W_MOE + c + 3, p, PASS_CHUNKS)
            rms("f", lambda t: x[:, t], lambda t: act.wait_ge(sem("x_final"), t + 1))

        @block.vector
        def _(ve):
            own = Chain(ve, sem("ve_own"))
            core = {1: core1, 2: core2, 3: core3}

            def split(c, reg=None, per=0):
                ck = Chunk(c, reg, per)
                ve.wait_ge(hi_done, ck.n + 1)
                k, n = chunk_shape(c)
                ve.tensor_tensor(wlo[ck.half][:, 0:k * n], raws[ck.slot][:, 0:k * n],
                                 whi[ck.half][:, 0:k * n].bitcast(F32), ALU.subtract).then_inc(lo_done, 1)

            def norm(s):
                ve.wait_ge(sem("std"), RMS0[s] + 1)
                own.link(ve.reciprocal(rstd, std))
                for t in range(NT):
                    ve.tensor_scalar(xn[:, t], x[:, t], rstd[:, t:t + 1], None, ALU.mult)\
                        .then_inc(sem("xn_ready"), 1)

            def turned(s, scale, shift=None, tiles=KT):
                for k in range(tiles):
                    ve.wait_ge(sem("turned"), TURN0[s] + min(tiles, k // 2 * 2 + 2))
                    if k >= 2:
                        ve.wait_ge(sem("aT_ready"), TURN0[s] + k - 1)
                    src = ps[:, k // 2, k % 2 * S:(k % 2 + 1) * S]
                    if shift is None:
                        m = ve.tensor_scalar(hm[:, k % 2], src, scale[:, k:k + 1], None, ALU.mult)
                    else:
                        m = ve.tensor_scalar(hm[:, k % 2], src, scale[:, k:k + 1], shift[:, k:k + 1], ALU.mult, ALU.add)
                    m.then_inc(sem("modulated"), 1)

            def modulate_part(layer, j, col=None, reg=None, per=0):
                g = layer * ADA_CHUNKS + j
                loads = 16 * (g // NADA + 1) if reg is None else 16 * (g // NADA + 1) + 16 * (per // NADA) * reg
                ve.wait_ge(ada_in[g % NADA], loads)
                col = 256 * j if col is None else col
                w = view(ada[:, g % NADA], KT, 256)
                cs = vec("c")
                dst = [acc[:, bass.ds(col, 256)], odd]
                marks = [None, None]
                for k in range(KT):
                    o = dst[k % 2]
                    if k == 1:
                        ve.wait_ge(ada_used, (g if reg is None else g + per * reg) + NADA)
                    if k < 2:
                        m = ve.tensor_scalar(o, w[:, k], cs[:, k:k + 1], None, ALU.mult)
                    else:
                        own.after(marks[k % 2])
                        m = ve.scalar_tensor_tensor(o, w[:, k], cs[:, k:k + 1], o, ALU.mult, ALU.add)
                    marks[k % 2] = own.mark(m)
                own.after(marks[1])
                ve.tensor_tensor(dst[0], dst[0], odd, ALU.add).then_inc(ada_used, 1)

            ve.memset(epsc, EPS).then_inc(sem("eps_set"), 1)
            ve.sem_inc(ada_used, NADA)
            z1 = own.mark(ve.memset(wr, 0.0))
            own.after(z1)
            ve.memset(wi, 0.0).then_inc(sem("wri_zero"), 1)
            ve.wait_ge(sem("x_in"), 16)
            ve.wait_ge(sem("vec_turned"), 1)
            for n, (col, count) in enumerate(VEC_TILES):
                m = ve.tensor_copy(vecs[:, col:col + count], ps[:, 0, n * P:n * P + count])
            m.then_inc(sem("vecs_ready"), 1)
            own.link(ve.memset(tbl, NEG))
            ve.wait_ge(sem("rel_mm"), 1)
            own.link(ve.tensor_copy(tbl[:, 0:S], ps[0:H1, 1, 0:S]))
            ve.sem_inc(sem("tbl_ready"), 1)
            ve.sem_inc(sem("rel_read"), 1)
            norm(0)
            turned(0, vec("g_pre_mix"))
            ve.wait_ge(sem("lam_exp"), 1)
            e_, z, z2, q = lamw[:, 1], lamw[:, 2], lamw[:, 3], lamw[:, 4]
            own.link(ve.tensor_scalar(z, e_, 2.0, None, ALU.add))
            own.link(ve.reciprocal(z2, z))
            own.link(ve.tensor_tensor(z, e_, z2, ALU.mult))
            own.link(ve.tensor_tensor(z2, z, z, ALU.mult))
            own.link(ve.memset(q, 1.0 / 17))
            for n in (15, 13, 11, 9, 7, 5, 3, 1):
                own.link(ve.tensor_tensor(q, q, z2, ALU.mult))
                own.link(ve.tensor_scalar(q, q, 1.0 / n, None, ALU.add))
            own.link(ve.tensor_tensor(q, q, z, ALU.mult))
            own.link(ve.tensor_scalar(z, vec("lam"), -1.0, 0.0, ALU.mult, ALU.max))
            own.link(ve.scalar_tensor_tensor(z, q, 2.0, z, ALU.mult, ALU.add))
            ve.tensor_scalar(sp8, z, -8.0, None, ALU.mult).then_inc(sem("sp_ready"), 1)
            ve.wait_ge(sem("wri_dma"), 64)
            ve.sem_inc(sem("wri_in"), 1)

            split(0)
            split(1)
            wc = vec("w_conv_lru")
            for c in range(10):
                split(c + 2)
                if c < 2:
                    for f in range(2):
                        k = 2 * c + f
                        ve.wait_ge(sem("tap3"), 2 * c + 2)
                        src = ps[:, 4 + c, f * S:(f + 1) * S]
                        for tap in range(CW - 1):
                            d = CW - 1 - tap
                            m = ve.scalar_tensor_tensor(lru[0][:, k, d:S], src[:, 0:S - d], wc[:, tap * LT + k:tap * LT + k + 1],
                                                        lru[0][:, k, d:S], ALU.mult, ALU.add)
                            if tap < CW - 2:
                                own.link(m)
                        m.then_inc(sem("xc_ready"), 1)
                    ve.wait_ge(sem("xc_ready"), 2 * c + 2)
                    ve.sem_inc(sem("in_free"), 1)
            ve.wait_ge(sem("in_free"), 10)
            ve.sem_inc(sem("qkv_ready"), 1)
            for k in range(LT):
                ve.wait_ge(sem("exp_a"), k + 1)
                own.link(ve.tensor_tensor(lru[5][:, k], lru[2][:, k], lru[2][:, k], ALU.mult))
                own.link(ve.scalar_tensor_tensor(lru[4][:, k], lru[5][:, k], 1.0, lru[4][:, k], ALU.add, ALU.mult))
                ve.tensor_scalar(lru[4][:, k], lru[4][:, k], -1.0, 0.0, ALU.mult, ALU.max).then_inc(sem("lru_v"), 1)
            for k in range(LT):
                own.link(ve.tensor_tensor(lru[3][:, k], lru[3][:, k], lru[0][:, k], ALU.mult))

            def attention(n, scale, bias=None, late=None):
                heads, causal, seg = attention_plan(n)
                for i in range(heads + 5):
                    if i < heads:
                        ve.wait_ge(sem("a_score"), HEADS0[n] + i + 1)
                        w_all = 384 if causal else 512
                        sc = ps[:, i % 2, 0:w_all]
                        if bias:
                            if i >= 2:
                                ve.wait_ge(sem("a_exp"), HEADS0[n] + i - 1)
                            src = core[n][0][:, i % 2, 0:w_all]
                            bias_ready(i) if n == 2 else None
                            ve.scalar_tensor_tensor(src, sc, scale, bias(i), ALU.mult, ALU.add)\
                                .then_inc(sem("a_sfree"), 1)
                            ve.wait_ge(sem("a_sfree"), HEADS0[n] + i + 1)
                        else:
                            src = sc
                        if causal:
                            own.mark(ve.tensor_reduce(mx[:, i, 0:1], src[:, 0:P], AXX, ALU.max, negate=True))
                            m = ve.tensor_reduce(mx[:, i, 1:2], src[:, P:384], AXX, ALU.max, negate=True)
                        else:
                            m = ve.tensor_reduce(mx[:, i, :], src.rearrange("p (t n) -> p t n", t=NT), AXX, ALU.max, negate=True)
                        if not bias:
                            own.link(m)
                            m = ve.tensor_scalar(nmx[:, i, :], mx[:, i, :], scale, None, ALU.mult)
                        m.then_inc(sem("a_max"), 1)
                    h = i - 1
                    if 0 <= h < heads:
                        ve.wait_ge(sem("a_exp"), HEADS0[n] + h + 1)
                        ve.reciprocal(rsum[:, h, :], sume[:, h, :]).then_inc(sem("a_rsum"), 1)
                    h = i - 4
                    if 0 <= h < heads and h % 2 == 1:
                        j = h // 2
                        ve.wait_ge(sem("a_ohi"), HEADS0[n] // 2 + j + 1)
                        ve.tensor_tensor(alo[:, j], ps[:, 4 + j % 2, 0:S], ahi[:, j].bitcast(F32), ALU.subtract)\
                            .then_inc(sem("a_out"), 1)
                    if late and 0 <= i - 1 < LT:
                        late(i - 1)

            def bias_ready(i):
                ve.wait_ge(sem("bias2_masked"), 1 + i // HB)

            def lru_late(k):
                ve.wait_ge(sem("lru_sqrt"), k + 1)
                own.link(ve.tensor_tensor(lru[3][:, k], lru[3][:, k], lru[4][:, k], ALU.mult))
                own.link(ve.tensor_tensor_scan(lru[5][:, k], lru[2][:, k], lru[3][:, k], 0.0, ALU.mult, ALU.add))
                ve.tensor_tensor(lru[0][:, k], lru[5][:, k], lru[1][:, k], ALU.mult).then_inc(sem("lru_out"), 1)

            ve.wait_ge(sem("bias1_in"), 32)
            attention(1, HD ** -0.5, lambda i: bias1[:, i, :], lru_late)
            for k in range(LT):
                ve.wait_ge(sem("lru_hi"), k + 1)
                own.mark(ve.tensor_tensor(alo[:, LT + k], lru[0][:, k], ahi[:, LT + k].bitcast(F32), ALU.subtract))
            own.after(own.count())
            ve.wait_ge(sem("a_out"), HEADS0[2] // 2)
            ve.sem_inc(sem("mix_ready"), 1)
            ve.wait_ge(sem("mix_ready"), 1)
            ve.sem_inc(sem("ada_free"), 1)

            def residual_norm(s, loads, nxt):
                ve.wait_ge(sem("std"), RMS0[f"r{s}"] + 1)
                ve.wait_ge(sem("gvec_in"), 16 * loads)
                own.link(ve.reciprocal(rstd, std))
                for t in range(NT):
                    o = ps[:, 4 + 2 * t:6 + 2 * t, :].rearrange("p b n -> p (b n)")
                    own.link(ve.scalar_tensor_tensor(xn[:, t], o, rstd[:, t:t + 1], gvec, ALU.mult, ALU.mult))
                    ve.tensor_tensor(x[:, t], x[:, t], xn[:, t], ALU.add).then_inc(sem("x_ready"), 1)

            def residual_gate(g, first, nxt):
                ve.wait_ge(mm_done, first)
                for t in range(NT):
                    o = ps[:, 4 + 2 * t:6 + 2 * t, :].rearrange("p b n -> p (b n)")
                    own.link(ve.tensor_tensor(xn[:, t], o, gates[:, g], ALU.mult))
                    ve.tensor_tensor(x[:, t], x[:, t], xn[:, t], ALU.add).then_inc(sem("x_ready"), 1)

            def down(first, chunks, layer=None):
                for c in range(chunks):
                    split(first + c + 2)
                    if layer is not None:
                        modulate_part(layer, ADA_IN_GU + c)

            down(W_OUT, 4)
            residual_norm(0, 1, 1)
            norm(1)
            turned(1, vec("g_pre_ffn"))

            def gate_up(gu, stage, layer):
                def taps(j, s):
                    ve.wait_ge(sem("tap2"), j + 1)
                    w01 = vec("w_conv_ffn01")
                    for d in (1, 2):
                        for h in range(2):
                            for f in range(2):
                                k = (2 - d) * 2 * FT + (1 - h) * FT + f + 2 * j
                                m = own.mark(ve.scalar_tensor_tensor(
                                    cv[:, h, f, d:S], ps[:, 2 * s + h, f * S:f * S + S - d], w01[:, bass.ds(k, 1)],
                                    cv[:, h, f, d:S], ALU.mult, ALU.add))
                        own.after(m)
                    ve.sem_inc(sem("conv_done"), 1)

                def evac(j, s):
                    if stage == 1:
                        taps(j, s)
                        ve.wait_ge(sem("gelu_done"), j + 1)
                        up = cv[:, 1]
                    else:
                        ve.wait_ge(sem("silu_done"), j + 1)
                        up = ps[:, 2 * s + 1, :].rearrange("p (f s) -> p f s", f=2)
                    ve.wait_ge(sem(f"gT_ready{stage}"), j) if isinstance(j, int) and j > 0 else None
                    if not isinstance(j, int):
                        ve.wait_ge(sem(f"pr_free{stage}"), j + 1)
                    own.link(ve.tensor_tensor(pr, cv[:, 0], up, ALU.mult))
                    ve.sem_inc(sem(f"pr_ready{stage}"), 1)
                    ve.sem_inc(sem(f"gu_free{stage}"), 1)

                ve.sem_inc(sem(f"pr_ready{stage}"), 1)
                for _ in range(2):
                    ve.sem_inc(sem(f"gu_free{stage}"), 1)
                per = (9 if stage == 3 else 9 + 8) * 2
                with ve.Fori(0, GU_STEPS // 2) as i:
                    own.enter(i, per + 0)
                    for s in range(2):
                        split(gu + 2 * s + 2, i, 4)
                        split(gu + 2 * s + 3, i, 4)
                        modulate_part(layer, s, s * 256 + i * 512, i, 2)
                        evac(2 * i + s, s)
                    own.leave(GU_STEPS // 2)
                split(gu + 2 * GU_STEPS)
                split(gu + 2 * GU_STEPS + 1)
                for j in range(GU_STEPS - 1, ADA_IN_GU):
                    modulate_part(layer, j)
                evac(GU_STEPS - 1, 0)

            def modulation(layer):
                ve.wait_ge(sem(f"mod_sum{layer}"), 1)
                b = vec("b_ada")[:, layer * 6 * KT:(layer + 1) * 6 * KT]
                for n, part in enumerate((0, 1, 3, 4)):
                    m = ve.scalar_tensor_tensor(mod[:, n * KT:(n + 1) * KT], ps[:, 0, n * KT:(n + 1) * KT],
                                                1.0 if n % 2 else 0.0, b[:, part * KT:(part + 1) * KT], ALU.add, ALU.add)
                m.then_inc(sem(f"mod_read{layer}"), 1)

            def gate_rows(layer):
                ve.wait_ge(sem(f"gate_sum{layer}"), 1)
                ve.wait_ge(sem("gbias_in"), 32 * (layer + 1))
                for g in range(2):
                    for n in range(2):
                        o = gates[:, g, n * 512:(n + 1) * 512]
                        m = ve.tensor_tensor(o, o, ps[:, (1 + 2 * g + n) % 4, :], ALU.add)
                m.then_inc(sem(f"gate_read{layer}"), 1)

            gate_up(W_UP, 1, 0)
            down(W_DOWN, DN_CHUNKS, 0)
            residual_norm(1, 2, 2)
            modulation(0)
            gate_rows(0)
            norm(2)
            turned(2, mod[:, KT:2 * KT], mod[:, 0:KT])
            for c in range(12):
                split(W_QKV + c + 2)
            attention(2, HD ** -0.5, lambda i: bias2[i // HB][:, i % HB].rearrange("p t n -> p (t n)"))
            ve.wait_ge(sem("a_out"), HEADS0[3] // 2)
            ve.sem_inc(sem("mix_ready2"), 1)
            ve.wait_ge(sem("mix_ready2"), 1)
            ve.sem_inc(sem("ada_free2"), 1)
            down(W_NAO, 4)
            residual_gate(0, W_GU, 3)
            norm(3)
            turned(3, mod[:, 3 * KT:4 * KT], mod[:, 2 * KT:3 * KT])
            gate_up(W_GU, 3, 1)
            down(W_DN2, DN_CHUNKS, 1)
            residual_gate(1, W_MDN, 4)
            modulation(1)
            gate_rows(1)
            norm(4)
            turned(4, mod[:, KT:2 * KT], mod[:, 0:KT])
            split(W_UQ)
            split(W_UQ + 1)
            ve.wait_ge(mm_done, W_UQ)
            for t in range(NT):
                for c in range(2):
                    n = MLA_DN // 2
                    m = ve.tensor_copy(xn[:, t, c * n:(c + 1) * n], ps[:, 4 + t + 2 * c, 0:n])
            m.then_inc(sem("mla_down"), 1)
            ve.wait_ge(sem("mla_down"), 1)
            for t in range(NT):
                own.mark(ve.tensor_copy(qtok[:, t, H2, HD:QKW], xn[:, t, QL + KVL:MLA_DN]))
            ve.wait_ge(sem("stdm"), 2)
            own.link(ve.reciprocal(rsm, stm))
            for t in range(NT):
                own.mark(ve.tensor_scalar(xn[:, t, 0:QL], xn[:, t, 0:QL], rsm[:, t:t + 1], None, ALU.mult))
                ve.tensor_scalar(xn[:, t, QL:QL + KVL], xn[:, t, QL:QL + KVL], rsm[:, 2 + t:3 + t], None, ALU.mult)\
                    .then_inc(sem("xn_ready"), 1)
            own.after(own.count())
            turned("m", vecs[:, VEC["q_norm"][3]:VEC["q_norm"][3] + 3], None, 3)
            split(W_UKV)
            split(W_MLO)
            ve.wait_ge(sem("uq_read"), 2)
            shape = [P, NT, NH3, 16]
            qr = qtok[:, :, :, HD:QKW].rearrange("p t h (i two) -> p t h i two", two=2)
            trig = [cst[:, at_:at_ + 32].rearrange("p (t o i) -> p t o i", t=NT, o=1).broadcast_to(shape)
                    for at_ in (C_COS, C_SIN)]
            for n, (two, f) in enumerate(((0, 0), (1, 1), (0, 1), (1, 0))):
                for t in range(NT):
                    own.mark(ve.tensor_tensor(rt[:, n, t], qr[:, t, :, :, two], trig[f][:, t], ALU.mult))
            own.after(own.count())
            for n, op in ((0, ALU.subtract), (1, ALU.add)):
                for t in range(NT):
                    m = own.mark(ve.tensor_tensor(qr[:, t, :, :, n], rt[:, 2 * n, t], rt[:, 2 * n + 1, t], op))
            own.after(m)
            ve.sem_inc(sem("roped"), 1)
            for t in range(NT):
                k_rope = qtok[:, t, H2:NH3, HD:QKW].broadcast_to([P, H2, ROPE])
                own.mark(ve.tensor_copy(ktok[:, t, :, HD:QKW], k_rope))
            own.after(own.count())
            ve.wait_ge(sem("k_rows"), 1)

            for t in range(NT):
                for n in range(4):
                    own.mark(ve.tensor_copy(v3[:, t, n * 256:(n + 1) * 256].rearrange("p (h d) -> p h d", d=HD),
                                            ps[:, 4 * t + n, :].rearrange("p (h d) -> p h d", d=2 * HD)[:, :, HD:2 * HD]))
            own.after(own.count())
            ve.sem_inc(sem("ktok_ready"), 1)
            split(W_MLO + 1)
            attention(3, QKW ** -0.5)
            ve.wait_ge(sem("a_out"), (HEADS0[3] + H2) // 2)
            ve.sem_inc(sem("mix_ready3"), 1)
            for c in range(4):
                split(W_MLO + c + 2)
            residual_gate(0, W_MOE, 5)
            norm(5)
            turned(5, mod[:, 3 * KT:4 * KT], mod[:, 2 * KT:3 * KT])
            ve.wait_ge(sem("router_hi"), 1)
            ve.tensor_tensor(rtlo.rearrange("p k e -> p (k e)"), rtr, rthi.rearrange("p k e -> p (k e)").bitcast(F32),
                             ALU.subtract).then_inc(sem("router_ready"), 1)
            own.link(ve.memset(y, 0.0))
            own.link(ve.memset(dc, 0.0))
            own.link(ve.memset(pickT, 0.0))
            own.link(ve.memset(posn, -1.0))
            own.link(ve.memset(wcol, 0.0))
            ve.wait_ge(sem("logits"), 1)
            lg = ps[:, 4, 0:2 * NE].rearrange("p (t e) -> p t e", t=NT)
            ve.tensor_reduce(nmx[:, 0, :], lg, AXX, ALU.max, negate=True).then_inc(sem("router_max"), 1)
            ve.wait_ge(sem("router_exp"), NT)
            own.link(ve.reciprocal(rsum[:, 0, :], sume[:, 0, :]))
            full = [P, NT, NE]
            full4 = [P, NT, NE, NE]
            pr8 = rw[:, 2:4, :]
            own.link(ve.tensor_tensor(pr8, rw[:, 0:2, :], rsum[:, 0, :].rearrange("p (t o) -> p t o", o=1).broadcast_to(full), ALU.mult))
            c4 = cmp_.rearrange("p (r t e f) -> p r t e f", r=4, t=NT, e=NE)
            other = pr8.rearrange("p t (o e) -> p t o e", o=1).broadcast_to(full4)
            this = pr8.rearrange("p t (e o) -> p t e o", o=1).broadcast_to(full4)
            lt = cst[:, C_LT:C_LT + 64].rearrange("p (e f) -> p e f", e=NE)
            for t in range(NT):
                own.mark(ve.tensor_tensor(c4[:, 0, t], other[:, t], this[:, t], ALU.is_gt))
                own.link(ve.tensor_tensor(c4[:, 1, t], other[:, t], this[:, t], ALU.is_equal))
                own.link(ve.tensor_tensor(c4[:, 2, t], c4[:, 1, t], lt, ALU.mult))
                own.link(ve.tensor_tensor(c4[:, 3, t], c4[:, 0, t], c4[:, 2, t], ALU.add))
            rank, chosen, wts = rw[:, 4:6, :], rw[:, 8:10, :], rw[:, 10:12, :]
            own.link(ve.tensor_reduce(rank, c4[:, 3], AXX, ALU.add))
            ve.tensor_scalar(chosen, rank, 1.5, None, ALU.is_lt).then_inc(sem("chosen"), 1)
            ve.wait_ge(sem("chosen"), 1)
            own.link(ve.tensor_tensor(wts, pr8, chosen, ALU.mult))
            own.link(ve.tensor_reduce(rsum[:, 1, :], wts, AXX, ALU.add))
            own.link(ve.reciprocal(rsum[:, 2, :], rsum[:, 1, :]))
            own.link(ve.tensor_tensor(wts, wts, rsum[:, 2, :].rearrange("p (t o) -> p t o", o=1).broadcast_to(full), ALU.mult))
            ve.wait_ge(sem("places"), 1)
            place = rw[:, 12:14, :]
            pl = ps[:, 5, 0:2 * NE].rearrange("p (t e) -> p t e", t=NT)
            own.link(ve.scalar_tensor_tensor(place, pl, 1.0, chosen, ALU.add, ALU.mult))
            own.link(ve.tensor_scalar(posn[:, :, 0:NE], place, -1.0, None, ALU.add))
            own.link(ve.tensor_copy(wcol[:, :, 1:1 + NE], wts))

            def make_pick(col):
                for t in range(NT):
                    m = ve.tensor_scalar(pick[:, t], cst[:, C_IOTA:C_IOTA + P], posn[:, t, bass.ds(col, 1)], None, ALU.is_equal)
                m.then_inc(sem("pick_ready"), 1)

            make_pick(0)
            over, order, tmp, tmp2 = rw[:, 14, :], rw[:, 15, :], rw[:, 16, :], rw[:, 18:20, :]
            own.link(ve.tensor_scalar(over, ps[:, 5, 2 * NE:3 * NE], 128.5, None, ALU.is_gt))
            own.link(ve.tensor_tensor(c4[:, 0, 0], lt, over.rearrange("p (o e) -> p o e", o=1).broadcast_to([P, NE, NE]), ALU.mult))
            own.link(ve.tensor_reduce(order, c4[:, 0, 0], AXX, ALU.add))
            own.link(ve.memset(eidf, 0.0))
            own.link(ve.tensor_copy(eidf[:, 0:NE], cst[:, C_EID:C_EID + NE]))
            for j in range(3):
                own.link(ve.scalar_tensor_tensor(tmp, order, float(j), over, ALU.is_equal, ALU.mult))
                both = tmp.rearrange("p (o e) -> p o e", o=1).broadcast_to(full)
                own.link(ve.tensor_scalar(tmp2, place, -128.0, None, ALU.add))
                own.link(ve.tensor_tensor(tmp2, tmp2, both, ALU.mult))
                own.link(ve.tensor_reduce(rsum[:, 3, :], tmp2, AXX, ALU.add))
                own.link(ve.tensor_scalar(posn[:, :, NE + j], rsum[:, 3, :], -1.0, None, ALU.add))
                own.link(ve.tensor_tensor(tmp2, wts, both, ALU.mult))
                own.link(ve.tensor_reduce(wcol[:, :, 1 + NE + j], tmp2, AXX, ALU.add))
                own.link(ve.tensor_tensor(rw[:, 20, :], tmp, cst[:, C_EID:C_EID + NE], ALU.mult))
                own.link(ve.tensor_reduce(eidf[:, NE + j:NE + j + 1], rw[:, 20, :], AXX, ALU.add))
            own.link(ve.tensor_reduce(rw[:, 20, 0:1], over, AXX, ALU.add))
            own.link(ve.tensor_scalar(eidf[:, N_PASS:N_PASS + 1], rw[:, 20, 0:1], float(NE), None, ALU.add))
            ve.tensor_copy(eidi, eidf).then_inc(sem("experts_known"), 1)

            def gathered(count):
                ve.wait_ge(sem("gathered"), count)
                for k in range(KT):
                    m = ve.tensor_scalar(hc[:, k], ps[:, 6 + k // 4, k % 4 * P:(k % 4 + 1) * P],
                                         mod[:, 3 * KT + k:3 * KT + k + 1], mod[:, 2 * KT + k:2 * KT + k + 1], ALU.mult, ALU.add)
                m.then_inc(sem("hc_f32"), 1)

            def add_y(t, col):
                for n in range(2):
                    o = y[:, t, n * 512:(n + 1) * 512]
                    m = ve.scalar_tensor_tensor(o, ps[:, 6 + n, :], wcol[:, t, bass.ds(col, 1)], o, ALU.mult, ALU.add)
                m.then_inc(sem("y_added"), 1)

            for name in ("ge_turned", "ge_ready", "gc_ready"):
                ve.sem_inc(sem(name), 4)
            ve.sem_inc(sem("dc_ready"), 1)
            ve.sem_inc(sem("pickT_ready"), 1)
            split(W_MOE + 2)
            gathered(1)

            def turned_lo(q, p):
                ve.wait_ge(sem("gc_hi"), (q + 1) + 4 * p)
                n = min(4, ET - 4 * q)
                ve.tensor_tensor(gclo[:, 4 * q:4 * q + n].rearrange("p k s -> p (k s)"), ps[:, q, 0:n * P],
                                 gchi[:, 4 * q:4 * q + n].rearrange("p k s -> p (k s)").bitcast(F32), ALU.subtract)\
                    .then_inc(sem("gc_ready"), 1)

            ve.wait_ge(sem("experts_known"), 1)
            passes = number_of_passes(ve)
            with ve.Fori(0, passes) as p:
                for c in range(PASS_CHUNKS):
                    if c in (3, 7, 11, 15):
                        j = c // 4
                        ve.wait_ge(sem("sg_ready"), (j + 1) + 4 * p)
                        if j == 0:
                            ve.wait_ge(sem("ge_turned"), 4 + 4 * p)
                        ve.tensor_tensor(ge[:, j * EC:(j + 1) * EC], sg[:, j % 2], ps[:, (2 * j + 1) % 4, 0:EC], ALU.mult)\
                            .then_inc(sem("ge_ready"), 1)
                    if c in (4, 8):
                        t = c // 4 - 1
                        ve.wait_ge(sem("combined"), (t + 1) + 2 * p)
                        add_y(t, p)
                    if c == 12:
                        ve.wait_ge(sem("pick_turned"), 1 + p)
                        make_pick(p + 1)
                    if c == 14:
                        turned_lo(0, p)
                        turned_lo(1, p)
                    if c == 17:
                        turned_lo(2, p)
                        turned_lo(3, p)
                    if c == 18:
                        gathered(2 + p)
                    split(W_MOE + c + 3, p, PASS_CHUNKS)
            for t in range(NT):
                ve.wait_ge(sem("combined"), (t + 1) + 2 * passes)
                add_y(t, passes)
            ve.wait_ge(sem("y_added"), 2 + 2 * passes)
            for t in range(NT):
                own.link(ve.tensor_tensor(y[:, t], y[:, t], gates[:, 1], ALU.mult))
                ve.tensor_tensor(x[:, t], x[:, t], y[:, t], ALU.add).then_inc(sem("x_final"), 1)
            ve.wait_ge(sem("std"), RMS0["f"] + 1)
            own.link(ve.reciprocal(rstd, std))
            ve.wait_ge(sem("final_in"), 16)
            for t in range(NT):
                ve.scalar_tensor_tensor(xn[:, t], x[:, t], rstd[:, t:t + 1], gvec, ALU.mult, ALU.mult)\
                    .then_inc(sem("result"), 1)

        @block.gpsimd
        def _(po):
            core = {1: core1, 2: core2, 3: core3}

            def turned(s, tiles=KT):
                for k in range(tiles):
                    po.wait_ge(sem("aT_hi"), TURN0[s] + k + 1)
                    po.tensor_tensor(alo[:, k], hm[:, k % 2], ahi[:, k].bitcast(F32), ALU.subtract)\
                        .then_inc(sem("aT_ready"), 1)

            def attention(n):
                heads, causal, seg = attention_plan(n)
                for h in range(heads):
                    po.wait_ge(sem("a_rsum"), HEADS0[n] + h + 1)
                    for qt, col, w in seg:
                        v = core[n][1][:, h % 3, col:col + w]
                        m = po.tensor_scalar(v, v, rsum[:, h, qt:qt + 1], 1.0, ALU.mult, ALU.mult)
                    m.then_inc(sem("a_norm"), 1)

            def gate_up(stage):
                def step(j):
                    po.wait_ge(sem(f"pr_ready{stage}"), j + 2)
                    o = ghi[:, bass.ds(2 * j, 2), :]
                    po.tensor_copy(o, pr).then_inc(sem(f"pr_hi{stage}"), 1)
                    po.wait_ge(sem(f"pr_hi{stage}"), j + 1)
                    po.tensor_tensor(glo[:, bass.ds(2 * j, 2), :], pr, o.bitcast(F32), ALU.subtract)\
                        .then_inc(sem(f"gT_ready{stage}"), 1)
                    po.wait_ge(sem(f"gT_ready{stage}"), j + 1)
                    po.sem_inc(sem(f"pr_free{stage}"), 1)

                po.sem_inc(sem(f"pr_free{stage}"), 1)
                with po.Fori(0, GU_STEPS) as j:
                    step(j)

            po.wait_ge(sem("eps_set"), 1)
            turned(0)
            attention(1)
            turned(1)
            gate_up(1)
            turned(2)
            for hb in range(2):
                po.wait_ge(sem(f"bias2_in{hb}"), 16 * GR * GR)
                mask = cst[:, C_NAM:C_NAM + GW].rearrange("p (o j) -> p o j", o=1).broadcast_to([P, HB * NT * GR, GW])
                v = bias2[hb].rearrange("p h t (i j) -> p (h t i) j", j=GW)
                po.tensor_tensor(v, v, mask, ALU.add).then_inc(sem("bias2_masked"), 1)
            attention(2)
            turned(3)
            gate_up(3)
            turned(4)
            turned("m", 3)
            attention(3)
            po.wait_ge(sem("mix_ready3"), 1)
            po.dma_start(rtr.rearrange("p (k e) -> p k e", k=KT), a["moe_w_router_2"][0].rearrange("(k p) e -> p k e", p=P))\
                .then_inc(sem("router_dma"), 16)
            po.dma_start(gvec, a["final_norm_2"].rearrange("(o n) -> o n", o=1).broadcast_to([P, D])).then_inc(sem("final_in"), 16)
            po.wait_ge(sem("router_dma"), 16)
            po.sem_inc(sem("router_in"), 1)
            turned(5)

            def gathered_lo(count):
                po.wait_ge(sem("hc_hi"), count)
                po.tensor_tensor(hclo, hc, hchi.bitcast(F32), ALU.subtract).then_inc(sem("hc_ready"), 1)

            gathered_lo(1)
            po.wait_ge(sem("experts_known"), 1)
            with po.Fori(0, number_of_passes(po)) as p:
                gathered_lo(2 + p)


def _rows(name, rows):
    return lambda a: a[name][0].rearrange("(r c) -> r c", c=P)[0:rows]


VEC_SRC = {
    "c": _rows("c_2", 8),
    "g_pre_mix": _rows("g_pre_mix", 8),
    "g_pre_ffn": _rows("g_pre_ffn", 8),
    "w_conv_lru": lambda a: a["w_conv_lru"][0].rearrange("w (k c) -> (w k) c", c=P),
    "b_conv_lru": _rows("b_conv_lru", 4),
    "b_r": _rows("b_r", 4),
    "b_i": _rows("b_i", 4),
    "lam": _rows("lam", 4),
    "q_norm": _rows("mla_q_norm_2", 2),
    "kv_norm": _rows("mla_kv_norm_2", 1),
    "b_conv_ffn": _rows("b_conv_ffn", 44),
    "b_ada": lambda a: a["b_ada_2"].rearrange("l (k c) -> (l k) c", c=P),
    "w_conv_ffn01": lambda a: a["w_conv_ffn"][0, 0:2].rearrange("w (k c) -> (w k) c", c=P),
    "w_conv_ffn2": lambda a: a["w_conv_ffn"][0, 2:3].rearrange("w (k c) -> (w k) c", c=P),
}
ROW_DMAS = len(VEC_SRC)

_INS = ["x", "g_pre_mix", "w_in", "rel_bias", "w_conv_lru", "b_conv_lru", "w_r", "b_r", "w_i", "b_i", "lam", "w_out",
        "g_post_mix", "g_pre_ffn", "w_up", "w_conv_ffn", "b_conv_ffn", "w_down", "g_post_ffn", "c_2", "w_ada_2",
        "b_ada_2", "na_w_qkv_2", "na_rpb_2", "na_w_o_2", "ffn_w_gu_2", "ffn_w_down_2", "mla_w_down_2",
        "mla_q_norm_2", "mla_w_uq_2", "mla_kv_norm_2", "mla_w_ukv_2", "mla_w_o_2", "moe_w_router_2", "moe_w_gu_2",
        "moe_w_down_2", "final_norm_2"]


def kernel(**inputs):
    import concourse.bacc as _bacc
    from concourse.bass_utils import run_bass_kernel_spmd as _run

    nc = _bacc.Bacc("TRN2", target_bir_lowering=False, num_devices=1)
    arrays = {f"in_{n}": np.ascontiguousarray(inputs[n]) for n in _INS}
    arrays["in_consts"] = shape_constants()
    aps = {n[3:]: nc.dram_tensor(n, v.shape, mybir.dt.from_np(v.dtype), kind="ExternalInput").ap()
           for n, v in arrays.items()}
    out = nc.dram_tensor("out_0", (1, S, D), F32, kind="ExternalOutput").ap()
    blocks(nc, aps, out)
    return _run(nc, [arrays], core_ids=[0]).results[0]["out_0"]
```

```python
import math
from contextlib import ExitStack

import numpy as np

import concourse.bass as bass
from concourse import mybir

F32 = mybir.dt.float32
F32R = mybir.dt.float32r
I32 = mybir.dt.int32
ALU = mybir.AluOpType
ACT = mybir.ActivationFunctionType
AXX = mybir.AxisListType.X

P = 128
S = 256
NT = S // P
D = 1024
KT = D // P
EPS = 1e-6
HD = 64
H1 = 8
DA = H1 * HD
DL = D // 2
LT = DL // P
NBK = 32
CW = 4
FF = 2816
FT = FF // P
GU_STEPS = FT // 2
DN_CHUNKS = FT // 2
H2 = 16
GW = 64
GR = S // GW
RPB_H, RPB_W = 15, 31
QL, KVL, ROPE = 256, 128, 32
QKW = HD + ROPE
MLA_DN = QL + KVL + ROPE
NE = 8
ED = 1792
ET = ED // P
EC = ED // 4
MAX_PASSES = NE + 3
PASS_CHUNKS = 24
NEG = -1.0e30

CHUNK = 2048
NRAW, NSPLIT, NADA = 4, 2, 2
MOE_RAW, MOE_SPLIT = NRAW + NADA, NSPLIT + 1
NHM = 4
N_PASS = 15

W_IN = 0
W_OUT = W_IN + 10
W_UP = W_OUT + 4
W_DOWN = W_UP + 2 * GU_STEPS
W_QKV = W_DOWN + DN_CHUNKS
W_NAO = W_QKV + 12
W_GU = W_NAO + 4
W_DN2 = W_GU + 2 * GU_STEPS
W_MDN = W_DN2 + DN_CHUNKS
W_UQ = W_MDN + 2
W_UKV = W_UQ + 2
W_MLO = W_UKV + 1
W_MOE = W_MLO + 4

ADA_CHUNKS = 24
ADA_MIX = 3
ADA_EARLY = ADA_MIX + 2
ADA_LATE = ADA_EARLY + GU_STEPS

VEC = {}


def _plan_vectors():
    tiles = [
        [("c", 8), ("g_pre_mix", 8), ("g_pre_ffn", 8), ("w_conv_lru", 16), ("b_conv_lru", 4), ("b_r", 4),
         ("b_i", 4), ("lam", 4), ("q_norm", 2), ("kv_norm", 1), ("b_conv_ffn", 44)],
        [("b_ada", 96)],
        [("w_conv_ffn01", 88)],
        [("w_conv_ffn2", 44)],
    ]
    at = 0
    out = []
    for n, tile in enumerate(tiles):
        row = 0
        for name, rows in tile:
            VEC[name] = (n, row, rows, at + row)
            row += rows
        out.append((at, row))
        at += row
    return out, at


VEC_TILES, VEC_COLS = _plan_vectors()

C_ID, C_IOTA, C_TRI, C_ONE = 0, 128, 256, 384
C_NAM = 512
C_COS = C_NAM + GW
C_SIN = C_COS + 32
C_LT = C_SIN + 32
C_EID = C_LT + 64
C_HOT = C_EID + 8
C_SEL = C_HOT + S
C_ALL = C_SEL + 64


def shape_constants():
    c = np.zeros((P, C_ALL), np.float32)
    i = np.arange(P)
    c[:, C_ID:C_ID + P] = np.eye(P)
    c[:, C_IOTA:C_IOTA + P] = i[None, :]
    c[:, C_TRI:C_TRI + P] = i[:, None] < i[None, :]
    c[:, C_ONE:C_ONE + P] = 1.0
    col, key = (GW - 1 - i % GW)[:, None], np.arange(GW)[None, :]
    first = np.clip(col - 8, 0, GW - 16)
    c[:, C_NAM:C_NAM + GW] = np.where((key >= first) & (key < first + 16), 0.0, NEG)
    t = np.arange(S)
    n = ROPE // 4
    inv = np.float32(10000.0) ** (-np.arange(n, dtype=np.float32) / np.float32(n))
    ang = np.concatenate([(t // GW).astype(np.float32)[:, None] * inv, (t % GW).astype(np.float32)[:, None] * inv], 1)
    for at, f in ((C_COS, np.cos), (C_SIN, np.sin)):
        c[:, at:at + 32] = f(ang.astype(np.float32)).reshape(NT, P, 16).transpose(1, 0, 2).reshape(P, 32)
    e = np.arange(NE)
    c[:, C_LT:C_LT + 64] = (e[None, :] < e[:, None]).reshape(1, 64)
    c[:, C_EID:C_EID + 8] = e
    dist = 255 - np.arange(S)
    nf = np.maximum(dist, 1).astype(np.float32)
    large = 16 + (np.log(nf / np.float32(16)) / np.float32(math.log(8.0)) * np.float32(16)).astype(np.int32)
    bucket = np.where(dist < 16, dist, np.minimum(large, NBK - 1))
    c[bucket, C_HOT + np.arange(S)] = 1.0
    c[:, C_SEL + 31] = 1.0
    return c


STAGES = [0, 1, 2, 3, 4, "m", 5]
TILES_OF = {s: 3 if s == "m" else KT for s in STAGES}
TURN0 = {s: sum(TILES_OF[r] for r in STAGES[:n]) for n, s in enumerate(STAGES)}
XN0 = {s: NT * n for n, s in enumerate(STAGES)}
RMS0 = {s: n for n, s in enumerate([0, "r0", 1, "r1", 2, 3, 4, 5, "f"])}
HEADS0 = {1: 0, 2: H1, 3: H1 + H2}
TURN_BANK = {s: 4 if s in (1, 3) else 0 for s in STAGES}


class Chunk:

    def __init__(self, base, reg=None, per=0):
        self.moe = base >= W_MOE
        first, ring, halves = (W_MOE, MOE_RAW, MOE_SPLIT) if self.moe else (0, NRAW, NSPLIT)
        assert per % ring == 0 and per % halves == 0
        self.n = base if reg is None else base + reg * per
        at, part = (base - first) % ring, (base - first) % halves
        self.slot = (first + at) % NRAW if at < NRAW else at
        self.half = (first + part) % NSPLIT if part < NSPLIT else part
        self.first_use = reg is None and base - first < ring
        self.first_half = reg is None and base - first < halves
        self.ring, self.halves = ring, halves
        loads = (base - first) // ring + 1
        self.loads = loads if reg is None else loads + reg * (per // ring)


def reversed_in(ap, n):
    return ap.rearrange("p (b n) -> p b n", n=n)[:, :, ::-1]


class Chain:

    def __init__(self, eng, sem):
        self.eng, self.sem, self.n, self.loop = eng, sem, 0, None

    def count(self):
        return self.n if self.loop is None else self.n + self.loop[0] * self.loop[1]

    def mark(self, ins):
        ins.then_inc(self.sem, 1)
        self.n += 1
        return self.count()

    def after(self, mark):
        self.eng.wait_ge(self.sem, mark)

    def link(self, ins):
        self.after(self.mark(ins))

    def enter(self, reg, per):
        self.loop = (reg, per, self.n)

    def leave(self, times):
        reg, per, start = self.loop
        assert self.n - start == per, (self.n - start, per)
        self.loop = None
        self.n = start + per * times


def blocks(nc, a, out):
    ctx = ExitStack()
    with ctx:
        base = [(nc.sbuf_base + 63) // 64 * 64]

        def at(name, cols, dt=F32, offset=None, parts=P):
            if offset is None:
                offset = base[0]
                base[0] += (cols * 4 + 31) // 32 * 32
                assert base[0] <= nc.sbuf_usable_end, (name, base[0], nc.sbuf_usable_end)
            t = nc.alloc_sbuf_tensor_at(name, [parts, cols], dt, offset=offset)
            return t.ap() if hasattr(t, "ap") and callable(t.ap) else t[:, :]

        def room(cols):
            o = base[0]
            base[0] += cols * 4
            assert base[0] <= nc.sbuf_usable_end, base[0]
            return o

        sems = {}

        def sem(name):
            if name not in sems:
                sems[name] = ctx.enter_context(nc.semaphore(name))
            return sems[name]

        raw = at("raw", NRAW * CHUNK).rearrange("p (s n) -> p s n", s=NRAW)
        whi2 = at("whi", NSPLIT * CHUNK, F32R).rearrange("p (s n) -> p s n", s=NSPLIT)
        wlo2 = at("wlo", NSPLIT * CHUNK, F32R).rearrange("p (s n) -> p s n", s=NSPLIT)
        ada_at = room(NADA * CHUNK)
        ada = at("ada", NADA * CHUNK, offset=ada_at).rearrange("p (s n) -> p s n", s=NADA)
        x = at("x", NT * D).rearrange("p (t n) -> p t n", t=NT)
        xn_at = room(NT * D)
        xn = at("xn", NT * D, offset=xn_at).rearrange("p (t n) -> p t n", t=NT)
        ahi_flat, alo_flat = at("ahi", KT * S, F32R), at("alo", KT * S, F32R)
        ahi, alo = (f.rearrange("p (k s) -> p k s", k=KT) for f in (ahi_flat, alo_flat))
        raws = [raw[:, s] for s in range(NRAW)] + [ada[:, s] for s in range(NADA)]
        whi = [whi2[:, s] for s in range(NSPLIT)] + [ahi_flat]
        wlo = [wlo2[:, s] for s in range(NSPLIT)] + [alo_flat]
        gates = at("gates", 2 * D).rearrange("p (g n) -> p g n", g=2)
        gvec = at("gvec", D)
        gate_row = [[gates[:, 0], gates[:, 1]], [gates[:, 0], gvec]]
        final_scale = gates[:, 1]
        vecs = at("vecs", VEC_COLS)
        cst = at("cst", C_ALL)
        small = at("small", 256)
        mod = at("mod", 4 * KT)
        hm = at("hm", NHM * S).rearrange("p (r s) -> p r s", r=NHM)
        odd = at("odd", S)
        union = base[0]
        here = [union]

        def u(name, cols, dt=F32, parts=P):
            o = here[0]
            here[0] += (cols * 4 + 31) // 32 * 32
            assert here[0] <= nc.sbuf_usable_end, (name, here[0], nc.sbuf_usable_end)
            return at(name, cols, dt, offset=o, parts=parts)

        ghi = u("ghi", FT * S, F32R).rearrange("p (k s) -> p k s", k=FT)
        glo = u("glo", FT * S, F32R).rearrange("p (k s) -> p k s", k=FT)
        acc = u("acc", 6 * D)
        cv = at("cv", 2 * 2 * 2 * S, offset=xn_at)[:, 0:4 * S].rearrange("p (h f s) -> p h f s", h=2, f=2)
        pr = at("pr", 4 * S, offset=xn_at + 4 * S * 4)[:, 0:2 * S].rearrange("p (f s) -> p f s", f=2)

        def core_buffers(tag):
            sbf = u(f"scores{tag}", 2 * 512).rearrange("p (r n) -> p r n", r=2)
            pbf = u(f"probs{tag}", 3 * 512).rearrange("p (r n) -> p r n", r=3)
            ptb = u(f"probsT{tag}", 2 * 512).rearrange("p (r n) -> p r n", r=2)
            return sbf, pbf, ptb

        here[0] = union
        core1 = core_buffers("1")
        qT1 = u("qT1", LT * S).rearrange("p (k s) -> p k s", k=LT)
        kT1 = u("kT1", LT * S).rearrange("p (k s) -> p k s", k=LT)
        v1 = u("v1", NT * DA).rearrange("p (t n) -> p t n", t=NT)
        bias1 = u("bias1", H1 * 384).rearrange("p (h n) -> p h n", h=H1)
        lru = [u(f"lru{n}", LT * S).rearrange("p (k s) -> p k s", k=LT) for n in range(6)]
        here[0] = union
        rows = u("rows", 4 * P).rearrange("p (n c) -> p n c", n=4)
        here[0] = base[0]
        wr = at("wr", LT * P, offset=ada_at).rearrange("p (k c) -> p k c", k=LT)
        wi = at("wi", LT * P, offset=ada_at + LT * P * 4).rearrange("p (k c) -> p k c", k=LT)
        tbl = at("tbl", 512, offset=ada_at + 2 * LT * P * 4, parts=8)
        relb = at("relb", H1, offset=ada_at + 2 * LT * P * 4 + 2048, parts=NBK)

        here[0] = union
        core2 = core_buffers("2")
        qT2 = u("qT2", KT * S).rearrange("p (k s) -> p k s", k=KT)
        kT2 = u("kT2", KT * S).rearrange("p (k s) -> p k s", k=KT)
        v2 = u("v2", NT * D).rearrange("p (t n) -> p t n", t=NT)
        HB = H2 // 2
        bias2 = [u("bias2a", HB * 512), at("bias2b", HB * 512, offset=ada_at)]
        bias2 = [b.rearrange("p (h t n) -> p h t n", h=HB, t=NT) for b in bias2]

        here[0] = union
        core3 = core_buffers("3")
        NH3 = H2 + 1
        qtok = u("qtok", NT * NH3 * QKW).rearrange("p (t h n) -> p t h n", t=NT, h=NH3)
        ktok = u("ktok", NT * H2 * QKW).rearrange("p (t h n) -> p t h n", t=NT, h=H2)
        v3 = u("v3", NT * D).rearrange("p (t n) -> p t n", t=NT)
        qkT = u("qkT", 2 * 512).rearrange("p (r n) -> p r n", r=2)
        rt = at("rt", 4 * NT * NH3 * 16, offset=ada_at).rearrange("p (r t h i) -> p r t h i", r=4, t=NT, h=NH3)

        here[0] = union
        hchi = u("hchi", KT * P, F32R).rearrange("p (k s) -> p k s", k=KT)
        hclo = u("hclo", KT * P, F32R).rearrange("p (k s) -> p k s", k=KT)
        gchi = u("gchi", ET * P, F32R).rearrange("p (k s) -> p k s", k=ET)
        gclo = u("gclo", ET * P, F32R).rearrange("p (k s) -> p k s", k=ET)
        xhi = u("xhi", NT * D, F32R).rearrange("p (t n) -> p t n", t=NT)
        xlo = at("xlo", NT * D, F32R, offset=xn_at).rearrange("p (t n) -> p t n", t=NT)
        hc = u("hc", KT * P).rearrange("p (k s) -> p k s", k=KT)
        ge = u("ge", ED)
        sg = u("sg", 2 * EC).rearrange("p (r n) -> p r n", r=2)
        hrow = u("hrow", D)
        dchi, dclo = u("dchi", D, F32R), u("dclo", D, F32R)
        y = u("y", NT * D).rearrange("p (t n) -> p t n", t=NT)
        pick = u("pick", NT * P, F32R).rearrange("p (t s) -> p t s", t=NT)
        pickT = u("pickT", S, F32R)
        rw = u("rw", 32 * NE).rearrange("p (r n) -> p r n", r=32)
        rtr = u("rtr", KT * NE)
        rthi = u("rthi", KT * NE, F32R).rearrange("p (k e) -> p k e", k=KT)
        rtlo = u("rtlo", KT * NE, F32R).rearrange("p (k e) -> p k e", k=KT)
        cmp_ = u("cmp", 4 * NT * NE * NE)
        lgT = u("lgT", S, parts=NE)
        posn = u("posn", NT * 12).rearrange("p (t n) -> p t n", t=NT)
        wcol = u("wcol", NT * 12).rearrange("p (t n) -> p t n", t=NT)
        eidf = u("eidf", 16)
        eidi = u("eidi", 16, I32)

        core = {1: core1, 2: core2, 3: core3}

        ps = ctx.enter_context(nc.psum_tensor("ps", [P, 8, 512], F32))

        ident = cst[:, C_ID:C_ID + P]
        ones = cst[:, C_ONE:C_ONE + P]
        epsc = small[:, 0:1]
        ss = small[:, 2:4]
        std = small[:, 4:6]
        rstd = small[:, 6:8]
        mx = small[:, 8:8 + 32].rearrange("p (h t) -> p h t", t=NT)
        sume = small[:, 40:72].rearrange("p (h t) -> p h t", t=NT)
        rsum = small[:, 72:104].rearrange("p (h t) -> p h t", t=NT)
        nmx = small[:, 104:136].rearrange("p (h t) -> p h t", t=NT)
        sp8 = small[:, 136:140]
        lamw = small[:, 140:164].rearrange("p (r k) -> p r k", k=LT)
        ssm = small[:, 164:168]
        stm = small[:, 168:172]
        rsm = small[:, 172:176]

        def vec(name):
            _, _, n, col = VEC[name]
            return vecs[:, col:col + n]

        scratch = nc.dram_tensor("rel_table", [H1, 512], F32).ap()

        def view(slot_ap, k, n):
            return slot_ap[:, 0:k * n].rearrange("p (k n) -> p k n", k=k)

        def kn(ap, k0, k, n0, n):
            return ap[k0 * P:(k0 + k) * P, n0:n0 + n].rearrange("(k p) n -> p k n", p=P)

        def chunk_shape(c):
            if c < W_OUT or W_UP <= c < W_DOWN or W_QKV <= c < W_NAO or W_GU <= c < W_DN2:
                return KT, 256
            if W_MDN <= c < W_UQ:
                return KT, MLA_DN // 2
            if W_UQ <= c < W_UKV:
                return 2, 768
            if c == W_UKV:
                return 1, 2048
            if c < W_MOE:
                return 2, D
            c = (c - W_MOE) % PASS_CHUNKS
            return (4, EC) if c < 16 else (2, D) if c < 22 else (1, D)

        IN_COLS = [3 * DA, 3 * DA + 256, 3 * DA + DL, 3 * DA + DL + 256, 0, 256, DA, DA + 256, 2 * DA, 2 * DA + 256]

        def dram_chunk(c):
            k, n = chunk_shape(c)
            if c < W_OUT:
                return kn(a["w_in"][0], 0, k, IN_COLS[c], n)
            if c < W_UP:
                return kn(a["w_out"][0], 2 * (c - W_OUT), k, 0, n)
            if c < W_DOWN:
                g = c - W_UP
                return kn(a["w_up"][0], 0, k, (1 - g % 2) * FF + g // 2 * 256, n)
            if c < W_QKV:
                return kn(a["w_down"][0], 2 * (c - W_DOWN), k, 0, n)
            if c < W_NAO:
                return kn(a["na_w_qkv_2"][0], 0, k, 256 * (c - W_QKV), n)
            if c < W_GU:
                return kn(a["na_w_o_2"][0], 2 * (c - W_NAO), k, 0, n)
            if c < W_DN2:
                g = c - W_GU
                return kn(a["ffn_w_gu_2"][0], 0, k, g % 2 * FF + g // 2 * 256, n)
            if c < W_MDN:
                return kn(a["ffn_w_down_2"][0], 2 * (c - W_DN2), k, 0, n)
            if c < W_UQ:
                return kn(a["mla_w_down_2"][0], 0, k, (c - W_MDN) * n, n)
            if c < W_UKV:
                return kn(a["mla_w_uq_2"][0], 0, k, (c - W_UQ) * n, n)
            if c < W_MLO:
                return kn(a["mla_w_ukv_2"][0], 0, k, 0, n)
            return kn(a["mla_w_o_2"][0], 2 * (c - W_MLO), k, 0, n)

        raw_in = [sem(f"raw_in{s}") for s in range(NRAW)]
        moe_in = [sem(f"moe_in{s}") for s in range(MOE_RAW)]
        ada_in = [sem(f"ada_in{s}") for s in range(NADA)]
        hi_done, lo_done, mm_done = sem("hi_done"), sem("lo_done"), sem("mm_done")
        ada_used = sem("ada_used")

        def attention_plan(n):
            causal = n == 1
            seg = [(0, 0, P), (1, P, S)] if causal else [(0, 0, S), (1, S, S)]
            return (H1 if causal else H2), causal, seg

        def number_of_passes(eng):
            return eng.value_load(eidi[0:1, N_PASS:N_PASS + 1], min_val=NE, max_val=MAX_PASSES)

        block = ctx.enter_context(nc.Block())

        @block.sync
        def _(sp):
            def load(c, src=None, reg=None, per=0):
                ck = Chunk(c, reg, per)
                if ck.first_use and ck.slot >= NRAW:
                    sp.wait_ge(sem("roped"), 1)
                elif c >= NRAW:
                    sp.wait_ge(lo_done, ck.n - ((NRAW if ck.first_use else ck.ring) - 1))
                    if reg is not None:
                        sp.sem_inc(sem("sync_step"), 1)
                k, n = chunk_shape(c)
                sp.dma_start(view(raws[ck.slot], k, n), dram_chunk(c) if src is None else src)\
                    .then_inc((moe_in if ck.moe else raw_in)[ck.slot], 16)

            def load_ada(layer, j, col=None, reg=None, per=0):
                g = layer * ADA_CHUNKS + j
                n = g if reg is None else g + reg * per
                sp.wait_ge(ada_used, n + 1)
                col = 256 * j if col is None else col
                w = a["w_ada_2"][layer].rearrange("(k p) n -> p k n", p=P)
                sp.dma_start(view(ada[:, g % NADA], KT, 256), w[:, :, bass.ds(col, 256)])\
                    .then_inc(ada_in[g % NADA], 16)

            def load_ffn(gu, w, halves, layer):
                w = w.rearrange("(k p) n -> p k n", p=P)
                sp.wait_ge(sem(f"ada_free{layer}"), 1)
                load_ada(layer, 0)
                for c in range(NRAW):
                    load_ada(layer, 1 + c)
                    load(gu + c)
                with sp.Fori(0, GU_STEPS // 2 - 1) as i:
                    for s in range(2):
                        for part in range(2):
                            src = w[:, :, bass.ds(halves[part] + (s + 2) * 256 + i * 512, 256)]
                            load(gu + NRAW + 2 * s + part, src, i, 4)
                        j = ADA_EARLY + s
                        load_ada(layer, j, 256 * j + i * 512, i, 2)
                j = ADA_EARLY + GU_STEPS - 3
                for c in range(2 * GU_STEPS - 2, 2 * GU_STEPS + 2, 2):
                    load(gu + c)
                    load(gu + c + 1)
                    load_ada(layer, j)
                    j += 1
                c = 2 * GU_STEPS + 2
                while j < ADA_CHUNKS:
                    load(gu + c)
                    load_ada(layer, j)
                    c, j = c + 1, j + 1
                return gu + c

            sp.dma_start(x, a["x"][0].rearrange("(t p) n -> p t n", p=P)).then_inc(sem("x_in"), 16)
            sp.dma_start(cst, a["consts"]).then_inc(sem("cst_in"), 16)
            sp.wait_ge(sem("rows_in"), 16 * ROW_DMAS)
            for c in range(W_UP):
                load(c)
            at_ = load_ffn(W_UP, a["w_up"][0], [FF, 0], 0)

            def load_bias2(hb, r):
                for i in range(GR):
                    rp = a["na_rpb_2"]
                    first = (hb * HB * RPB_H + i + 7 - r) * RPB_W + 15 - (GW - 1)
                    src = bass.AP(rp.tensor, rp.offset + first, [[1, GW], [RPB_H * RPB_W, HB], [1, GW]])
                    dst = bias2[hb][GW * (r % 2):GW * (r % 2) + GW, :, r // 2, i * GW:(i + 1) * GW]
                    sp.dma_start(dst, src).then_inc(sem(f"bias2_in{hb}"), 16)

            for c in range(at_, W_GU):
                load(c)
                n = c - (W_QKV + NRAW)
                if n == 0:
                    sp.wait_ge(mm_done, W_QKV)
                    sp.wait_ge(sem("gate_sum0"), 2)
                if 0 <= n < 2 * GR:
                    load_bias2(n // GR, n % GR)
            at_ = load_ffn(W_GU, a["ffn_w_gu_2"][0], [0, FF], 1)
            for c in range(at_, W_MOE):
                load(c)

            gu = a["moe_w_gu_2"][0].rearrange("e (k p) n -> p e k n", p=P)
            dn = a["moe_w_down_2"][0].rearrange("e (k p) n -> p e k n", p=P)

            def expert_chunk(c, e):
                if c < 16:
                    j, part, half = c // 4, c % 4 // 2, c % 2
                    return gu[:, bass.ds(e, 1), 4 * half:4 * half + 4, part * ED + j * EC:part * ED + (j + 1) * EC]\
                        .rearrange("p e k n -> p (e k) n")
                k0 = 2 * (c - 16) if c < 22 else 12 + c - 22
                return dn[:, bass.ds(e, 1), k0:k0 + chunk_shape(W_MOE + c)[0], :].rearrange("p e k n -> p (e k) n")

            for c in range(MOE_SPLIT):
                load(W_MOE + c, expert_chunk(c, 0))
            sp.wait_ge(sem("experts_known"), 1)
            passes = number_of_passes(sp)
            with sp.Fori(0, passes) as p:
                e = sp.value_load(eidi[0:1, bass.ds(p, 1)], min_val=0, max_val=NE - 1)
                for c in range(MOE_SPLIT, PASS_CHUNKS):
                    load(W_MOE + c, expert_chunk(c, e), p, PASS_CHUNKS)
                e2 = sp.value_load(eidi[0:1, bass.ds(p + 1, 1)], min_val=0, max_val=NE - 1)
                for c in range(MOE_SPLIT):
                    load(W_MOE + PASS_CHUNKS + c, expert_chunk(c, e2), p, PASS_CHUNKS)
            for c in range(MOE_SPLIT):
                ck = Chunk(W_MOE + c, passes, PASS_CHUNKS)
                sp.wait_ge(moe_in[ck.slot], 16 * ck.loads)
                sp.sem_inc(sem("sync_step"), 1)
            sp.wait_ge(sem("result"), NT)
            sp.dma_start(out[0].rearrange("(t p) n -> p t n", p=P), xn).then_inc(sem("stored"), 16)
            sp.wait_ge(sem("stored"), 16)

        @block.tensor
        def _(pe):
            def columns_form(ck, f, psum_ap, k_tiles, width, bhi, blo, turn0=None):
                h, l = (view(w[ck.half], k_tiles, width) for w in (whi, wlo))
                cols = slice(f * P, f * P + P)
                for k in range(k_tiles):
                    if turn0 is not None:
                        pe.wait_ge(sem("aT_ready"), turn0 + k + 1)
                    pe.matmul(psum_ap, h[:, k, cols], bhi[:, k], start=(k == 0), stop=False)
                    pe.matmul(psum_ap, h[:, k, cols], blo[:, k], start=False, stop=False)
                    m = pe.matmul(psum_ap, l[:, k, cols], bhi[:, k], start=False, stop=(k == k_tiles - 1))
                return m

            def rows_form(ck, k_tiles, width, k0, k_all, bhi, blo, toks, psums, turn0=None, tile_done=None):
                h, l = (view(w[ck.half], k_tiles, width) for w in (whi, wlo))
                for t in toks:
                    tok = slice(t * P, t * P + P)
                    mine = [(n0, n, o) for tt, n0, n, o in psums if tt == t]
                    for k in range(k_tiles):
                        if turn0 is not None and t == 0:
                            pe.wait_ge(sem("aT_ready"), turn0 + k + 1)
                        first, last = k0 + k == 0, k0 + k == k_all - 1
                        for n0, n, o in mine:
                            pe.matmul(o, bhi[:, k0 + k, tok], h[:, k, n0:n0 + n], start=first, stop=False)
                        for n0, n, o in mine:
                            pe.matmul(o, bhi[:, k0 + k, tok], l[:, k, n0:n0 + n], start=False, stop=False)
                        for n0, n, o in mine:
                            m = pe.matmul(o, blo[:, k0 + k, tok], h[:, k, n0:n0 + n], start=False, stop=last)
                    if tile_done is not None and t == 0:
                        m.then_inc(tile_done, 1)
                return m

            def begin(c, reg=None, per=0):
                ck = Chunk(c, reg, per)
                pe.wait_ge(lo_done, ck.n + 1)
                return ck

            def transposes(s, tiles=KT):
                for t in range(NT):
                    pe.wait_ge(sem("xn_ready"), XN0[s] + t + 1)
                    for k in range(tiles):
                        m = pe.transpose(ps[:, TURN_BANK[s] + k // 2, k % 2 * S + t * P:k % 2 * S + t * P + P],
                                         xn[:, t, k * P:(k + 1) * P], ident)
                        if t == NT - 1:
                            m.then_inc(sem("turned"), 1)

            def output_projection(first, k_all, bhi, blo, s, gated=None, after=None):
                outs = [(t, n * 512, 512, ps[:, 4 + 2 * t + n, :]) for t in range(NT) for n in range(2)]
                for c in range(k_all // 2):
                    if gated:
                        pe.wait_ge(gated, c + 1)
                    ck = begin(first + c)
                    m = rows_form(ck, 2, D, 2 * c, k_all, bhi, blo, range(NT), outs,
                                  tile_done=sem("tile_done") if c == k_all // 2 - 1 else None)
                    m.then_inc(mm_done, 1)
                    if after:
                        after(c)

            def gate_up_step(gu, s, first, reg=None):
                j = s if reg is None else 2 * reg + s
                if reg is None:
                    j = GU_STEPS - 1
                pe.wait_ge(sem(f"gu_free{first}"), j + 1)
                for part in range(2):
                    ck = begin(gu + 2 * s + part, reg, 4) if reg is not None else begin(gu + 2 * j + part)
                    for f in range(2):
                        wait = reg is not None and s == part == f == 0
                        m = columns_form(ck, f, ps[:, 2 * s + part, f * S:(f + 1) * S], KT, 256, ahi, alo,
                                         TURN0[first] if wait else None)
                    m.then_inc(mm_done, 1)

            def gate_up(gu, stage):
                with pe.Fori(0, GU_STEPS // 2) as i:
                    for s in range(2):
                        gate_up_step(gu, s, stage, i)
                gate_up_step(gu, 0, stage)

            def modulation(layer):
                def gate(g, n, bank):
                    col = (2 + 3 * g) * D + n * 512
                    return pe.matmul(ps[:, bank, :], ones, acc[:, col:col + 512], start=True, stop=True)

                def after(c):
                    if c == DN_CHUNKS - 3:
                        pe.wait_ge(ada_used, NADA + ADA_CHUNKS * (layer + 1))
                        pe.wait_ge(sem(f"gu_free{1 + 2 * layer}"), GU_STEPS + 2)
                        tiles = [c for c in range(6 * KT) if c // KT not in (2, 5)]
                        for n, c in enumerate(tiles):
                            m = pe.matmul(ps[0:32, 0, 0:P], cst[:, C_SEL + 31 - n:C_SEL + 63 - n], acc[:, c * P:(c + 1) * P],
                                          start=(n == 0), stop=(n == len(tiles) - 1))
                        m.then_inc(sem(f"mod_sum{layer}"), 1)
                        for n in range(3):
                            m = gate(n // 2, n % 2, 1 + n)
                        m.then_inc(sem(f"gate_sum{layer}"), 1)
                    elif c == DN_CHUNKS - 2:
                        pe.wait_ge(sem(f"mod_rows{layer}"), 1)
                        pe.transpose(ps[:, 0, 0:32], odd[0:32, 0:P], ident[0:32, 0:32]).then_inc(sem(f"mod_turned{layer}"), 1)
                        pe.wait_ge(sem(f"gate_read{layer}"), 1)
                        gate(1, 1, 1).then_inc(sem(f"gate_sum{layer}"), 1)
                return after

            def attention(n, q_ap, k_ap, v_ap, before=None):
                heads, causal, seg = attention_plan(n)
                for i in range(-1 if before else 0, heads + 3):
                    if before and i + 1 < heads:
                        before(i + 1)
                    if 0 <= i < heads:
                        if i >= 2:
                            pe.wait_ge(sem("a_exp" if before else "a_sfree"), HEADS0[n] + i - 1)
                        if before:
                            pe.wait_ge(sem("a_qkT"), i + 1)
                        for qt, col, w in seg:
                            m = pe.matmul(ps[:, i % 2, col:col + w], q_ap(i)[:, qt * P:(qt + 1) * P],
                                          k_ap(i)[:, 0:w], start=True, stop=True)
                        m.then_inc(sem("a_score"), 1)
                    h = i - 2
                    if 0 <= h < heads:
                        pe.wait_ge(sem("a_norm"), HEADS0[n] + h + 1)
                        if h >= 2:
                            pe.wait_ge(sem("a_pT"), HEADS0[n] + h - 1)
                        for qt, col, w in seg:
                            for kt in range(w // P):
                                m = pe.transpose(ps[:, 2 + h % 2, kt * S + qt * P - (P if causal and kt else 0):][:, 0:P],
                                                 core[n][1][:, h % 3, col + kt * P:col + kt * P + P], ident)
                        m.then_inc(sem("a_turned"), 1)
                    h = i - 3
                    if 0 <= h < heads:
                        pe.wait_ge(sem("a_pT"), HEADS0[n] + h + 1)
                        if h % 2 == 0 and h >= 4:
                            pe.wait_ge(sem("a_out"), HEADS0[n] // 2 + h // 2 - 1)
                        half = slice(HD * (h % 2), HD * (h % 2) + HD)
                        o = ps[half, 4 + h // 2 % 2, :]
                        pT = core[n][2][:, h % 2]
                        pe.matmul(o[:, 0:S], v_ap(h, 0), pT[:, 0:S], start=True, stop=False)
                        if causal:
                            m = pe.matmul(o[:, P:S], v_ap(h, 1), pT[:, S:S + P], start=False, stop=True)
                        else:
                            m = pe.matmul(o[:, 0:S], v_ap(h, 1), pT[:, S:2 * S], start=False, stop=True)
                        m.then_inc(sem("a_pv"), 1)

            pe.wait_ge(sem("cst_in"), 16)
            pe.wait_ge(sem("rows_in"), 16 * ROW_DMAS)
            for n, (col, count) in enumerate(VEC_TILES):
                m = pe.transpose(ps[:, 5, n * P:n * P + count], rows[0:count, n, :], ident[0:count, 0:count])
            m.then_inc(sem("vec_turned"), 1)
            pe.wait_ge(sem("relb_in"), 16)
            pe.matmul(ps[0:H1, 7, 0:S], relb, cst[0:NBK, C_HOT:C_HOT + S], start=True, stop=True)\
                .then_inc(sem("rel_mm"), 1)

            transposes(0)
            pe.wait_ge(sem("vecs_ready"), 1)

            def projection(first, chunks, v_from, tag, stage, after=None):
                for c in range(chunks):
                    if c >= 4:
                        pe.wait_ge(sem(f"{tag}_free"), c - 3)
                    ck = begin(first + c)
                    b = 4 + c % 4
                    if c < v_from:
                        for f in range(2):
                            m = columns_form(ck, f, ps[:, b, f * S:(f + 1) * S], KT, 256, ahi, alo,
                                             TURN0[stage] if c == f == 0 else None)
                    else:
                        m = rows_form(ck, KT, 256, 0, KT, ahi, alo, range(NT),
                                      [(t, 0, 256, ps[:, b, t * S:(t + 1) * S]) for t in range(NT)])
                    m.then_inc(mm_done, 1)
                    if after:
                        after(c)

            def lru_gates(c):
                if c == 2:
                    pe.wait_ge(sem("rel_read"), 1)
                if c == 4:
                    pe.wait_ge(sem("wri_in"), 1)
                    pe.wait_ge(sem("xc_ready"), LT)
                    for g, w in enumerate((wr, wi)):
                        for k in range(LT):
                            m = pe.matmul(ps[:, 2 * g + k // 2, k % 2 * S:(k % 2 + 1) * S], w[:, k, :], lru[0][:, k, :],
                                          start=True, stop=True)
                        m.then_inc(sem("ri_mm"), 1)

            projection(W_IN, 10, 8, "in", 0, lru_gates)
            pe.wait_ge(sem("qkv_ready"), 1)
            pe.wait_ge(sem("ri_read"), 2)

            def head(ap):
                return lambda h: ap[HD * (h % 2):HD * (h % 2) + HD, h // 2, :]

            attention(1, head(qT1), head(kT1), lambda h, kt: v1[:, kt, HD * h:HD * h + HD])
            pe.wait_ge(sem("mix_ready"), 1)
            output_projection(W_OUT, KT, ahi, alo, 0)
            transposes(1)
            gate_up(W_UP, 1)
            output_projection(W_DOWN, FT, ghi, glo, 1, sem("gT_ready1"), modulation(0))
            pe.wait_ge(sem("gate_read0"), 2)
            transposes(2)
            projection(W_QKV, 12, 8, "qkv2", 2)
            pe.wait_ge(sem("qkv2_free"), 12)
            attention(2, head(qT2), head(kT2), lambda h, kt: v2[:, kt, HD * h:HD * h + HD])
            pe.wait_ge(sem("mix_ready2"), 1)
            output_projection(W_NAO, KT, ahi, alo, 2)
            transposes(3)
            gate_up(W_GU, 3)
            output_projection(W_DN2, FT, ghi, glo, 3, sem("gT_ready3"), modulation(1))
            pe.wait_ge(sem("gate_read1"), 2)
            transposes(4)
            for c in range(2):
                ck = begin(W_MDN + c)
                n = MLA_DN // 2
                rows_form(ck, KT, n, 0, KT, ahi, alo, range(NT),
                          [(t, 0, n, ps[:, 4 + t + 2 * c, 0:n]) for t in range(NT)],
                          TURN0[4] if c == 0 else None).then_inc(mm_done, 1)
            transposes("m", 3)
            pe.wait_ge(sem("aT_ready"), TURN0["m"] + 3)
            for c in range(2):
                ck = begin(W_UQ + c)
                rows_form(ck, 2, 768, 0, 2, ahi, alo, range(NT),
                          [(t, n * 384, 384, ps[:, 4 * c + 2 * t + n, 0:384]) for t in range(NT) for n in range(2)])\
                    .then_inc(mm_done, 1)
            ck = begin(W_UKV)
            for t in range(NT):
                pe.wait_ge(sem("uq_read"), 2)
                m = rows_form(ck, 1, 2048, 0, 1, ahi[:, 2:3], alo[:, 2:3], [t],
                              [(t, n * 512, 512, ps[:, 4 * t + n, :]) for n in range(4)])
            m.then_inc(mm_done, 1)
            pe.wait_ge(sem("ktok_ready"), 1)
            pe.wait_ge(sem("roped"), 1)

            def mla_columns(h):
                if h >= 2:
                    pe.wait_ge(sem("a_qkT"), h - 1)
                for w, src in enumerate((qtok, ktok)):
                    for t in range(NT):
                        m = pe.transpose(ps[0:QKW, 6 + h % 2, w * S + t * P:w * S + (t + 1) * P],
                                         src[:, t, h, :], ident)
                m.then_inc(sem("a_qkmm"), 1)

            attention(3, lambda h: qkT[0:QKW, h % 2, 0:S], lambda h: qkT[0:QKW, h % 2, S:2 * S],
                      lambda h, kt: v3[:, kt, HD * h:HD * h + HD], mla_columns)
            pe.wait_ge(sem("mix_ready3"), 1)
            output_projection(W_MLO, KT, ahi, alo, 4)
            transposes(5)
            pe.wait_ge(sem("router_ready"), 1)
            for k in range(KT):
                pe.wait_ge(sem("aT_ready"), TURN0[5] + k + 1)
                pe.matmul(ps[0:NE, 6, 0:S], rthi[:, k], ahi[:, k], start=(k == 0), stop=False)
                pe.matmul(ps[0:NE, 6, 0:S], rtlo[:, k], ahi[:, k], start=False, stop=False)
                m = pe.matmul(ps[0:NE, 6, 0:S], rthi[:, k], alo[:, k], start=False, stop=(k == KT - 1))
            m.then_inc(sem("logits"), 1)
            pe.wait_ge(sem("logits_read"), 1)
            for t in range(NT):
                m = pe.transpose(ps[:, 4, t * NE:(t + 1) * NE], lgT[:, t * P:(t + 1) * P], ident[0:NE, 0:NE])
            m.then_inc(sem("logits"), 1)
            pe.wait_ge(sem("chosen"), 1)
            sel = [rw[:, 8 + t, :] for t in range(NT)]
            tri = cst[:, C_TRI:C_TRI + P]
            pe.matmul(ps[:, 5, 0:NE], tri, sel[0], start=True, stop=True)
            pe.matmul(ps[:, 5, NE:2 * NE], tri, sel[1], start=True, stop=False)
            pe.matmul(ps[:, 5, NE:2 * NE], ones, sel[0], start=False, stop=True)
            pe.matmul(ps[:, 5, 2 * NE:3 * NE], ones, sel[0], start=True, stop=False)
            pe.matmul(ps[:, 5, 2 * NE:3 * NE], ones, sel[1], start=False, stop=True).then_inc(sem("places"), 1)

            def gather(count):
                pe.wait_ge(sem("pick_ready"), count)
                for t in range(NT):
                    for part in (xhi, xlo):
                        for n in range(2):
                            m = pe.matmul(ps[:, 6 + n, :], pick[:, t, :], part[:, t, n * 512:(n + 1) * 512],
                                          start=(t == 0 and part is xhi), stop=(t == NT - 1 and part is xlo))
                m.then_inc(sem("gathered"), 1)

            def turn_gathered(count):
                pe.wait_ge(sem("rows_copied"), count)
                for k in range(KT):
                    m = pe.transpose(ps[:, 6 + k // 4, k % 4 * P:(k % 4 + 1) * P], hrow[:, k * P:(k + 1) * P], ident)
                m.then_inc(sem("gathered_turned"), 1)

            def combine(t):
                for n in range(2):
                    for d in (dchi, dclo):
                        m = pe.matmul(ps[:, 6 + n, :], pickT[:, t * P:(t + 1) * P], d[:, n * 512:(n + 1) * 512],
                                      start=(d is dchi), stop=(d is dclo))
                m.then_inc(sem("combined"), 1)

            def turn_gated(q):
                for k in range(4 * q, min(4 * q + 4, ET)):
                    m = pe.transpose(ps[:, q, (k - 4 * q) * P:(k - 4 * q + 1) * P], ge[:, k * P:(k + 1) * P], ident)
                m.then_inc(sem("ge_turned"), 1)

            pe.wait_ge(sem("x_lo"), 1)
            gather(1)
            turn_gathered(1)
            pe.wait_ge(sem("experts_known"), 1)
            passes = number_of_passes(pe)
            with pe.Fori(0, passes) as p:
                pe.wait_ge(sem("hc_ready"), 1 + p)
                for j in range(4):
                    if j >= 2:
                        pe.wait_ge(sem("ge_ready"), (j + 3) + 4 * p)
                    elif j == 0:
                        pe.wait_ge(sem("gc_ready"), 4 + 4 * p)
                    for part in range(2):
                        for half in range(2):
                            ck = begin(W_MOE + 4 * j + 2 * part + half, p, PASS_CHUNKS)
                            h, l = (view(w[ck.half], 4, EC) for w in (whi, wlo))
                            o = ps[:, (2 * j + part) % 4, 0:EC]
                            for k in range(4):
                                kk = 4 * half + k
                                pe.matmul(o, hchi[:, kk], h[:, k], start=(kk == 0), stop=False)
                                pe.matmul(o, hchi[:, kk], l[:, k], start=False, stop=False)
                                m = pe.matmul(o, hclo[:, kk], h[:, k], start=False, stop=(kk == KT - 1))
                            m.then_inc(mm_done, 1)
                        if (j, part) == (3, 0):
                            pe.wait_ge(sem("ge_ready"), 7 + 4 * p)
                            turn_gated(0)
                            turn_gated(1)
                    if j == 0:
                        pe.wait_ge(sem("dc_ready"), 1 + p)
                        combine(0)
                    if j == 1:
                        pe.wait_ge(sem("y_added"), 1 + 2 * p)
                        combine(1)
                    if j == 2:
                        pe.wait_ge(sem("y_added"), 2 + 2 * p)
                        for t in range(NT):
                            m = pe.transpose(ps[:, 6, t * P:(t + 1) * P], pick[:, t, :].bitcast(F32), ident)
                        m.then_inc(sem("pick_turned"), 1)
                pe.wait_ge(sem("pickT_ready"), 2 + p)
                gather(2 + p)
                k0 = 0
                for c in range(16, PASS_CHUNKS):
                    kc = chunk_shape(W_MOE + c)[0]
                    pe.wait_ge(sem("gc_ready"), (4 + (k0 + kc - 1) // 4 + 1) + 4 * p)
                    ck = begin(W_MOE + c, p, PASS_CHUNKS)
                    h, l = (view(w[ck.half], kc, D) for w in (whi, wlo))
                    for k in range(kc):
                        for lhs, rhs, stop in ((gchi, h, False), (gchi, l, False), (gclo, h, k0 + k == ET - 1)):
                            for n in range(2):
                                m = pe.matmul(ps[:, 4 + n, :], lhs[:, k0 + k], rhs[:, k, n * 512:(n + 1) * 512],
                                              start=(k0 + k == 0 and rhs is h and lhs is gchi), stop=stop)
                    m.then_inc(mm_done, 1)
                    k0 += kc
                    if c == 16:
                        pe.wait_ge(sem("ge_ready"), 8 + 4 * p)
                        turn_gated(2)
                        turn_gated(3)
                    if c == 17:
                        turn_gathered(2 + p)
            pe.wait_ge(sem("dc_ready"), 1 + passes)
            pe.wait_ge(sem("hc_ready"), 1 + passes)
            combine(0)
            pe.wait_ge(sem("y_added"), 1 + 2 * passes)
            combine(1)

        @block.scalar
        def _(act):
            def split(c, reg=None, per=0):
                ck = Chunk(c, reg, per)
                act.wait_ge((moe_in if ck.moe else raw_in)[ck.slot], 16 * ck.loads)
                if ck.first_half and ck.half >= NSPLIT:
                    act.wait_ge(sem("logits"), 1)
                elif c >= NSPLIT:
                    act.wait_ge(mm_done, ck.n - ((NSPLIT if ck.first_half else ck.halves) - 1))
                k, n = chunk_shape(c)
                act.activation(whi[ck.half][:, 0:k * n], raws[ck.slot][:, 0:k * n], ACT.Copy).then_inc(hi_done, 1)

            def rms(s, src, first_wait, n=D):
                for t in range(NT):
                    first_wait(t)
                    act.activation(xn[:, t, 0:n], src(t), ACT.Square, accum_out=ss[:, t:t + 1])\
                        .then_inc(sem("sum_squares"), 1)
                    act.wait_ge(sem("sum_squares"), NT * RMS0[s] + t + 1)
                    act.activation(std[:, t:t + 1], ss[:, t:t + 1], ACT.Sqrt, scale=1.0 / n, bias=epsc)\
                        .then_inc(sem("std"), 1)

            def norm(s):
                rms(s, lambda t: x[:, t], lambda t: act.wait_ge(sem("x_ready"), NT * (s - 1) + t + 1) if s else act.wait_ge(sem("x_in"), 16))

            def turned(s, tiles=KT):
                for k in range(tiles):
                    act.wait_ge(sem("modulated"), TURN0[s] + k + 1)
                    act.activation(ahi[:, k], hm[:, k % NHM], ACT.Copy).then_inc(sem("aT_hi"), 1)

            def ld(dst, src, s, n=16):
                act.dma_start(dst, src).then_inc(sem(s), n)

            for name, (tile, row, count, _) in VEC.items():
                ld(rows[row:row + count, tile, :], VEC_SRC[name](a), "rows_in")
            ld(relb, a["rel_bias"], "relb_in")
            for w, dram in ((wr, a["w_r"]), (wi, a["w_i"])):
                act.wait_ge(sem("wri_zero"), 1)
                v = dram[0].rearrange("(k two) c d -> two c k d", two=2)
                for two in range(2):
                    ld(w[64 * two:64 * two + 64, :, 64 * two:64 * two + 64], v[two], "wri_dma")
            act.dma_start(gvec, a["g_post_mix"][0:1, :].broadcast_to([P, D])).then_inc(sem("gvec_in"), 16)

            act.wait_ge(sem("eps_set"), 1)
            norm(0)
            split(0)
            turned(0)
            split(1)
            wc, bc = vec("w_conv_lru"), vec("b_conv_lru")
            for c in range(10):
                split(c + 2)
                if c == 1:
                    act.wait_ge(sem("vecs_ready"), 1)
                    act.activation(lamw[:, 0], vec("lam"), ACT.Abs).then_inc(sem("lam_abs"), 1)
                    act.wait_ge(sem("lam_abs"), 1)
                    act.activation(lamw[:, 1], lamw[:, 0], ACT.Exp, scale=-1.0).then_inc(sem("lam_exp"), 1)
                    act.activation(vec("c"), vec("c"), ACT.Silu).then_inc(sem("c_ready"), 1)
                if c == 2:
                    act.wait_ge(sem("tbl_ready"), 1)
                    ld(scratch, tbl, "tbl_out")
                if c == 4:
                    act.wait_ge(sem("tbl_out"), 16)
                    for off, col, w in ((P, 0, P), (0, P, S)):
                        src = bass.AP(scratch.tensor, scratch.offset + off, [[1, P], [512, H1], [1, w]])
                        ld(bias1[:, :, col:col + w], src, "bias1_in")
                if c in (6, 7):
                    g = c - 6
                    name, dst = (("b_r", lru[2]), ("b_i", lru[3]))[g]
                    act.wait_ge(sem("ri_mm"), g + 1)
                    for k in range(LT):
                        m = act.activation(dst[:, k], ps[:, 2 * g + k // 2, k % 2 * S:(k % 2 + 1) * S], ACT.Sigmoid,
                                           bias=vec(name)[:, k:k + 1])
                    m.then_inc(sem("ri_read"), 1)
                if c == 8:
                    act.wait_ge(sem("ri_read"), 2)
                    act.wait_ge(sem("sp_ready"), 1)
                    for k in range(LT):
                        act.activation(lru[4][:, k], lru[2][:, k], ACT.Tanh, scale=sp8[:, k:k + 1]).then_inc(sem("tanh_a"), 1)
                if c == 9:
                    act.wait_ge(sem("tanh_a"), LT)
                    for k in range(LT):
                        act.activation(lru[2][:, k], lru[2][:, k], ACT.Exp, scale=sp8[:, k:k + 1]).then_inc(sem("exp_a"), 1)
                act.wait_ge(mm_done, W_IN + c + 1)
                b = 4 + c % 4
                if c < 2:
                    for f in range(2):
                        k = 2 * c + f
                        act.activation(lru[0][:, k], ps[:, b, f * S:(f + 1) * S], ACT.Identity,
                                       scale=wc[:, 3 * LT + k:3 * LT + k + 1], bias=bc[:, k:k + 1])\
                            .then_inc(sem("tap3"), 1)
                    continue
                dst = lru[1] if c < 4 else qT1 if c < 6 else kT1 if c < 8 else v1
                if c < 8:
                    k = 2 * (c % 2)
                    o = dst[:, k:k + 2, :]
                    i = ps[:, b, :].rearrange("p (f s) -> p f s", f=2)
                else:
                    o = v1[:, :, 256 * (c - 8):256 * (c - 8) + 256]
                    i = ps[:, b, :].rearrange("p (t n) -> p t n", t=NT)
                if 4 <= c < 6:
                    o, i = o.rearrange("p f (b n) -> p (f b) n", n=P), reversed_in(ps[:, b, :], P)
                act.activation(o, i, ACT.Gelu_apprx_tanh if c < 4 else ACT.Copy).then_inc(sem("in_free"), 1)

            def attention(n, scale, side=None):
                heads, causal, seg = attention_plan(n)
                biased = n != 3
                for i in range(-1 if side else 0, heads + 5):
                    if side and 0 <= i + 1 < heads:
                        side(i + 1)
                    if 0 <= i < heads:
                        act.wait_ge(sem("a_max"), HEADS0[n] + i + 1)
                        if i >= 3:
                            act.wait_ge(sem("a_turned"), HEADS0[n] + i - 2)
                        for s, (qt, col, w) in enumerate(seg):
                            src = core[n][0][:, i % 2, col:col + w] if biased else ps[:, i % 2, col:col + w]
                            m = act.activation(core[n][1][:, i % 3, col:col + w], src, ACT.Exp,
                                               scale=1.0 if biased else scale,
                                               bias=(mx if biased else nmx)[:, i, qt:qt + 1],
                                               accum_out=sume[:, i, qt:qt + 1])
                        m.then_inc(sem("a_exp"), 1)
                    h = i - 2
                    if 0 <= h < heads:
                        act.wait_ge(sem("a_turned"), HEADS0[n] + h + 1)
                        if h >= 2:
                            act.wait_ge(sem("a_pv"), HEADS0[n] + h - 1)
                        w = 384 if causal else 512
                        o, src = core[n][2][:, h % 2, 0:w], ps[:, 2 + h % 2, 0:w]
                        if biased:
                            run = P if causal else GW
                            o, src = o.rearrange("p (b n) -> p b n", n=run), reversed_in(src, run)
                        act.activation(o, src, ACT.Copy)\
                            .then_inc(sem("a_pT"), 1)
                    h = i - 4
                    if 0 <= h < heads and h % 2 == 1:
                        j = h // 2
                        act.wait_ge(sem("a_pv"), HEADS0[n] + h + 1)
                        act.activation(ahi[:, j], ps[:, 4 + j % 2, 0:S], ACT.Copy).then_inc(sem("a_ohi"), 1)

            def residual_rms(s, first):
                rms(f"r{s}", lambda t: ps[:, 4 + 2 * t:6 + 2 * t, :].rearrange("p b n -> p (b n)"),
                    lambda t: act.wait_ge(mm_done, first) if t else act.wait_ge(sem("tile_done"), s + 1))

            def gate_biases(layer):
                for g in range(2):
                    src = a["b_ada_2"][layer:layer + 1, (2 + 3 * g) * D:(3 + 3 * g) * D].broadcast_to([P, D])
                    act.dma_start(gate_row[layer][g], src).then_inc(sem("gbias_in"), 16)

            def down(first, chunks):
                for c in range(chunks - 1):
                    split(first + c + 2)

            for k in range(LT):
                act.wait_ge(sem("lru_v"), k + 1)
                act.activation(lru[4][:, k], lru[4][:, k], ACT.Sqrt).then_inc(sem("lru_sqrt"), 1)
            attention(1, 1.0)
            for k in range(LT):
                act.wait_ge(sem("lru_out"), k + 1)
                act.activation(ahi[:, LT + k], lru[0][:, k], ACT.Copy).then_inc(sem("lru_hi"), 1)

            down(W_OUT, 4)
            residual_rms(0, W_UP)
            norm(1)
            split(W_UP + 1)
            act.dma_start(gvec, a["g_post_ffn"][0:1, :].broadcast_to([P, D])).then_inc(sem("gvec_in"), 16)
            turned(1)
            gate_biases(0)

            def ffn_conv(j, s):
                taps, b = vec("w_conv_ffn2"), vec("b_conv_ffn")
                for h in range(2):
                    for f in range(2):
                        k = (1 - h) * FT + f + 2 * j
                        m = act.activation(cv[:, h, f], ps[:, 2 * s + h, f * S:(f + 1) * S], ACT.Identity,
                                           scale=taps[:, bass.ds(k, 1)], bias=b[:, bass.ds(k, 1)])
                m.then_inc(sem("tap2"), 1)
                act.wait_ge(sem("conv_done"), j + 1)
                act.activation(cv[:, 0], cv[:, 0], ACT.Gelu_apprx_tanh).then_inc(sem("gelu_done"), 1)

            def gate_up(gu, stage):
                def evac(j, s, used):
                    act.wait_ge(mm_done, used)
                    act.wait_ge(sem(f"pr_ready{stage}"), j + 1)
                    if stage == 1:
                        ffn_conv(j, s)
                    else:
                        act.activation(cv[:, 0].rearrange("p f s -> p (f s)"), ps[:, 2 * s, :], ACT.Silu)\
                            .then_inc(sem("silu_done"), 1)

                with act.Fori(0, GU_STEPS // 2) as i:
                    for s in range(2):
                        split(gu + 2 * s + 2, i, 4)
                        split(gu + 2 * s + 3, i, 4)
                        evac(2 * i + s, s, (gu + 2 * s + 2) + 4 * i)
                split(gu + 2 * GU_STEPS)
                split(gu + 2 * GU_STEPS + 1)
                evac(GU_STEPS - 1, 0, gu + 2 * GU_STEPS)

            gate_up(W_UP, 1)
            down(W_DOWN, DN_CHUNKS)
            residual_rms(1, W_QKV)
            norm(2)
            split(W_QKV + 1)
            turned(2)
            for c in range(12):
                split(W_QKV + c + 2)
                act.wait_ge(mm_done, W_QKV + c + 1)
                b = 4 + c % 4
                if c < 8:
                    o = (qT2 if c < 4 else kT2)[:, 2 * (c % 4):2 * (c % 4) + 2, :]
                    i = ps[:, b, :].rearrange("p (f s) -> p f s", f=2)
                else:
                    o = v2[:, :, 256 * (c - 8):256 * (c - 8) + 256]
                    i = ps[:, b, :].rearrange("p (t n) -> p t n", t=NT)
                if c < 4:
                    o, i = o.rearrange("p f (b n) -> p (f b) n", n=GW), reversed_in(ps[:, b, :], GW)
                act.activation(o, i, ACT.Copy).then_inc(sem("qkv2_free"), 1)
            attention(2, 1.0)
            down(W_NAO, 4)
            norm(3)
            split(W_GU + 1)
            turned(3)
            gate_biases(1)
            gate_up(W_GU, 3)
            down(W_DN2, DN_CHUNKS)
            norm(4)
            split(W_MDN + 1)
            turned(4)
            split(W_UQ)
            split(W_UQ + 1)
            act.wait_ge(mm_done, W_UQ)
            act.wait_ge(sem("aT_ready"), TURN0[4] + KT)
            act.wait_ge(sem("mla_down"), 1)
            for t in range(NT):
                for w, (c0, n) in enumerate(((0, QL), (QL, KVL))):
                    act.activation(xn[:, t, 512 + c0:512 + c0 + n], xn[:, t, c0:c0 + n], ACT.Square,
                                   accum_out=ssm[:, 2 * w + t:2 * w + t + 1]).then_inc(sem("act_ssm"), 1)
            act.wait_ge(sem("act_ssm"), 4)
            act.activation(stm[:, 0:2], ssm[:, 0:2], ACT.Sqrt, scale=1.0 / QL, bias=epsc).then_inc(sem("stdm"), 1)
            act.activation(stm[:, 2:4], ssm[:, 2:4], ACT.Sqrt, scale=1.0 / KVL, bias=epsc).then_inc(sem("stdm"), 1)
            turned("m", 3)
            split(W_UKV)
            split(W_MLO)
            for c in range(2):
                act.wait_ge(mm_done, W_UQ + c + 1)
                for t in range(NT):
                    for n in range(2):
                        m = act.activation(qtok[:, t, 8 * c + 4 * n:8 * c + 4 * n + 4, :],
                                           ps[:, 4 * c + 2 * t + n, 0:384].rearrange("p (h d) -> p h d", d=QKW), ACT.Copy)
                m.then_inc(sem("uq_read"), 1)
            act.wait_ge(mm_done, W_UKV + 1)
            for t in range(NT):
                for n in range(4):
                    m = act.activation(ktok[:, t, 4 * n:4 * n + 4, 0:HD],
                                       ps[:, 4 * t + n, :].rearrange("p (h d) -> p h d", d=2 * HD)[:, :, 0:HD], ACT.Copy)
            m.then_inc(sem("k_rows"), 1)
            split(W_MLO + 1)

            def mla_columns(h):
                act.wait_ge(sem("a_qkmm"), h + 1)
                if h >= 2:
                    act.wait_ge(sem("a_score"), HEADS0[3] + h - 1)
                act.activation(qkT[0:QKW, h % 2], ps[0:QKW, 6 + h % 2, :], ACT.Copy).then_inc(sem("a_qkT"), 1)

            attention(3, QKW ** -0.5, side=mla_columns)
            down(W_MLO, 4)
            norm(5)
            split(W_MOE + 1)
            turned(5)
            act.wait_ge(sem("router_in"), 1)
            act.activation(rthi.rearrange("p k e -> p (k e)"), rtr, ACT.Copy).then_inc(sem("router_hi"), 1)
            act.activation(xhi.rearrange("p t n -> p (t n)"), xn.rearrange("p t n -> p (t n)"), ACT.Copy).then_inc(sem("x_hi"), 1)
            for t in range(NT):
                act.wait_ge(sem("router_max"), 1)
                act.activation(rw[:, t, :], ps[:, 4, t * NE:(t + 1) * NE], ACT.Exp, bias=nmx[:, 0, t:t + 1],
                               accum_out=sume[:, 0, t:t + 1]).then_inc(sem("router_exp"), 1)

            def gathered_rows(count):
                act.wait_ge(sem("gathered"), count)
                act.activation(hrow, ps[:, 6:8, :].rearrange("p b n -> p (b n)"), ACT.Copy).then_inc(sem("rows_copied"), 1)

            def gathered_hi(count):
                act.wait_ge(sem("hc_f32"), count)
                act.activation(hchi.rearrange("p k s -> p (k s)"), hc.rearrange("p k s -> p (k s)"), ACT.Copy)\
                    .then_inc(sem("hc_hi"), 1)

            def turned_hi(q, p):
                act.wait_ge(sem("ge_turned"), (5 + q) + 4 * p)
                n = min(4, ET - 4 * q)
                act.activation(gchi[:, 4 * q:4 * q + n].rearrange("p k s -> p (k s)"), ps[:, q, 0:n * P], ACT.Copy)\
                    .then_inc(sem("gc_hi"), 1)

            gathered_rows(1)
            split(W_MOE + 2)
            gathered_hi(1)
            act.wait_ge(sem("experts_known"), 1)
            with act.Fori(0, number_of_passes(act)) as p:
                for c in range(PASS_CHUNKS):
                    if c in (3, 7, 11, 15):
                        j = c // 4
                        act.wait_ge(mm_done, (W_MOE + c + 1) + PASS_CHUNKS * p)
                        act.wait_ge(sem("ge_ready"), (j + 3) + 4 * p)
                        act.activation(sg[:, j % 2], ps[:, 2 * j % 4, 0:EC], ACT.Silu).then_inc(sem("sg_ready"), 1)
                    if c == 12:
                        act.wait_ge(sem("pick_turned"), 1 + p)
                        act.activation(pickT, ps[:, 6, 0:S], ACT.Copy).then_inc(sem("pickT_ready"), 1)
                    if c == 14:
                        turned_hi(0, p)
                        turned_hi(1, p)
                    if c == 16:
                        gathered_rows(2 + p)
                    if c == 17:
                        turned_hi(2, p)
                        turned_hi(3, p)
                    if c == 19:
                        gathered_hi(2 + p)
                    if c == PASS_CHUNKS - 1:
                        act.wait_ge(mm_done, (W_MOE + PASS_CHUNKS) + PASS_CHUNKS * p)
                        act.activation(dchi, ps[:, 4:6, :].rearrange("p b n -> p (b n)"), ACT.Copy).then_inc(sem("dc_hi"), 1)
                    split(W_MOE + c + 3, p, PASS_CHUNKS)
            rms("f", lambda t: x[:, t], lambda t: act.wait_ge(sem("x_final"), t + 1))

        @block.vector
        def _(ve):
            own = Chain(ve, sem("ve_own"))
            def split(c, reg=None, per=0):
                ck = Chunk(c, reg, per)
                ve.wait_ge(hi_done, ck.n + 1)
                k, n = chunk_shape(c)
                ve.tensor_tensor(wlo[ck.half][:, 0:k * n], raws[ck.slot][:, 0:k * n],
                                 whi[ck.half][:, 0:k * n].bitcast(F32), ALU.subtract).then_inc(lo_done, 1)

            def norm(s):
                for t in range(NT):
                    ve.wait_ge(sem("std"), NT * RMS0[s] + t + 1)
                    own.link(ve.reciprocal(rstd[:, t:t + 1], std[:, t:t + 1]))
                    ve.tensor_scalar(xn[:, t], x[:, t], rstd[:, t:t + 1], None, ALU.mult)\
                        .then_inc(sem("xn_ready"), 1)

            def turned(s, scale, shift=None, tiles=KT, between=None):
                for k in range(tiles):
                    ve.wait_ge(sem("turned"), TURN0[s] + min(tiles, k // 2 * 2 + 2))
                    if k >= NHM:
                        ve.wait_ge(sem("aT_ready"), TURN0[s] + k - NHM + 1)
                    src = ps[:, TURN_BANK[s] + k // 2, k % 2 * S:(k % 2 + 1) * S]
                    if shift is None:
                        m = ve.tensor_scalar(hm[:, k % NHM], src, scale[:, k:k + 1], None, ALU.mult)
                    else:
                        m = ve.tensor_scalar(hm[:, k % NHM], src, scale[:, k:k + 1], shift[:, k:k + 1], ALU.mult, ALU.add)
                    m.then_inc(sem("modulated"), 1)
                    if between is not None and k == 3:
                        split(between)

            def modulate_part(layer, j, col=None, reg=None, per=0):
                g = layer * ADA_CHUNKS + j
                loads = 16 * (g // NADA + 1) if reg is None else 16 * (g // NADA + 1) + 16 * (per // NADA) * reg
                ve.wait_ge(ada_in[g % NADA], loads)
                col = 256 * j if col is None else col
                w = view(ada[:, g % NADA], KT, 256)
                cs = vec("c")
                dst = [acc[:, bass.ds(col, 256)], odd]
                marks = [None, None]
                for k in range(KT):
                    o = dst[k % 2]
                    if k == 1:
                        ve.wait_ge(ada_used, (g if reg is None else g + per * reg) + NADA)
                    if k < 2:
                        m = ve.tensor_scalar(o, w[:, k], cs[:, k:k + 1], None, ALU.mult)
                    else:
                        own.after(marks[k % 2])
                        m = ve.scalar_tensor_tensor(o, w[:, k], cs[:, k:k + 1], o, ALU.mult, ALU.add)
                    marks[k % 2] = own.mark(m)
                own.after(marks[1])
                ve.tensor_tensor(dst[0], dst[0], odd, ALU.add).then_inc(ada_used, 1)

            ve.memset(epsc, EPS).then_inc(sem("eps_set"), 1)
            ve.sem_inc(ada_used, NADA)
            for stage in (1, 3):
                ve.sem_inc(sem(f"pr_ready{stage}"), 1)
                ve.sem_inc(sem(f"gu_free{stage}"), 2)
            z1 = own.mark(ve.memset(wr, 0.0))
            own.after(z1)
            ve.memset(wi, 0.0).then_inc(sem("wri_zero"), 1)
            ve.wait_ge(sem("vec_turned"), 1)
            for n, (col, count) in enumerate(VEC_TILES):
                m = ve.tensor_copy(vecs[:, col:col + count], ps[:, 5, n * P:n * P + count])
            m.then_inc(sem("vecs_ready"), 1)
            norm(0)
            turned(0, vec("g_pre_mix"), between=0)
            split(1)
            own.link(ve.memset(tbl, NEG))
            ve.wait_ge(sem("rel_mm"), 1)
            own.link(ve.tensor_copy(tbl[:, 0:S], ps[0:H1, 7, 0:S]))
            ve.sem_inc(sem("tbl_ready"), 1)
            ve.sem_inc(sem("rel_read"), 1)
            ve.wait_ge(sem("wri_dma"), 64)
            ve.sem_inc(sem("wri_in"), 1)

            def decay():
                ve.wait_ge(sem("lam_exp"), 1)
                e_, z, z2, q = lamw[:, 1], lamw[:, 2], lamw[:, 3], lamw[:, 4]
                own.link(ve.tensor_scalar(z, e_, 2.0, None, ALU.add))
                own.link(ve.reciprocal(z2, z))
                own.link(ve.tensor_tensor(z, e_, z2, ALU.mult))
                own.link(ve.tensor_tensor(z2, z, z, ALU.mult))
                own.link(ve.memset(q, 1.0 / 17))
                for n in (15, 13, 11, 9, 7, 5, 3, 1):
                    own.link(ve.tensor_tensor(q, q, z2, ALU.mult))
                    own.link(ve.tensor_scalar(q, q, 1.0 / n, None, ALU.add))
                own.link(ve.tensor_tensor(q, q, z, ALU.mult))
                own.link(ve.tensor_scalar(z, vec("lam"), -1.0, 0.0, ALU.mult, ALU.max))
                own.link(ve.scalar_tensor_tensor(z, q, 2.0, z, ALU.mult, ALU.add))
                ve.tensor_scalar(sp8, z, -8.0, None, ALU.mult).then_inc(sem("sp_ready"), 1)

            wc = vec("w_conv_lru")
            for c in range(10):
                split(c + 2)
                if c < 2:
                    for f in range(2):
                        k = 2 * c + f
                        ve.wait_ge(sem("tap3"), 2 * c + 2)
                        src = ps[:, 4 + c, f * S:(f + 1) * S]
                        for tap in range(CW - 1):
                            d = CW - 1 - tap
                            m = ve.scalar_tensor_tensor(lru[0][:, k, d:S], src[:, 0:S - d], wc[:, tap * LT + k:tap * LT + k + 1],
                                                        lru[0][:, k, d:S], ALU.mult, ALU.add)
                            if tap < CW - 2:
                                own.link(m)
                        m.then_inc(sem("xc_ready"), 1)
                    ve.wait_ge(sem("xc_ready"), 2 * c + 2)
                    ve.sem_inc(sem("in_free"), 1)
                if c == 4:
                    decay()
            ve.wait_ge(sem("in_free"), 10)
            ve.sem_inc(sem("qkv_ready"), 1)
            for k in range(LT):
                ve.wait_ge(sem("exp_a"), k + 1)
                own.link(ve.tensor_tensor(lru[5][:, k], lru[2][:, k], lru[2][:, k], ALU.mult))
                own.link(ve.scalar_tensor_tensor(lru[4][:, k], lru[5][:, k], 1.0, lru[4][:, k], ALU.add, ALU.mult))
                ve.tensor_scalar(lru[4][:, k], lru[4][:, k], -1.0, 0.0, ALU.mult, ALU.max).then_inc(sem("lru_v"), 1)
            for k in range(LT):
                own.link(ve.tensor_tensor(lru[3][:, k], lru[3][:, k], lru[0][:, k], ALU.mult))

            def attention(n, scale, bias=None, late=None):
                heads, causal, seg = attention_plan(n)
                for i in range(heads + 5):
                    if i < heads:
                        ve.wait_ge(sem("a_score"), HEADS0[n] + i + 1)
                        w_all = 384 if causal else 512
                        sc = ps[:, i % 2, 0:w_all]
                        if bias:
                            if i >= 2:
                                ve.wait_ge(sem("a_exp"), HEADS0[n] + i - 1)
                            src = core[n][0][:, i % 2, 0:w_all]
                            if n == 2:
                                ve.wait_ge(sem("bias2_masked"), 1 + i // HB)
                            ve.scalar_tensor_tensor(src, sc, scale, bias(i), ALU.mult, ALU.add)\
                                .then_inc(sem("a_sfree"), 1)
                            ve.wait_ge(sem("a_sfree"), HEADS0[n] + i + 1)
                        else:
                            src = sc
                        if causal:
                            own.mark(ve.tensor_reduce(mx[:, i, 0:1], src[:, 0:P], AXX, ALU.max, negate=True))
                            m = ve.tensor_reduce(mx[:, i, 1:2], src[:, P:384], AXX, ALU.max, negate=True)
                        else:
                            m = ve.tensor_reduce(mx[:, i, :], src.rearrange("p (t n) -> p t n", t=NT), AXX, ALU.max, negate=True)
                        if not bias:
                            own.link(m)
                            m = ve.tensor_scalar(nmx[:, i, :], mx[:, i, :], scale, None, ALU.mult)
                        m.then_inc(sem("a_max"), 1)
                    h = i - 1
                    if 0 <= h < heads:
                        ve.wait_ge(sem("a_exp"), HEADS0[n] + h + 1)
                        ve.reciprocal(rsum[:, h, :], sume[:, h, :]).then_inc(sem("a_rsum"), 1)
                    h = i - 4
                    if 0 <= h < heads and h % 2 == 1:
                        j = h // 2
                        ve.wait_ge(sem("a_ohi"), HEADS0[n] // 2 + j + 1)
                        ve.tensor_tensor(alo[:, j], ps[:, 4 + j % 2, 0:S], ahi[:, j].bitcast(F32), ALU.subtract)\
                            .then_inc(sem("a_out"), 1)
                    if late and 0 <= i - 1 < LT:
                        late(i - 1)

            def lru_late(k):
                ve.wait_ge(sem("lru_sqrt"), k + 1)
                own.link(ve.tensor_tensor(lru[3][:, k], lru[3][:, k], lru[4][:, k], ALU.mult))
                own.link(ve.tensor_tensor_scan(lru[5][:, k], lru[2][:, k], lru[3][:, k], 0.0, ALU.mult, ALU.add))
                ve.tensor_tensor(lru[0][:, k], lru[5][:, k], lru[1][:, k], ALU.mult).then_inc(sem("lru_out"), 1)

            ve.wait_ge(sem("bias1_in"), 32)
            attention(1, HD ** -0.5, lambda i: bias1[:, i, :], lru_late)
            for k in range(LT):
                ve.wait_ge(sem("lru_hi"), k + 1)
                own.mark(ve.tensor_tensor(alo[:, LT + k], lru[0][:, k], ahi[:, LT + k].bitcast(F32), ALU.subtract))
            own.after(own.count())
            ve.wait_ge(sem("a_out"), HEADS0[2] // 2)
            ve.sem_inc(sem("mix_ready"), 1)
            ve.wait_ge(sem("mix_ready"), 1)
            ve.sem_inc(sem("ada_free0"), 1)

            def residual_norm(s, loads):
                ve.wait_ge(sem("gvec_in"), 16 * loads)
                for t in range(NT):
                    ve.wait_ge(sem("std"), NT * RMS0[f"r{s}"] + t + 1)
                    own.link(ve.reciprocal(rstd[:, t:t + 1], std[:, t:t + 1]))
                    o = ps[:, 4 + 2 * t:6 + 2 * t, :].rearrange("p b n -> p (b n)")
                    own.link(ve.scalar_tensor_tensor(xn[:, t], o, rstd[:, t:t + 1], gvec, ALU.mult, ALU.mult))
                    ve.tensor_tensor(x[:, t], x[:, t], xn[:, t], ALU.add).then_inc(sem("x_ready"), 1)

            def residual_gate(s, first):
                gate = gate_row[(s - 2) // 2][(s - 2) % 2]
                for t in range(NT):
                    if t == 0:
                        ve.wait_ge(sem("tile_done"), s + 1)
                    else:
                        ve.wait_ge(mm_done, first)
                    o = ps[:, 4 + 2 * t:6 + 2 * t, :].rearrange("p b n -> p (b n)")
                    own.link(ve.tensor_tensor(xn[:, t], o, gate, ALU.mult))
                    ve.tensor_tensor(x[:, t], x[:, t], xn[:, t], ALU.add).then_inc(sem("x_ready"), 1)

            def down(first, chunks, layer=None, j=0, end=ADA_CHUNKS, also=None):
                for c in range(chunks):
                    if c < chunks - 1:
                        split(first + c + 2)
                    if layer is not None and j + c < end:
                        modulate_part(layer, j + c)
                    if also:
                        also(c)

            down(W_OUT, 4, 0, 0, ADA_MIX)
            residual_norm(0, 1)
            norm(1)
            turned(1, vec("g_pre_ffn"), between=W_UP + 1)
            for j in range(ADA_MIX, ADA_EARLY):
                modulate_part(0, j)

            def gate_up(gu, stage, layer):
                def taps(j, s):
                    ve.wait_ge(sem("tap2"), j + 1)
                    w01 = vec("w_conv_ffn01")
                    for d in (1, 2):
                        for h in range(2):
                            for f in range(2):
                                k = (2 - d) * 2 * FT + (1 - h) * FT + f + 2 * j
                                m = own.mark(ve.scalar_tensor_tensor(
                                    cv[:, h, f, d:S], ps[:, 2 * s + h, f * S:f * S + S - d], w01[:, bass.ds(k, 1)],
                                    cv[:, h, f, d:S], ALU.mult, ALU.add))
                        own.after(m)
                    ve.sem_inc(sem("conv_done"), 1)
                    ve.sem_inc(sem("gu_free1"), 1)

                def evac(j, s):
                    if stage == 1:
                        ve.wait_ge(sem("gelu_done"), j + 1)
                        up = cv[:, 1]
                    else:
                        ve.wait_ge(sem("silu_done"), j + 1)
                        up = ps[:, 2 * s + 1, :].rearrange("p (f s) -> p f s", f=2)
                    ve.wait_ge(sem(f"pr_free{stage}"), j + 1)
                    own.link(ve.tensor_tensor(pr, cv[:, 0], up, ALU.mult))
                    ve.sem_inc(sem(f"pr_ready{stage}"), 1)
                    if stage == 3:
                        ve.sem_inc(sem("gu_free3"), 1)

                per = (9 if stage == 3 else 9 + 8) * 2
                with ve.Fori(0, GU_STEPS // 2) as i:
                    own.enter(i, per)
                    for s in range(2):
                        split(gu + 2 * s + 2, i, 4)
                        split(gu + 2 * s + 3, i, 4)
                        if stage == 1:
                            taps(2 * i + s, s)
                        j = ADA_EARLY + s
                        modulate_part(layer, j, 256 * j + i * 512, i, 2)
                        evac(2 * i + s, s)
                    own.leave(GU_STEPS // 2)
                split(gu + 2 * GU_STEPS)
                split(gu + 2 * GU_STEPS + 1)
                if stage == 1:
                    taps(GU_STEPS - 1, 0)
                evac(GU_STEPS - 1, 0)
                modulate_part(layer, ADA_LATE - 1)

            def modulation_rows(layer):
                ve.wait_ge(sem(f"mod_sum{layer}"), 1)
                ve.tensor_copy(odd[0:32, 0:P], ps[0:32, 0, 0:P]).then_inc(sem(f"mod_rows{layer}"), 1)

            def modulation(layer):
                ve.wait_ge(sem(f"mod_turned{layer}"), 1)
                b = vec("b_ada")[:, layer * 6 * KT:(layer + 1) * 6 * KT]
                for n, part in enumerate((0, 1, 3, 4)):
                    m = own.mark(ve.scalar_tensor_tensor(mod[:, n * KT:(n + 1) * KT], ps[:, 0, n * KT:(n + 1) * KT],
                                                         1.0 if n % 2 else 0.0, b[:, part * KT:(part + 1) * KT], ALU.add, ALU.add))
                own.after(m)

            def gate_rows(layer, first, count):
                ve.wait_ge(sem(f"gate_sum{layer}"), first // 3 + 1)
                ve.wait_ge(sem("gbias_in"), 32 * (layer + 1))
                for n in range(first, first + count):
                    o = gate_row[layer][n // 2][:, n % 2 * 512:(n % 2 + 1) * 512]
                    m = ve.tensor_tensor(o, o, ps[:, 1 + n % 3, :], ALU.add)
                m.then_inc(sem(f"gate_read{layer}"), 1)

            def modulate(layer):
                def also(c):
                    if c == DN_CHUNKS - 2:
                        modulation_rows(layer)
                        gate_rows(layer, 0, 3)
                    elif c == DN_CHUNKS - 1:
                        modulation(layer)
                        gate_rows(layer, 3, 1)
                return also

            gate_up(W_UP, 1, 0)
            down(W_DOWN, DN_CHUNKS, 0, ADA_LATE, also=modulate(0))
            residual_norm(1, 2)
            norm(2)
            turned(2, mod[:, KT:2 * KT], mod[:, 0:KT], between=W_QKV + 1)
            for c in range(12):
                split(W_QKV + c + 2)
            attention(2, HD ** -0.5, lambda i: bias2[i // HB][:, i % HB].rearrange("p t n -> p (t n)"))
            ve.wait_ge(sem("a_out"), HEADS0[3] // 2)
            ve.sem_inc(sem("mix_ready2"), 1)
            ve.wait_ge(sem("mix_ready2"), 1)
            ve.sem_inc(sem("ada_free1"), 1)
            down(W_NAO, 4, 1, 0, ADA_MIX)
            residual_gate(2, W_GU)
            norm(3)
            turned(3, mod[:, 3 * KT:4 * KT], mod[:, 2 * KT:3 * KT], between=W_GU + 1)
            for j in range(ADA_MIX, ADA_EARLY):
                modulate_part(1, j)
            gate_up(W_GU, 3, 1)
            down(W_DN2, DN_CHUNKS, 1, ADA_LATE, also=modulate(1))
            residual_gate(3, W_MDN)
            norm(4)
            turned(4, mod[:, KT:2 * KT], mod[:, 0:KT], between=W_MDN + 1)
            split(W_UQ)
            split(W_UQ + 1)
            ve.wait_ge(mm_done, W_UQ)
            for t in range(NT):
                for c in range(2):
                    n = MLA_DN // 2
                    m = ve.tensor_copy(xn[:, t, c * n:(c + 1) * n], ps[:, 4 + t + 2 * c, 0:n])
            m.then_inc(sem("mla_down"), 1)
            ve.wait_ge(sem("mla_down"), 1)
            for t in range(NT):
                own.mark(ve.tensor_copy(qtok[:, t, H2, HD:QKW], xn[:, t, QL + KVL:MLA_DN]))
            ve.wait_ge(sem("stdm"), 2)
            own.link(ve.reciprocal(rsm, stm))
            for t in range(NT):
                own.mark(ve.tensor_scalar(xn[:, t, 0:QL], xn[:, t, 0:QL], rsm[:, t:t + 1], None, ALU.mult))
                ve.tensor_scalar(xn[:, t, QL:QL + KVL], xn[:, t, QL:QL + KVL], rsm[:, 2 + t:3 + t], None, ALU.mult)\
                    .then_inc(sem("xn_ready"), 1)
            own.after(own.count())
            turned("m", vecs[:, VEC["q_norm"][3]:VEC["q_norm"][3] + 3], None, 3)
            split(W_UKV)
            split(W_MLO)
            ve.wait_ge(sem("uq_read"), 2)
            shape = [P, NT, NH3, 16]
            qr = qtok[:, :, :, HD:QKW].rearrange("p t h (i two) -> p t h i two", two=2)
            trig = [cst[:, at_:at_ + 32].rearrange("p (t o i) -> p t o i", t=NT, o=1).broadcast_to(shape)
                    for at_ in (C_COS, C_SIN)]
            for n, (two, f) in enumerate(((0, 0), (1, 1), (0, 1), (1, 0))):
                for t in range(NT):
                    own.mark(ve.tensor_tensor(rt[:, n, t], qr[:, t, :, :, two], trig[f][:, t], ALU.mult))
            own.after(own.count())
            for n, op in ((0, ALU.subtract), (1, ALU.add)):
                for t in range(NT):
                    m = own.mark(ve.tensor_tensor(qr[:, t, :, :, n], rt[:, 2 * n, t], rt[:, 2 * n + 1, t], op))
            own.after(m)
            ve.sem_inc(sem("roped"), 1)
            for t in range(NT):
                k_rope = qtok[:, t, H2:NH3, HD:QKW].broadcast_to([P, H2, ROPE])
                own.mark(ve.tensor_copy(ktok[:, t, :, HD:QKW], k_rope))
            own.after(own.count())
            ve.wait_ge(sem("k_rows"), 1)

            for t in range(NT):
                for n in range(4):
                    own.mark(ve.tensor_copy(v3[:, t, n * 256:(n + 1) * 256].rearrange("p (h d) -> p h d", d=HD),
                                            ps[:, 4 * t + n, :].rearrange("p (h d) -> p h d", d=2 * HD)[:, :, HD:2 * HD]))
            own.after(own.count())
            ve.sem_inc(sem("ktok_ready"), 1)
            split(W_MLO + 1)
            attention(3, QKW ** -0.5)
            ve.wait_ge(sem("a_out"), (HEADS0[3] + H2) // 2)
            ve.sem_inc(sem("mix_ready3"), 1)
            own.link(ve.memset(y, 0.0))
            for buffer in (dchi, dclo, pickT):
                own.mark(ve.tensor_copy(buffer, y[:, 0, 0:buffer.shape[-1]]))
            own.mark(ve.memset(wcol, 0.0))
            own.link(ve.memset(posn, -1.0))
            down(W_MLO, 4)
            residual_gate(4, W_MOE)
            norm(5)
            turned(5, mod[:, 3 * KT:4 * KT], mod[:, 2 * KT:3 * KT], between=W_MOE + 1)
            ve.wait_ge(sem("router_hi"), 1)
            ve.tensor_tensor(rtlo.rearrange("p k e -> p (k e)"), rtr, rthi.rearrange("p k e -> p (k e)").bitcast(F32),
                             ALU.subtract).then_inc(sem("router_ready"), 1)
            ve.wait_ge(sem("x_hi"), 1)
            ve.tensor_tensor(xlo, xn, xhi.bitcast(F32), ALU.subtract).then_inc(sem("x_lo"), 1)
            ve.wait_ge(sem("logits"), 1)
            ve.tensor_copy(lgT, ps[0:NE, 6, 0:S]).then_inc(sem("logits_read"), 1)
            ve.wait_ge(sem("logits"), 2)
            lg = ps[:, 4, 0:2 * NE].rearrange("p (t e) -> p t e", t=NT)
            ve.tensor_reduce(nmx[:, 0, :], lg, AXX, ALU.max, negate=True).then_inc(sem("router_max"), 1)
            ve.wait_ge(sem("router_exp"), NT)
            own.link(ve.reciprocal(rsum[:, 0, :], sume[:, 0, :]))
            full = [P, NT, NE]
            full4 = [P, NT, NE, NE]
            pr8 = rw[:, 2:4, :]
            own.link(ve.tensor_tensor(pr8, rw[:, 0:2, :], rsum[:, 0, :].rearrange("p (t o) -> p t o", o=1).broadcast_to(full), ALU.mult))
            c4 = cmp_.rearrange("p (r t e f) -> p r t e f", r=4, t=NT, e=NE)
            other = pr8.rearrange("p t (o e) -> p t o e", o=1).broadcast_to(full4)
            this = pr8.rearrange("p t (e o) -> p t e o", o=1).broadcast_to(full4)
            lt = cst[:, C_LT:C_LT + 64].rearrange("p (e f) -> p e f", e=NE)
            for t in range(NT):
                own.mark(ve.tensor_tensor(c4[:, 0, t], other[:, t], this[:, t], ALU.is_gt))
                own.link(ve.tensor_tensor(c4[:, 1, t], other[:, t], this[:, t], ALU.is_equal))
                own.link(ve.tensor_tensor(c4[:, 2, t], c4[:, 1, t], lt, ALU.mult))
                own.link(ve.tensor_tensor(c4[:, 3, t], c4[:, 0, t], c4[:, 2, t], ALU.add))
            rank, chosen, wts = rw[:, 4:6, :], rw[:, 8:10, :], rw[:, 10:12, :]
            own.link(ve.tensor_reduce(rank, c4[:, 3], AXX, ALU.add))
            ve.tensor_scalar(chosen, rank, 1.5, None, ALU.is_lt).then_inc(sem("chosen"), 1)
            ve.wait_ge(sem("chosen"), 1)
            own.link(ve.tensor_tensor(wts, pr8, chosen, ALU.mult))
            own.link(ve.tensor_reduce(rsum[:, 1, :], wts, AXX, ALU.add))
            own.link(ve.reciprocal(rsum[:, 2, :], rsum[:, 1, :]))
            own.link(ve.tensor_tensor(wts, wts, rsum[:, 2, :].rearrange("p (t o) -> p t o", o=1).broadcast_to(full), ALU.mult))
            ve.wait_ge(sem("places"), 1)
            place = rw[:, 12:14, :]
            pl = ps[:, 5, 0:2 * NE].rearrange("p (t e) -> p t e", t=NT)
            own.link(ve.scalar_tensor_tensor(place, pl, 1.0, chosen, ALU.add, ALU.mult))
            own.link(ve.tensor_scalar(posn[:, :, 0:NE], place, -1.0, None, ALU.add))
            own.link(ve.tensor_copy(wcol[:, :, 1:1 + NE], wts))

            def make_pick(col):
                for t in range(NT):
                    m = ve.tensor_scalar(pick[:, t], cst[:, C_IOTA:C_IOTA + P], posn[:, t, bass.ds(col, 1)], None, ALU.is_equal)
                m.then_inc(sem("pick_ready"), 1)

            make_pick(0)
            over, order, tmp2 = rw[:, 14, :], rw[:, 15, :], rw[:, 18:20, :]
            which, ids = rw[:, 21:24, :], rw[:, 24:27, :]
            mine = cmp_[:, 256:256 + 12 * NE].rearrange("p (n t j e) -> p n t j e", n=2, t=NT, j=3)
            places_ = rw[:, 27, 0:6].rearrange("p (t j) -> p t j", t=NT)
            own.link(ve.tensor_scalar(over, ps[:, 5, 2 * NE:3 * NE], 128.5, None, ALU.is_gt))
            own.link(ve.tensor_tensor(c4[:, 0, 0], lt, over.rearrange("p (o e) -> p o e", o=1).broadcast_to([P, NE, NE]), ALU.mult))
            own.link(ve.tensor_reduce(order, c4[:, 0, 0], AXX, ALU.add))
            own.link(ve.memset(eidf, 0.0))
            own.link(ve.tensor_copy(eidf[:, 0:NE], cst[:, C_EID:C_EID + NE]))
            for j in range(3):
                own.mark(ve.scalar_tensor_tensor(which[:, j], order, float(j), over, ALU.is_equal, ALU.mult))
            own.link(ve.tensor_scalar(tmp2, place, -float(P), None, ALU.add))
            part = [P, 3, NE]
            for t in range(NT):
                for n, src in enumerate((tmp2, wts)):
                    own.mark(ve.tensor_tensor(mine[:, n, t], which, src[:, t:t + 1, :].broadcast_to(part), ALU.mult))
            own.mark(ve.tensor_tensor(ids, which, cst[:, C_EID:C_EID + NE].rearrange("p (o e) -> p o e", o=1).broadcast_to(part), ALU.mult))
            own.after(own.count())
            own.mark(ve.tensor_reduce(places_, mine[:, 0], AXX, ALU.add))
            own.mark(ve.tensor_reduce(wcol[:, :, 1 + NE:4 + NE], mine[:, 1], AXX, ALU.add))
            own.mark(ve.tensor_reduce(eidf[:, NE:NE + 3], ids, AXX, ALU.add))
            own.after(own.count())
            own.link(ve.tensor_scalar(posn[:, :, NE:NE + 3], places_, -1.0, None, ALU.add))
            own.link(ve.tensor_reduce(rw[:, 20, 0:1], over, AXX, ALU.add))
            own.link(ve.tensor_scalar(eidf[:, N_PASS:N_PASS + 1], rw[:, 20, 0:1], float(NE), None, ALU.add))
            ve.tensor_copy(eidi, eidf).then_inc(sem("experts_known"), 1)

            def gathered(count):
                ve.wait_ge(sem("gathered_turned"), count)
                for k in range(KT):
                    m = ve.tensor_scalar(hc[:, k], ps[:, 6 + k // 4, k % 4 * P:(k % 4 + 1) * P],
                                         mod[:, 3 * KT + k:3 * KT + k + 1], mod[:, 2 * KT + k:2 * KT + k + 1], ALU.mult, ALU.add)
                m.then_inc(sem("hc_f32"), 1)

            def add_y(t, col):
                for n in range(2):
                    o = y[:, t, n * 512:(n + 1) * 512]
                    m = ve.scalar_tensor_tensor(o, ps[:, 6 + n, :], wcol[:, t, bass.ds(col, 1)], o, ALU.mult, ALU.add)
                m.then_inc(sem("y_added"), 1)

            for name in ("ge_turned", "ge_ready", "gc_ready"):
                ve.sem_inc(sem(name), 4)
            ve.sem_inc(sem("dc_ready"), 1)
            ve.sem_inc(sem("pickT_ready"), 1)
            split(W_MOE + 2)
            gathered(1)
            ve.wait_ge(sem("hc_hi"), 1)
            ve.tensor_tensor(hclo, hc, hchi.bitcast(F32), ALU.subtract).then_inc(sem("hc_ready"), 1)

            def turned_lo(q, p):
                ve.wait_ge(sem("gc_hi"), (q + 1) + 4 * p)
                n = min(4, ET - 4 * q)
                ve.tensor_tensor(gclo[:, 4 * q:4 * q + n].rearrange("p k s -> p (k s)"), ps[:, q, 0:n * P],
                                 gchi[:, 4 * q:4 * q + n].rearrange("p k s -> p (k s)").bitcast(F32), ALU.subtract)\
                    .then_inc(sem("gc_ready"), 1)

            ve.wait_ge(sem("experts_known"), 1)
            passes = number_of_passes(ve)
            with ve.Fori(0, passes) as p:
                for c in range(PASS_CHUNKS):
                    if c in (3, 7, 11, 15):
                        j = c // 4
                        ve.wait_ge(sem("sg_ready"), (j + 1) + 4 * p)
                        if j == 0:
                            ve.wait_ge(sem("ge_turned"), 4 + 4 * p)
                        ve.tensor_tensor(ge[:, j * EC:(j + 1) * EC], sg[:, j % 2], ps[:, (2 * j + 1) % 4, 0:EC], ALU.mult)\
                            .then_inc(sem("ge_ready"), 1)
                    if c in (4, 8):
                        t = c // 4 - 1
                        ve.wait_ge(sem("combined"), (t + 1) + 2 * p)
                        add_y(t, p)
                    if c == 12:
                        ve.wait_ge(sem("pick_turned"), 1 + p)
                        make_pick(p + 1)
                    if c == 14:
                        turned_lo(0, p)
                        turned_lo(1, p)
                    if c == 17:
                        turned_lo(2, p)
                        turned_lo(3, p)
                    if c == 18:
                        gathered(2 + p)
                    if c == PASS_CHUNKS - 1:
                        ve.wait_ge(sem("dc_hi"), 1 + p)
                        ve.tensor_tensor(dclo, ps[:, 4:6, :].rearrange("p b n -> p (b n)"), dchi.bitcast(F32), ALU.subtract)\
                            .then_inc(sem("dc_ready"), 1)
                    split(W_MOE + c + 3, p, PASS_CHUNKS)
            for t in range(NT):
                ve.wait_ge(sem("combined"), (t + 1) + 2 * passes)
                add_y(t, passes)
            ve.wait_ge(sem("y_added"), 2 + 2 * passes)
            for t in range(NT):
                own.link(ve.tensor_tensor(y[:, t], y[:, t], gate_row[1][1], ALU.mult))
                ve.tensor_tensor(x[:, t], x[:, t], y[:, t], ALU.add).then_inc(sem("x_final"), 1)
            ve.wait_ge(sem("final_in"), 16)
            for t in range(NT):
                ve.wait_ge(sem("std"), NT * RMS0["f"] + t + 1)
                own.link(ve.reciprocal(rstd[:, t:t + 1], std[:, t:t + 1]))
                ve.scalar_tensor_tensor(xn[:, t], x[:, t], rstd[:, t:t + 1], final_scale, ALU.mult, ALU.mult)\
                    .then_inc(sem("result"), 1)

        @block.gpsimd
        def _(po):
            def turned(s, tiles=KT):
                for k in range(tiles):
                    po.wait_ge(sem("aT_hi"), TURN0[s] + k + 1)
                    po.tensor_tensor(alo[:, k], hm[:, k % NHM], ahi[:, k].bitcast(F32), ALU.subtract)\
                        .then_inc(sem("aT_ready"), 1)

            def attention(n):
                heads, causal, seg = attention_plan(n)
                for h in range(heads):
                    po.wait_ge(sem("a_rsum"), HEADS0[n] + h + 1)
                    for qt, col, w in seg:
                        v = core[n][1][:, h % 3, col:col + w]
                        m = po.tensor_scalar(v, v, rsum[:, h, qt:qt + 1], 1.0, ALU.mult, ALU.mult)
                    m.then_inc(sem("a_norm"), 1)

            def gate_up(stage):
                def step(j):
                    po.wait_ge(sem(f"pr_ready{stage}"), j + 2)
                    o = ghi[:, bass.ds(2 * j, 2), :]
                    po.tensor_copy(o, pr).then_inc(sem(f"pr_hi{stage}"), 1)
                    po.wait_ge(sem(f"pr_hi{stage}"), j + 1)
                    po.tensor_tensor(glo[:, bass.ds(2 * j, 2), :], pr, o.bitcast(F32), ALU.subtract)\
                        .then_inc(sem(f"gT_ready{stage}"), 1)
                    po.wait_ge(sem(f"gT_ready{stage}"), j + 1)
                    po.sem_inc(sem(f"pr_free{stage}"), 1)

                po.sem_inc(sem(f"pr_free{stage}"), 1)
                with po.Fori(0, GU_STEPS) as j:
                    step(j)

            po.wait_ge(sem("eps_set"), 1)
            turned(0)
            attention(1)
            turned(1)
            gate_up(1)
            turned(2)
            for hb in range(2):
                po.wait_ge(sem(f"bias2_in{hb}"), 16 * GR * GR)
                mask = cst[:, C_NAM:C_NAM + GW].rearrange("p (o j) -> p o j", o=1).broadcast_to([P, HB * NT * GR, GW])
                v = bias2[hb].rearrange("p h t (i j) -> p (h t i) j", j=GW)
                po.tensor_tensor(v, v, mask, ALU.add).then_inc(sem("bias2_masked"), 1)
            attention(2)
            turned(3)
            gate_up(3)
            turned(4)
            turned("m", 3)
            attention(3)
            po.wait_ge(sem("mix_ready3"), 1)
            po.dma_start(rtr.rearrange("p (k e) -> p k e", k=KT), a["moe_w_router_2"][0].rearrange("(k p) e -> p k e", p=P))\
                .then_inc(sem("router_dma"), 16)
            po.dma_start(final_scale, a["final_norm_2"].rearrange("(o n) -> o n", o=1).broadcast_to([P, D])).then_inc(sem("final_in"), 16)
            po.wait_ge(sem("router_dma"), 16)
            po.sem_inc(sem("router_in"), 1)
            turned(5)

            def gathered_lo(count):
                po.wait_ge(sem("hc_hi"), count)
                po.tensor_tensor(hclo, hc, hchi.bitcast(F32), ALU.subtract).then_inc(sem("hc_ready"), 1)

            po.wait_ge(sem("experts_known"), 1)
            with po.Fori(0, number_of_passes(po)) as p:
                gathered_lo(2 + p)


def _rows(name, rows):
    return lambda a: a[name][0].rearrange("(r c) -> r c", c=P)[0:rows]


VEC_SRC = {
    "c": _rows("c_2", 8),
    "g_pre_mix": _rows("g_pre_mix", 8),
    "g_pre_ffn": _rows("g_pre_ffn", 8),
    "w_conv_lru": lambda a: a["w_conv_lru"][0].rearrange("w (k c) -> (w k) c", c=P),
    "b_conv_lru": _rows("b_conv_lru", 4),
    "b_r": _rows("b_r", 4),
    "b_i": _rows("b_i", 4),
    "lam": _rows("lam", 4),
    "q_norm": _rows("mla_q_norm_2", 2),
    "kv_norm": _rows("mla_kv_norm_2", 1),
    "b_conv_ffn": _rows("b_conv_ffn", 44),
    "b_ada": lambda a: a["b_ada_2"].rearrange("l (k c) -> (l k) c", c=P),
    "w_conv_ffn01": lambda a: a["w_conv_ffn"][0, 0:2].rearrange("w (k c) -> (w k) c", c=P),
    "w_conv_ffn2": lambda a: a["w_conv_ffn"][0, 2:3].rearrange("w (k c) -> (w k) c", c=P),
}
ROW_DMAS = len(VEC_SRC)

_INS = ["x", "g_pre_mix", "w_in", "rel_bias", "w_conv_lru", "b_conv_lru", "w_r", "b_r", "w_i", "b_i", "lam", "w_out",
        "g_post_mix", "g_pre_ffn", "w_up", "w_conv_ffn", "b_conv_ffn", "w_down", "g_post_ffn", "c_2", "w_ada_2",
        "b_ada_2", "na_w_qkv_2", "na_rpb_2", "na_w_o_2", "ffn_w_gu_2", "ffn_w_down_2", "mla_w_down_2",
        "mla_q_norm_2", "mla_w_uq_2", "mla_kv_norm_2", "mla_w_ukv_2", "mla_w_o_2", "moe_w_router_2", "moe_w_gu_2",
        "moe_w_down_2", "final_norm_2"]


def kernel(**inputs):
    import concourse.bacc as _bacc
    from concourse.bass_utils import run_bass_kernel_spmd as _run

    nc = _bacc.Bacc("TRN2", target_bir_lowering=False, num_devices=1)
    arrays = {f"in_{n}": np.ascontiguousarray(inputs[n]) for n in _INS}
    arrays["in_consts"] = shape_constants()
    aps = {n[3:]: nc.dram_tensor(n, v.shape, mybir.dt.from_np(v.dtype), kind="ExternalInput").ap()
           for n, v in arrays.items()}
    out = nc.dram_tensor("out_0", (1, S, D), F32, kind="ExternalOutput").ap()
    blocks(nc, aps, out)
    return _run(nc, [arrays], core_ids=[0]).results[0]["out_0"]
```
